# Optimizing a Trainium2 kernel written in Bass

```python
import math
import jax, jax.numpy as jnp
from jax import lax
import numpy as np

D_MODEL = 1024
BATCH = 1
SEQ = 256
DEPTH = 1

D_MIX = D_MODEL
D_LRU = D_MIX // 2
N_LRU_BLOCKS = 8
LRU_BLOCK = D_LRU // N_LRU_BLOCKS
CONV_WIDTH = 4
RG_C = 8.0
N_HEADS = 8
HEAD_DIM = (D_MIX - D_LRU) // N_HEADS
D_ATTN = N_HEADS * HEAD_DIM
ROT_DIM = HEAD_DIM // 4
ROPE_THETA = 500000.0
MOBA_BLOCK = 256
MOBA_TOPK = 3
Q_CHUNK = 8
MEM_LEN = 256
N_XHEADS = 4
XHEAD_DIM = D_MODEL // N_XHEADS
N_GROUPS = 4
EXPERTS_PER_GROUP = 8
N_EXPERTS = N_GROUPS * EXPERTS_PER_GROUP
EXPERT_TOPK = 2
D_FF_EXPERT = D_MODEL // 2
MOE_ROWS = 128
D_IN = 2 * D_LRU + 3 * D_ATTN
EPS = 1e-6

kernel_name = 'hymba_rglru_moba_hmoe_block'

def rms_norm(x, g):
    xf = x.astype(jnp.float32)
    y = xf * lax.rsqrt(jnp.mean(xf * xf, axis=-1, keepdims=True) + EPS)
    return (y * g.astype(jnp.float32)).astype(x.dtype)

def partial_rope(x, pos):
    half = ROT_DIM // 2
    inv_freq = ROPE_THETA ** (-jnp.arange(0, ROT_DIM, 2, dtype=jnp.float32) / ROT_DIM)
    ang = pos.astype(jnp.float32)[:, None] * inv_freq[None, :]
    cos, sin = jnp.cos(ang), jnp.sin(ang)
    xf = x.astype(jnp.float32)
    x1, x2, rest = xf[..., :half], xf[..., half:ROT_DIM], xf[..., ROT_DIM:]
    out = jnp.concatenate([x1 * cos - x2 * sin, x2 * cos + x1 * sin, rest], axis=-1)
    return out.astype(x.dtype)

def causal_depthwise_conv(x, w, b):
    C = x.shape[-1]
    y = lax.conv_general_dilated(x, w[:, None, :].astype(x.dtype), window_strides=(1,),
                                 padding=[(CONV_WIDTH - 1, 0)],
                                 dimension_numbers=('NWC', 'WIO', 'NWC'),
                                 feature_group_count=C)
    return y + b

def rg_lru(xc, w_rg, b_rg, w_ig, b_ig, lru_lambda):
    B, S, C = xc.shape
    xh = xc.reshape(B, S, N_LRU_BLOCKS, LRU_BLOCK)
    r = jax.nn.sigmoid((jnp.einsum('bshi,hij->bshj', xh, w_rg).reshape(B, S, C) + b_rg).astype(jnp.float32))
    i = jax.nn.sigmoid((jnp.einsum('bshi,hij->bshj', xh, w_ig).reshape(B, S, C) + b_ig).astype(jnp.float32))
    log_a = -RG_C * r * jax.nn.softplus(-lru_lambda.astype(jnp.float32))
    a = jnp.exp(log_a)
    u = jnp.sqrt(-jnp.expm1(2.0 * log_a)) * (i * xc.astype(jnp.float32))

    def step(h, au):
        a_t, u_t = au
        h = a_t * h + u_t
        return h, h

    _, hs = lax.scan(step, jnp.zeros((B, C), jnp.float32), (jnp.swapaxes(a, 0, 1), jnp.swapaxes(u, 0, 1)))
    return jnp.swapaxes(hs, 0, 1).astype(xc.dtype)

def moba_attention(q, k, v):
    B, H, S, hd = q.shape
    nb = -(-S // MOBA_BLOCK)
    sp = nb * MOBA_BLOCK
    pad = ((0, 0), (0, 0), (0, sp - S), (0, 0))
    q, k, v = jnp.pad(q, pad), jnp.pad(k, pad), jnp.pad(v, pad)
    kb = k.reshape(B, H, nb, MOBA_BLOCK, hd)
    vb = v.reshape(B, H, nb, MOBA_BLOCK, hd)
    kmean = jnp.mean(kb.astype(jnp.float32), axis=3)
    pos = jnp.arange(sp, dtype=jnp.int32)
    qblk = pos // MOBA_BLOCK
    gate = jnp.einsum('bhsd,bhnd->bhsn', q.astype(jnp.float32), kmean)
    past = jnp.arange(nb, dtype=jnp.int32)[None, :] < qblk[:, None]
    gate = jnp.where(past, gate, -jnp.inf)
    n_pick = min(MOBA_TOPK, nb)
    _, top = lax.top_k(gate, n_pick)
    top = top.astype(jnp.int32)
    top_valid = top < qblk[:, None]
    own = jnp.broadcast_to(qblk[:, None], (B, H, sp, 1))
    idx = jnp.concatenate([top, own], axis=-1)
    valid = jnp.concatenate([top_valid, jnp.ones_like(own, dtype=bool)], axis=-1)
    nsel = n_pick + 1
    nc = sp // Q_CHUNK
    kflat = kb.reshape(B * H * nb, MOBA_BLOCK, hd)
    vflat = vb.reshape(B * H * nb, MOBA_BLOCK, hd)
    bh_off = (jnp.arange(B * H, dtype=jnp.int32) * nb).reshape(B, H, 1, 1)
    scale = HEAD_DIM ** -0.5

    def to_chunks(t):
        return jnp.moveaxis(t.reshape(B, H, nc, Q_CHUNK, *t.shape[3:]), 2, 0)

    def attend(args):
        q_c, idx_c, valid_c, t_c = args
        gidx = bh_off + idx_c
        kg = kflat[gidx]
        vg = vflat[gidx]
        s = jnp.einsum('bhqd,bhqnkd->bhqnk', q_c, kg).astype(jnp.float32) * scale
        keypos = idx_c[..., None] * MOBA_BLOCK + jnp.arange(MOBA_BLOCK, dtype=jnp.int32)
        mask = valid_c[..., None] & (keypos <= t_c[None, None, :, None, None])
        s = jnp.where(mask, s, -jnp.inf).reshape(B, H, Q_CHUNK, nsel * MOBA_BLOCK)
        p = jax.nn.softmax(s, axis=-1).astype(vg.dtype)
        return jnp.einsum('bhqm,bhqmd->bhqd', p, vg.reshape(B, H, Q_CHUNK, nsel * MOBA_BLOCK, hd))

    out = lax.map(attend, (to_chunks(q), to_chunks(idx), to_chunks(valid), pos.reshape(nc, Q_CHUNK)))
    out = jnp.moveaxis(out, 0, 2).reshape(B, H, sp, hd)
    return out[:, :, :S]

def hybrid_mixer(xn, w_in, conv_w, conv_b, w_rg, b_rg, w_ig, b_ig, lru_lambda,
                 norm_lru_out, norm_attn_out, w_out):
    B, S, _ = xn.shape
    proj = xn @ w_in
    x_lru, g_lru, q, k, v = jnp.split(
        proj, [D_LRU, 2 * D_LRU, 2 * D_LRU + D_ATTN, 2 * D_LRU + 2 * D_ATTN], axis=-1)
    xc = causal_depthwise_conv(x_lru, conv_w, conv_b)
    y_lru = rg_lru(xc, w_rg, b_rg, w_ig, b_ig, lru_lambda) * jax.nn.gelu(g_lru)
    pos = jnp.arange(S, dtype=jnp.int32)
    heads = lambda t: t.reshape(B, S, N_HEADS, HEAD_DIM).transpose(0, 2, 1, 3)
    qh = partial_rope(heads(q), pos)
    kh = partial_rope(heads(k), pos)
    y_att = moba_attention(qh, kh, heads(v)).transpose(0, 2, 1, 3).reshape(B, S, D_ATTN)
    y = jnp.concatenate([rms_norm(y_lru, norm_lru_out), rms_norm(y_att, norm_attn_out)], axis=-1)
    return y @ w_out

def memory_cross_attention(hn, mem, norm_mem, w_xq, w_xkv, w_xo):
    B, S, _ = hn.shape
    M = mem.shape[1]
    q = (hn @ w_xq).reshape(B, S, N_XHEADS, XHEAD_DIM)
    k, v = jnp.split(rms_norm(mem, norm_mem) @ w_xkv, 2, axis=-1)
    k = k.reshape(B, M, N_XHEADS, XHEAD_DIM)
    v = v.reshape(B, M, N_XHEADS, XHEAD_DIM)
    s = jnp.einsum('bshd,bmhd->bhsm', q, k).astype(jnp.float32) * (XHEAD_DIM ** -0.5)
    p = jax.nn.softmax(s, axis=-1).astype(v.dtype)
    o = jnp.einsum('bhsm,bmhd->bshd', p, v).reshape(B, S, D_MODEL)
    return o @ w_xo

def hier_moe(xn, w_router_group, b_router_group, w_router_expert, b_router_expert, w_gate_up, w_down):
    B, S, D = xn.shape
    N = B * S
    xt = xn.reshape(N, D)
    g_logits = (xt @ w_router_group + b_router_group).astype(jnp.float32)
    g_prob = jax.nn.softmax(g_logits, axis=-1)
    grp = jnp.argmax(g_logits, axis=-1).astype(jnp.int32)
    g_w = jnp.take_along_axis(g_prob, grp[:, None], axis=-1)
    e_logits = (xt @ w_router_expert + b_router_expert).astype(jnp.float32).reshape(N, N_GROUPS, EXPERTS_PER_GROUP)
    e_logits = jnp.take_along_axis(e_logits, grp[:, None, None], axis=1)[:, 0]
    e_prob = jax.nn.softmax(e_logits, axis=-1)
    top_p, top_i = lax.top_k(e_prob, EXPERT_TOPK)
    gates = g_w * top_p / jnp.sum(top_p, axis=-1, keepdims=True)
    expert = grp[:, None] * EXPERTS_PER_GROUP + top_i.astype(jnp.int32)
    M = N * EXPERT_TOPK
    e_flat = expert.reshape(M)
    g_flat = gates.reshape(M)
    order = jnp.argsort(e_flat).astype(jnp.int32)
    e_sorted = e_flat[order]
    tok_sorted = order // EXPERT_TOPK
    gate_sorted = g_flat[order]
    counts = jnp.bincount(e_flat, length=N_EXPERTS).astype(jnp.int32)
    starts = jnp.cumsum(counts) - counts
    padded = (counts + MOE_ROWS - 1) // MOE_ROWS * MOE_ROWS
    pad_ends = jnp.cumsum(padded)
    pad_starts = pad_ends - padded
    dest = pad_starts[e_sorted] + jnp.arange(M, dtype=jnp.int32) - starts[e_sorted]
    n_blocks = -(-M // MOE_ROWS) + N_EXPERTS
    x_buf = jnp.zeros((n_blocks * MOE_ROWS, D), xt.dtype).at[dest].set(xt[tok_sorted])
    blk_expert = jnp.minimum(
        jnp.searchsorted(pad_ends, jnp.arange(n_blocks, dtype=jnp.int32) * MOE_ROWS, side='right'),
        N_EXPERTS - 1).astype(jnp.int32)

    def expert_block(args):
        e, xb = args
        gate, up = jnp.split(xb @ w_gate_up[e], 2, axis=-1)
        return (jax.nn.silu(gate) * up) @ w_down[e]

    y_buf = lax.map(expert_block, (blk_expert, x_buf.reshape(n_blocks, MOE_ROWS, D))).reshape(-1, D)
    y = y_buf[dest] * gate_sorted[:, None].astype(xt.dtype)
    out = jnp.zeros((N, D), xt.dtype).at[tok_sorted].add(y)
    return out.reshape(B, S, D)

def setup_inputs(seed: int = 0) -> dict:
    key = jax.random.key(seed)
    ks = jax.random.split(key, 32)
    f32 = jnp.float32

    def nrm(k, shape, scale):
        return jax.random.normal(k, shape, f32) * scale

    def gain(k, shape):
        return 1.0 + 0.02 * jax.random.normal(k, shape, f32)

    u = jax.random.uniform(ks[8], (DEPTH, D_LRU), f32, minval=0.9, maxval=0.999)
    a = u ** (1.0 / RG_C)
    lru_lambda = jnp.log(a) - jnp.log1p(-a)
    return {
        'x': nrm(ks[0], (BATCH, SEQ, D_MODEL), 1.0),
        'mem': nrm(ks[1], (BATCH, MEM_LEN, D_MODEL), 1.0),
        'norm_mix': gain(ks[2], (DEPTH, D_MODEL)),
        'w_in': nrm(ks[3], (DEPTH, D_MODEL, D_IN), D_MODEL ** -0.5),
        'conv_w': nrm(ks[4], (DEPTH, CONV_WIDTH, D_LRU), CONV_WIDTH ** -0.5),
        'conv_b': nrm(ks[5], (DEPTH, D_LRU), 0.02),
        'w_rg': nrm(ks[6], (DEPTH, N_LRU_BLOCKS, LRU_BLOCK, LRU_BLOCK), LRU_BLOCK ** -0.5),
        'b_rg': nrm(ks[7], (DEPTH, D_LRU), 0.02),
        'w_ig': nrm(ks[9], (DEPTH, N_LRU_BLOCKS, LRU_BLOCK, LRU_BLOCK), LRU_BLOCK ** -0.5),
        'b_ig': nrm(ks[10], (DEPTH, D_LRU), 0.02),
        'lru_lambda': lru_lambda,
        'norm_lru_out': gain(ks[11], (DEPTH, D_LRU)),
        'norm_attn_out': gain(ks[12], (DEPTH, D_ATTN)),
        'w_out': nrm(ks[13], (DEPTH, D_MIX, D_MODEL), D_MIX ** -0.5),
        'norm_cross': gain(ks[14], (DEPTH, D_MODEL)),
        'norm_mem': gain(ks[15], (DEPTH, D_MODEL)),
        'w_xq': nrm(ks[16], (DEPTH, D_MODEL, D_MODEL), D_MODEL ** -0.5),
        'w_xkv': nrm(ks[17], (DEPTH, D_MODEL, 2 * D_MODEL), D_MODEL ** -0.5),
        'w_xo': nrm(ks[18], (DEPTH, D_MODEL, D_MODEL), D_MODEL ** -0.5),
        'norm_ffn': gain(ks[19], (DEPTH, D_MODEL)),
        'w_router_group': nrm(ks[20], (DEPTH, D_MODEL, N_GROUPS), D_MODEL ** -0.5),
        'b_router_group': nrm(ks[21], (DEPTH, N_GROUPS), 0.01),
        'w_router_expert': nrm(ks[22], (DEPTH, D_MODEL, N_EXPERTS), D_MODEL ** -0.5),
        'b_router_expert': nrm(ks[23], (DEPTH, N_EXPERTS), 0.01),
        'w_gate_up': nrm(ks[24], (DEPTH, N_EXPERTS, D_MODEL, 2 * D_FF_EXPERT), D_MODEL ** -0.5),
        'w_down': nrm(ks[25], (DEPTH, N_EXPERTS, D_FF_EXPERT, D_MODEL), D_FF_EXPERT ** -0.5),
        'norm_final': gain(ks[26], (D_MODEL,)),
    }

def reference(x, mem, norm_mix, w_in, conv_w, conv_b, w_rg, b_rg, w_ig, b_ig, lru_lambda,
              norm_lru_out, norm_attn_out, w_out, norm_cross, norm_mem, w_xq, w_xkv, w_xo,
              norm_ffn, w_router_group, b_router_group, w_router_expert, b_router_expert,
              w_gate_up, w_down, norm_final):
    h = x
    for l in range(DEPTH):
        h = h + hybrid_mixer(rms_norm(h, norm_mix[l]), w_in[l], conv_w[l], conv_b[l], w_rg[l], b_rg[l],
                             w_ig[l], b_ig[l], lru_lambda[l], norm_lru_out[l], norm_attn_out[l], w_out[l])
        h = h + memory_cross_attention(rms_norm(h, norm_cross[l]), mem, norm_mem[l], w_xq[l], w_xkv[l], w_xo[l])
        h = h + hier_moe(rms_norm(h, norm_ffn[l]), w_router_group[l], b_router_group[l],
                         w_router_expert[l], b_router_expert[l], w_gate_up[l], w_down[l])
    return rms_norm(h, norm_final)


_drawn_inputs = setup_inputs


def setup_inputs(seed=0):
    import zlib

    import numpy as np

    out = dict(_drawn_inputs(seed))
    spreads = {}
    factors = {'b_rg': 8.0,
     'b_ig': 6.727,
     'norm_lru_out': 3.459,
     'norm_attn_out': 3.43,
     'norm_cross': 8.0,
     'norm_mem': 8.0,
     'norm_ffn': 2.677,
     'b_router_group': 42.355,
     'b_router_expert': 8.0,
     'norm_final': 7.766}
    for name, (base, spread) in spreads.items():
        noise = np.random.default_rng([zlib.crc32(name.encode()), seed]).standard_normal(out[name].shape)
        drawn = base * np.exp(spread * noise) if base else spread * noise
        out[name] = __import__('jax').numpy.asarray(drawn.astype(out[name].dtype))
    for name, factor in factors.items():
        out[name] = (out[name] * factor).astype(out[name].dtype)
    return out
```

```python
from contextlib import ExitStack

import concourse.bass as bass
import numpy as np
from concourse import mybir

F32 = mybir.dt.float32
I32 = mybir.dt.int32
ALU = mybir.AluOpType
ACT = mybir.ActivationFunctionType
AX = mybir.AxisListType

P = 128
D = 1024
S = 256
NH = S // P
KC = D // P
DL = 512
CT = DL // P
CONV = 4
HEADS = 8
HD = 64
HALF_ROT = 8
XH = 4
XHD = 256
GROUPS = 4
EXPERTS = 32
PER_GROUP = EXPERTS // GROUPS
FF = 512
EPS = 1e-6
UNIT = 4096
UNITS = 12
SLOTS = 32
BATCH = P // SLOTS
BATCHES = EXPERTS // BATCH
BIG = 1e30
GELU_IN = 0.7978845608028654
GELU_CUBE = 0.044715

EXPERT_UNITS = [(3, 4, 5), (6, 7, 0), (1, 2, 8), (9, 10, 11)]

STREAM = ["x_lru", "q", "k", "v", "g_lru", "xk0", "xk1", "xv0", "xv1", "out0", "out1",
          "xq0", "xq1", "xo0", "xo1"]
STREAM_UNITS = 4
UNIT_OF = {name: n % STREAM_UNITS for n, name in enumerate(STREAM)}
LOADED = {name: 16 * (n // STREAM_UNITS + 1) for n, name in enumerate(STREAM)}
LOADS_IN_A = [sum(UNIT_OF[name] == u for name in STREAM) for u in range(UNITS)]

ROWS = {}
for _name, _rows in (("norm_mix", KC), ("norm_mem", KC), ("norm_cross", KC), ("norm_ffn", KC),
                     ("norm_lru_out", CT), ("norm_attn_out", CT), ("conv_b", CT), ("b_rg", CT),
                     ("b_ig", CT), ("lru_lambda", CT), ("conv_w", CONV * CT)):
    ROWS[_name] = (sum(n for _, n in ROWS.values()), _rows)
N_ROWS = sum(n for _, n in ROWS.values())

CONSTS = {}
for _name, _cols in (("ident", P), ("before", P), ("causal", S), ("ones", P), ("iota", EXPERTS),
                     ("cos", NH * HALF_ROT), ("sin", NH * HALF_ROT), ("power", 4)):
    CONSTS[_name] = (sum(n for _, n in CONSTS.values()), _cols)
N_CONSTS = sum(n for _, n in CONSTS.values())


def constants():
    t = np.zeros((P, N_CONSTS), np.float32)

    def put(name, value):
        a, n = CONSTS[name]
        t[:, a:a + n] = value

    i = np.arange(P)
    put("ident", np.eye(P))
    put("before", i[:, None] < i[None, :])
    put("causal", np.where(np.arange(S)[None, :] - P <= i[:, None], 0.0, -BIG))
    put("ones", 1.0)
    put("iota", np.arange(EXPERTS)[None, :])
    rot = 2 * HALF_ROT
    inv_freq = np.float32(500000.0) ** (-np.arange(0, rot, 2, dtype=np.float32) / np.float32(rot))
    angle = np.arange(S, dtype=np.float32)[:, None] * inv_freq[None, :].astype(np.float32)
    for name, f in (("cos", np.cos), ("sin", np.sin)):
        put(name, f(angle).astype(np.float32).reshape(NH, P, HALF_ROT).transpose(1, 0, 2).reshape(P, -1))
    put("power", -0.5)
    return t


JOBS = [("params", 1)]
JOBS += [(f"Tx{c}", 2) for c in range(4)]
JOBS += [(f"xl{c}", 1) for c in range(2)]
JOBS += [(f"Tm{c}", 2) for c in range(4)]
JOBS += [(f"q{h}", 1) for h in range(2)] + [(f"k{h}", 1) for h in range(2)]
JOBS += [(f"rg{c}", 2) for c in range(2)] + [(f"ig{c}", 2) for c in range(2)]
JOBS += [(f"v{h}", 1) for h in range(2)]
JOBS += [(f"Tqk{c}", 1) for c in range(4)]
JOBS += [(f"gl{c}", 1) for c in range(2)]
JOBS += [("s0e", 1), ("s0o", 1)] + [(f"s1{c}", 1) for c in range(4)]
JOBS += [(f"xk{c}", 1) for c in range(4)]
JOBS += [(f"Tp{c}", 1) for c in range(6)]
JOBS += [(f"xv{c}", 1) for c in range(4)]
JOBS += [(f"pv{c}", 2) for c in range(2)]
JOBS += [("ss", 1)]
JOBS += [(f"out{c}", 1) for c in range(8)]
JOBS += [(f"Th{c}", 2) for c in range(4)]
JOBS += [(f"xq{c}", 1) for c in range(4)]
JOBS += [(f"xs{c}", 2) for c in range(4)]
JOBS += [(f"Txp{c}", 1) for c in range(4)]
JOBS += [(f"xpv{c}", 1) for c in range(4)]
JOBS += [(f"xo{c}", 1) for c in range(4)]
JOBS += [(f"Tf{c}", 2) for c in range(4)]
JOBS += [("route", 1), ("rank", 1), ("over", 1)]
BANKS = 8
ACC_BANKS = (0, 1, 2, 3)
LATE = {"Tf0": 4, "Tf1": 5, "Tf2": 6, "Tf3": 7, "route": 4, "rank": 5, "over": 6}
BANK_OF, FILLS, FREED_BEFORE, FREED_AFTER = {}, {}, {}, {}
_fills, _reads = [0] * BANKS, [0] * BANKS
for _n, (_name, _parts) in enumerate(JOBS):
    _b = LATE.get(_name, _n % BANKS)
    BANK_OF[_name], FREED_BEFORE[_name] = _b, _reads[_b]
    _fills[_b] += 1
    _reads[_b] += _parts
    FILLS[_name], FREED_AFTER[_name] = _fills[_b], _reads[_b]
READS_IN_A = list(_reads)
LAST_JOB = {"x_lru": "xl1", "q": "q1", "k": "k1", "v": "v1", "g_lru": "gl1", "xk0": "xk1", "xk1": "xk3",
            "xv0": "xv1", "xv1": "xv3", "out0": "out3", "out1": "out7", "xq0": "xq1", "xq1": "xq3",
            "xo0": "xo1", "xo1": "xo3"}


def block_kernel(nc, x, mem, norm_mix, w_in, conv_w, conv_b, w_rg, b_rg, w_ig, b_ig, lru_lambda,
                 norm_lru_out, norm_attn_out, w_out, norm_cross, norm_mem, w_xq, w_xkv, w_xo,
                 norm_ffn, w_router_group, b_router_group, w_router_expert, b_router_expert,
                 w_gate_up, w_down, norm_final, consts, out):
    with ExitStack() as ctx:
        def sb(name, shape, dt=F32):
            return ctx.enter_context(nc.sbuf_tensor(name, shape, dt))[:]

        def sem(name):
            return ctx.enter_context(nc.semaphore(name))

        ring = sb("ring", [P, UNITS * UNIT])
        ctab = sb("ctab", [P, N_CONSTS])
        params = sb("params", [P, N_ROWS])
        router = sb("router", [P, KC, GROUPS + EXPERTS])
        brow = sb("brow", [1, GROUPS + EXPERTS])
        xtok = sb("xtok", [P, NH, D])
        xg = sb("xg", [P, 2, KC, P])
        ybuf = sb("ybuf", [P, D])
        take = sb("take", [P, NH, BATCH, SLOTS])
        gtake = sb("gtake", [P, NH, BATCH, SLOTS])
        give = sb("give", [P, S])
        th = sb("th", [P, P])
        hid = sb("hid", [P, P])
        hidT = sb("hidT", [P, P])
        rankm = sb("rankm", [P, NH, EXPERTS])
        gates = sb("gates", [P, NH, EXPERTS])
        stat = sb("stat", [P, 64])
        soft = sb("soft", [P, 64])
        lru = sb("lru", [P, 32])
        flag = sb("flag", [P, 1], I32)
        psum = ctx.enter_context(nc.psum_tensor("psum", [P, BANKS, 512], F32))[:]

        def unit(u, n=1):
            return ring[:, u * UNIT:(u + n) * UNIT]

        def scratch(u, off, n):
            return ring[:, u * UNIT + off:u * UNIT + off + n]

        def const(name):
            a, n = CONSTS[name]
            return ctab[:, a:a + n]

        def param(name, c=None):
            a, n = ROWS[name]
            return params[:, a:a + n] if c is None else params[:, a + c:a + c + 1]

        def bank(b):
            return psum[:, b, :]

        def pb(job):
            return bank(BANK_OF[job])

        ident, ones, iota = const("ident"), const("ones"), const("iota")
        cos = const("cos").rearrange("p (h r) -> p h r", h=NH)
        sin = const("sin").rearrange("p (h r) -> p h r", h=NH)

        def tiles(ap, c=CT):
            return ap.rearrange("p (c t) -> p c t", c=c)

        xc = tiles(scratch(4, 0, 1024))
        gate_r = tiles(scratch(4, 1024, 1024))
        gate_i = tiles(scratch(4, 2048, 1024))
        gx = tiles(scratch(4, 3072, 1024))
        PAD = S + CONV - 1
        xlp = tiles(scratch(5, 0, CT * PAD))
        root = tiles(scratch(5, 1040, 1024))
        decay = tiles(scratch(5, 2064, 1024))
        qk = tiles(scratch(6, 0, 2048), NH)
        qkT = tiles(scratch(6, 2048, 2048), 2 * CT)
        memraw = tiles(scratch(7, 0, 2048), NH)
        v = tiles(scratch(7, 0, 1024), NH)
        p0 = tiles(scratch(7, 1024, 1024), HEADS)
        p1 = tiles(scratch(7, 2048, 2048), HEADS)
        pTa = tiles(scratch(8, 0, 2048), HEADS)
        pTb = tiles(scratch(8, 2048, 1024), HEADS)
        rope = scratch(8, 3072, 1024).rearrange("p (k n) -> p k n", k=4)
        xp = scratch(8, 0, 2048).rearrange("p (h n k) -> p h n k", h=NH, n=XH)
        xpT = scratch(8, 2048, 2048).rearrange("p (m n q) -> p m n q", m=NH, n=XH)
        xkT = tiles(scratch(9, 0, 2048), KC)
        xv = tiles(scratch(9, 2048, 2048), NH)
        res = tiles(scratch(10, 0, 2048), NH)
        xT = tiles(scratch(10, 2048, 2048), KC)
        mT = tiles(scratch(11, 0, 2048), KC)
        xqT = mT
        yT = tiles(scratch(11, 2048, 2048), KC)
        oT = yT
        xg_flat = xg.rearrange("p a c t -> p (a c t)")
        sq = xg_flat[:, 0:D]
        sqT = tiles(xg_flat, KC)
        prow = xg_flat[0:N_ROWS, D:D + P]
        bd = tiles(ybuf, 2 * CT)

        def rt(n, m=EXPERTS):
            return ybuf[:, 80 + 64 * n:80 + 64 * n + NH * m].rearrange("p (h e) -> p h e", h=NH)

        logit = ybuf[:, 0:72].rearrange("p (h e) -> p h e", h=NH)

        x_in = x[0].rearrange("(h p) d -> p h d", p=P)
        mem_in = mem[0].rearrange("(h p) d -> p h d", p=P)
        out_d = out[0].rearrange("(h p) d -> p h d", p=P)

        def columns(w, a):
            return w[0].rearrange("(c p) n -> p c n", p=P)[:, :, a:a + 512]

        SOURCE = {
            "x_lru": columns(w_in, 0), "g_lru": columns(w_in, 512), "q": columns(w_in, 1024),
            "k": columns(w_in, 1536), "v": columns(w_in, 2048),
            "xk0": columns(w_xkv, 0), "xk1": columns(w_xkv, 512),
            "xv0": columns(w_xkv, 1024), "xv1": columns(w_xkv, 1536),
            "out0": columns(w_out, 0), "out1": columns(w_out, 512),
            "xq0": columns(w_xq, 0), "xq1": columns(w_xq, 512),
            "xo0": columns(w_xo, 0), "xo1": columns(w_xo, 512),
        }

        def weight(name):
            return unit(UNIT_OF[name]).rearrange("p (c n) -> p c n", c=KC)

        loaded = [sem(f"loaded{u}") for u in range(UNITS)]
        filled = [sem(f"filled{b}") for b in range(BANKS)]
        freed = [sem(f"freed{b}") for b in range(BANKS)]
        x_loaded, mem_loaded, rows_loaded = sem("x_loaded"), sem("mem_loaded"), sem("rows_loaded")
        router_loaded, consts_loaded, bd_loaded = sem("router_loaded"), sem("consts_loaded"), sem("bd_loaded")
        zeroed = sem("zeroed")
        dve_step, act_step = sem("dve_step"), sem("act_step")
        sumsq, meansq, rstd = sem("sumsq"), sem("meansq"), sem("rstd")
        sub_rstd = sem("sub_rstd")
        normed_act, normed_dve = sem("normed_act"), sem("normed_dve")
        conv_done = sem("conv_done")
        lambda_abs, lambda_exp, lru_params = sem("lambda_abs"), sem("lambda_exp"), sem("lru_params")
        tanh_gates, t2_ready, root_ready = sem("tanh_gates"), sem("t2_ready"), sem("root_ready")
        gelu_arg, gelu_tanh = sem("gelu_arg"), sem("gelu_tanh")
        ylru_ready, ylru_squared, ylru_scaled = sem("ylru_ready"), sem("ylru_squared"), sem("ylru_scaled")
        rope_done = sem("rope_done")
        smax, sexp, snorm = sem("smax"), sem("sexp"), sem("snorm")
        xmax, xexp, xnorm = sem("xmax"), sem("xexp"), sem("xnorm")
        acc_set = sem("acc_set")
        group_arg, group_exp, expert_exp = sem("group_arg"), sem("group_exp"), sem("expert_exp")
        chosen, rank_ready = sem("chosen"), sem("rank_ready")
        taken, gtaken = sem("taken"), sem("gtaken")
        gathered, xg_ready = sem("gathered"), sem("xg_ready")
        turned, give_ready = sem("turned"), sem("give_ready")
        gu_done, gu_tanh, gu_half, hid_ready = sem("gu_done"), sem("gu_tanh"), sem("gu_half"), sem("hid_ready")
        hid_turned, hidT_ready = sem("hid_turned"), sem("hidT_ready")
        y_done, y_act, y_dve = sem("y_done"), sem("y_act"), sem("y_dve")
        scattered = sem("scattered")
        ov_turned, ov_xT = sem("ov_turned"), sem("ov_xT")
        ov_loaded, ov_gu, ov_tanh, ov_half, ov_hid = (
            sem("ov_loaded"), sem("ov_gu"), sem("ov_tanh"), sem("ov_half"), sem("ov_hid"))
        ov_hidT_done, ov_hidT, ov_y, ov_gate, ov_scaled, ov_added = (
            sem("ov_hidT_done"), sem("ov_hidT"), sem("ov_y"), sem("ov_gate"), sem("ov_scaled"), sem("ov_added"))
        gain_loaded, final_sq, final_ms, final_rstd, final_out, stored = (
            sem("gain_loaded"), sem("final_sq"), sem("final_ms"), sem("final_rstd"), sem("final_out"), sem("stored"))

        gain_final = unit(EXPERT_UNITS[0][0])[:, 0:D]
        fin = unit(EXPERT_UNITS[0][1])[:, 0:2048].rearrange("p (h n) -> p h n", h=NH)

        ov_gu_w = [unit(u).rearrange("p (c n) -> p c n", c=CT) for u in (6, 7)]
        ov_down_w = unit(8).rearrange("p (c n) -> p c n", c=CT)
        ov_x = tiles(scratch(9, 0, 2048), KC)
        ov_th, ov_h, ov_ht = scratch(9, 2048, 512), scratch(9, 2560, 512), scratch(9, 3072, 512)
        ov_ysc = scratch(10, 0, 1024)
        ov_g = scratch(10, 1024, 1)
        ov_gates = scratch(10, 1088, NH * EXPERTS).rearrange("p (h e) -> p h e", h=NH)

        SS, MS, RS = 0, 16, 32
        SUB, FINAL = 8, 12

        def expert_gu(j, part):
            return unit(EXPERT_UNITS[j][part]).rearrange("p (c n) -> p c n", c=CT)

        def expert_down(j):
            return unit(EXPERT_UNITS[j][2]).rearrange("p (c n) -> p c n", c=CT)

        def await_fill(eng, job):
            eng.wait_ge(filled[BANK_OF[job]], FILLS[job])

        def await_read(eng, job):
            eng.wait_ge(freed[BANK_OF[job]], FREED_AFTER[job])

        block = ctx.enter_context(nc.Block())

        @block.sync
        def _(sp):
            sp.dma_start(res, x_in).then_inc(x_loaded, 16)
            for n, name in enumerate(STREAM):
                if n >= STREAM_UNITS:
                    await_fill(sp, LAST_JOB[STREAM[n - STREAM_UNITS]])
                sp.dma_start(weight(name), SOURCE[name]).then_inc(loaded[UNIT_OF[name]], 16)
                if n == 0:
                    sp.dma_start(memraw, mem_in).then_inc(mem_loaded, 16)

            def load_expert(e, j, part):
                u = EXPERT_UNITS[j][part]
                if part < 2:
                    src = w_gate_up[0, e].rearrange("(two c p) n -> two p c n", p=P, two=2)[part]
                else:
                    src = w_down[0, e].rearrange("(c p) n -> p c n", p=P)
                sp.dma_start(unit(u).rearrange("p (c n) -> p c n", c=CT), src).then_inc(loaded[u], 16)

            await_fill(sp, LAST_JOB["out1"])
            load_expert(0, 0, 1)
            load_expert(0, 0, 2)
            load_expert(1, 1, 0)
            load_expert(1, 1, 1)
            await_fill(sp, LAST_JOB["xq0"])
            load_expert(0, 0, 0)
            await_fill(sp, LAST_JOB["xq1"])
            load_expert(1, 1, 2)
            await_fill(sp, LAST_JOB["xo0"])
            load_expert(2, 2, 0)
            await_fill(sp, LAST_JOB["xo1"])
            load_expert(2, 2, 1)
            load_expert(2, 2, 2)
            load_expert(3, 3, 0)
            load_expert(3, 3, 2)
            await_fill(sp, "route")
            sp.wait_ge(acc_set, 1)
            load_expert(3, 3, 1)
            with sp.Fori(1, BATCHES) as g:
                for j in range(BATCH):
                    sp.wait_ge(gu_done, BATCH * g + (j + 1 - BATCH))
                    load_expert(BATCH * g + j, j, 0)
                    load_expert(BATCH * g + j, j, 1)
                    sp.wait_ge(y_done, BATCH * g + (j + 1 - BATCH))
                    load_expert(BATCH * g + j, j, 2)
            sp.wait_ge(gu_done, EXPERTS - BATCH + 1)
            sp.dma_start(gain_final, norm_final.partition_broadcast(P)).then_inc(gain_loaded, 16)
            await_read(sp, "over")
            over = sp.value_load(flag[0:1, 0:1])
            with sp.If(over > 0):
                sp.wait_ge(scattered, BATCHES)
                with sp.Fori(0, EXPERTS) as e:
                    sp.wait_ge(ov_added, NH * e + 1)
                    for part in range(2):
                        sp.dma_start(ov_gu_w[part], w_gate_up[0, e].rearrange("(two c p) n -> two p c n", p=P, two=2)[part]
                                     ).then_inc(ov_loaded, 16)
                    sp.dma_start(ov_down_w, w_down[0, e].rearrange("(c p) n -> p c n", p=P)).then_inc(ov_loaded, 16)
            for h in range(NH):
                sp.wait_ge(final_out, h + 1)
                sp.dma_start(out_d[:, h], fin[:, h]).then_inc(stored, 16)
            sp.wait_ge(stored, 16 * NH)

        @block.tensor
        def _(pe):
            mm, tr = nc.tensor.matmul, nc.tensor.transpose

            def begin(job):
                if FREED_BEFORE[job]:
                    pe.wait_ge(freed[BANK_OF[job]], FREED_BEFORE[job])
                return pb(job)

            def end(ins, job):
                ins.then_inc(filled[BANK_OF[job]], 1)

            def await_weight(name):
                pe.wait_ge(loaded[UNIT_OF[name]], LOADED[name])

            def turn(prefix, src, stage):
                pe.wait_ge(normed_act, stage)
                pe.wait_ge(normed_dve, stage)
                for c in range(4):
                    b = begin(f"{prefix}{c}")
                    for k in range(2):
                        for h in range(NH):
                            i = tr(b[:, 256 * k + P * h:256 * k + P * h + P],
                                   src[:, h, (2 * c + k) * P:(2 * c + k + 1) * P], ident)
                    end(i, f"{prefix}{c}")

            def channels(name, jobs, src):
                await_weight(name)
                w = weight(name)
                for job, first in zip(jobs, (0, 2)):
                    b = begin(job)
                    for c in range(2):
                        for k in range(KC):
                            i = mm(b[:, 256 * c:256 * c + 256], w[:, k, P * (first + c):P * (first + c) + P],
                                   src[:, k, :], start=k == 0, stop=k == KC - 1)
                    end(i, job)

            def tokens(name, jobs, src, ks=range(KC)):
                await_weight(name)
                w = weight(name)
                for h in range(NH):
                    b = begin(jobs[h])
                    for k in ks:
                        i = mm(b, src[:, k, P * h:P * h + P], w[:, k, :], start=k == ks[0], stop=k == ks[-1])
                    end(i, jobs[h])

            pe.wait_ge(consts_loaded, 16)
            pe.wait_ge(rows_loaded, 16 * len(ROWS))
            end(tr(begin("params")[:, 0:N_ROWS], prow, ident[0:N_ROWS, 0:N_ROWS]), "params")
            turn("Tx", xtok, 1)
            for c in range(4):
                await_read(pe, f"Tx{c}")
            channels("x_lru", ["xl0", "xl1"], xT)
            turn("Tm", memraw, 2)
            tokens("q", ["q0", "q1"], xT)
            tokens("k", ["k0", "k1"], xT)
            pe.wait_ge(bd_loaded, 64)
            pe.wait_ge(conv_done, 1)
            for n, gate in enumerate(("rg", "ig")):
                for c in range(2):
                    b = begin(f"{gate}{c}")
                    for k in range(2):
                        i = mm(b[:, 256 * k:256 * k + 256], bd[:, CT * n + 2 * c + k, :], xc[:, 2 * c + k, :],
                               start=True, stop=True)
                    end(i, f"{gate}{c}")
            tokens("v", ["v0", "v1"], xT)
            pe.wait_ge(rope_done, 1)
            for c in range(4):
                b = begin(f"Tqk{c}")
                for k in range(2):
                    for h in range(NH):
                        i = tr(b[:, 256 * k + P * h:256 * k + P * h + P],
                               qk[:, h, (2 * c + k) * P:(2 * c + k + 1) * P], ident)
                end(i, f"Tqk{c}")
            channels("g_lru", ["gl0", "gl1"], xT)
            for c in range(4):
                await_read(pe, f"Tqk{c}")

            def score(n, tok, keys, out_ap):
                r = slice(HD * (n % 2), HD * (n % 2) + HD)
                return mm(out_ap, qkT[r, n // 2, tok], qkT[r, CT + n // 2, keys], start=True, stop=True)

            for job in ("s0e", "s0o"):
                begin(job)
            for n in range(HEADS):
                job = ("s0e", "s0o")[n % 2]
                i = score(n, slice(0, P), slice(0, P), pb(job)[:, P * (n // 2):P * (n // 2) + P])
                if n >= HEADS - 2:
                    end(i, job)
            for c in range(4):
                begin(f"s1{c}")
            for n in range(HEADS):
                job, k = f"s1{2 * (n // 4) + n % 2}", n // 2 % 2
                i = score(n, slice(P, S), slice(0, S), pb(job)[:, 256 * k:256 * k + 256])
                if k:
                    end(i, job)
            for c in range(4):
                await_read(pe, f"Tm{c}")
            channels("xk0", ["xk0", "xk1"], mT)
            channels("xk1", ["xk2", "xk3"], mT)
            pe.wait_ge(snorm, 2)
            for c in range(4):
                b = begin(f"Tp{c}")
                for k in range(2):
                    n = 2 * c + k
                    tr(b[:, 256 * k:256 * k + P], p0[:, n, :], ident)
                    i = tr(b[:, 256 * k + P:256 * k + 256], p1[:, n, 0:P], ident)
                end(i, f"Tp{c}")
            for c in range(2):
                b = begin(f"Tp{4 + c}")
                for k in range(4):
                    i = tr(b[:, P * k:P * k + P], p1[:, 4 * c + k, P:S], ident)
                end(i, f"Tp{4 + c}")
            for c in range(2):
                tokens(f"xv{c}", [f"xv{2 * c}", f"xv{2 * c + 1}"], mT)
            for c in range(6):
                await_read(pe, f"Tp{c}")
            for h in range(NH):
                await_read(pe, f"v{h}")
            for c in range(2):
                b = begin(f"pv{c}")
                for n in range(4 * c, 4 * c + 4):
                    r = slice(HD * (n % 2), HD * (n % 2) + HD)
                    k = n // 2 % 2
                    mm(b[r, 256 * k:256 * k + 256], v[:, 0, HD * n:HD * n + HD], pTa[:, n, :],
                       start=True, stop=False, skip_group_check=True)
                    i = mm(b[r, 256 * k + P:256 * k + 256], v[:, 1, HD * n:HD * n + HD], pTb[:, n, :],
                           start=False, stop=True, skip_group_check=True)
                end(i, f"pv{c}")
            pe.wait_ge(ylru_squared, 1)
            for c in range(2):
                await_read(pe, f"pv{c}")
            b = begin("ss")
            for part in range(2):
                for h in range(NH):
                    for c in range(CT):
                        i = mm(b[:, 2 * part + h:2 * part + h + 1], sqT[:, CT * part + c, P * h:P * h + P],
                               ones[:, 0:1], start=c == 0, stop=c == CT - 1)
            end(i, "ss")
            pe.wait_ge(ylru_scaled, 1)
            for cb in range(2):
                tokens(f"out{cb}", [f"out{4 * cb}", f"out{4 * cb + 1}"], yT, range(0, CT))
                tokens(f"out{cb}", [f"out{4 * cb + 2}", f"out{4 * cb + 3}"], yT, range(CT, KC))
            turn("Th", xtok, 3)
            for c in range(4):
                await_read(pe, f"Th{c}")
            channels("xq0", ["xq0", "xq1"], xT)
            channels("xq1", ["xq2", "xq3"], xT)
            for c in range(4):
                await_read(pe, f"xk{c}")
                await_read(pe, f"xq{c}")
            for h in range(NH):
                for c in range(2):
                    b = begin(f"xs{2 * h + c}")
                    for k in range(2):
                        n = 2 * c + k
                        for m in range(2):
                            i = mm(b[:, 256 * k:256 * k + 256], xqT[:, 2 * n + m, P * h:P * h + P],
                                   xkT[:, 2 * n + m, :], start=m == 0, stop=m == 1)
                    end(i, f"xs{2 * h + c}")
            pe.wait_ge(xnorm, 2)
            for m in range(2):
                for c in range(2):
                    b = begin(f"Txp{2 * m + c}")
                    for k in range(2):
                        for h in range(NH):
                            i = tr(b[:, 256 * k + P * h:256 * k + P * h + P],
                                   xp[:, h, 2 * c + k, P * m:P * m + P], ident)
                    end(i, f"Txp{2 * m + c}")
            for c in range(4):
                await_read(pe, f"Txp{c}")
                await_read(pe, f"xv{c}")
            for n in range(XH):
                b = begin(f"xpv{n}")
                for k in range(2):
                    for m in range(2):
                        i = mm(b[:, 256 * k:256 * k + 256], xv[:, m, XHD * n + P * k:XHD * n + P * k + P],
                               xpT[:, m, n, :], start=m == 0, stop=m == 1)
                end(i, f"xpv{n}")
            for n in range(XH):
                await_read(pe, f"xpv{n}")
            for cb in range(2):
                tokens(f"xo{cb}", [f"xo{2 * cb}", f"xo{2 * cb + 1}"], oT)
            for c in range(4):
                await_read(pe, f"xo{c}")
            for n, b in enumerate(ACC_BANKS):
                pe.wait_ge(freed[b], READS_IN_A[b])
                i = mm(bank(b), ident, res[:, n // 2, 512 * (n % 2):512 * (n % 2) + 512], start=True,
                       stop=True, skip_group_check=True)
            i.then_inc(acc_set, 1)
            turn("Tf", xtok, 4)
            for c in range(4):
                await_read(pe, f"Tf{c}")
            pe.wait_ge(router_loaded, 64)
            b = begin("route")
            for h in range(NH):
                o = b[:, 64 * h:64 * h + GROUPS + EXPERTS]
                for k in range(KC):
                    mm(o, xT[:, k, P * h:P * h + P], router[:, k, :], start=k == 0, stop=False)
                i = mm(o, ones[0:1, :], brow, start=False, stop=True)
            end(i, "route")
            pe.wait_ge(chosen, 1)
            picked = rt(4)
            b = begin("rank")
            mm(b[:, 0:EXPERTS], const("before"), picked[:, 0], start=True, stop=True)
            mm(b[:, EXPERTS:2 * EXPERTS], const("before"), picked[:, 1], start=True, stop=False)
            end(mm(b[:, EXPERTS:2 * EXPERTS], ones, picked[:, 0], start=False, stop=True), "rank")
            pe.wait_ge(rank_ready, 1)
            b = begin("over")
            end(mm(b[:, 0:1], ones, soft[:, 0:1], start=True, stop=True), "over")

            GATHER, HY, GU = 4, 6, 7
            await_read(pe, "rank")
            await_read(pe, "over")
            with pe.Fori(0, BATCHES) as g:
                pe.wait_ge(taken, g + 1)
                for k in range(KC):
                    for h in range(NH):
                        i = mm(bank(GATHER + k // 4)[:, P * (k % 4):P * (k % 4) + P], xtok[:, h, P * k:P * k + P],
                               take[:, h].rearrange("p e s -> p (e s)"), start=h == 0, stop=h == NH - 1)
                i.then_inc(gathered, 1)
                pe.wait_ge(gtaken, g + 1)
                for h in range(NH):
                    i = tr(bank(HY)[:, P * h:P * h + P], gtake[:, h].rearrange("p e s -> p (e s)"), ident)
                i.then_inc(turned, 1)
                pe.wait_ge(xg_ready, g + 1)
                for j in range(BATCH):
                    n = BATCH * g + (j + 1)
                    half = bank(GU)[:, 256 * (j % 2):256 * (j % 2) + 256]
                    for part in range(2):
                        u = EXPERT_UNITS[j][part]
                        pe.wait_ge(loaded[u], 16 * g + 16 * (LOADS_IN_A[u] + 1))
                        w = expert_gu(j, part).rearrange("p c (two n) -> p c two n", two=2)
                        for k in range(CT):
                            for strip in range(BATCH):
                                i = mm(half[SLOTS * strip:SLOTS * strip + SLOTS],
                                       xg[:, 0, CT * part + k, SLOTS * j:SLOTS * j + SLOTS],
                                       w[:, k, :, P * strip:P * strip + P],
                                       start=part == 0 and k == 0, stop=part == 1 and k == CT - 1,
                                       tile_position=(0, SLOTS * strip))
                    i.then_inc(gu_done, 1)
                    if j:
                        pe.wait_ge(y_act, n - 1)
                        pe.wait_ge(y_dve, n - 1)
                    else:
                        pe.wait_ge(give_ready, g + 1)
                    pe.wait_ge(hid_ready, n)
                    tr(bank(HY)[:, 256:256 + P], hid, ident).then_inc(hid_turned, 1)
                    u = EXPERT_UNITS[j][2]
                    pe.wait_ge(loaded[u], 16 * g + 16 * (LOADS_IN_A[u] + 1))
                    w = expert_down(j)
                    pe.wait_ge(hidT_ready, n)
                    for k in range(CT):
                        for strip in range(BATCH):
                            i = mm(bank(HY)[SLOTS * strip:SLOTS * strip + SLOTS, 0:256],
                                   hidT[:, SLOTS * k:SLOTS * k + SLOTS], w[:, k, 256 * strip:256 * strip + 256],
                                   start=k == 0, stop=k == CT - 1, tile_position=(0, SLOTS * strip))
                    i.then_inc(y_done, 1)
                pe.wait_ge(y_act, BATCH * g + BATCH)
                pe.wait_ge(y_dve, BATCH * g + BATCH)
                for n, b in enumerate(ACC_BANKS):
                    i = mm(bank(b), give[:, P * (n // 2):P * (n // 2) + P], ybuf[:, 512 * (n % 2):512 * (n % 2) + 512],
                           start=False, stop=True, skip_group_check=True)
                i.then_inc(scattered, 1)

            over = pe.value_load(flag[0:1, 0:1])
            with pe.If(over > 0):
                for half in range(2):
                    for k in range(4):
                        for h in range(NH):
                            i = tr(bank(GATHER + k // 2 + 2 * half)[:, 256 * (k % 2) + P * h:256 * (k % 2) + P * h + P],
                                   xtok[:, h, P * (4 * half + k):P * (4 * half + k) + P], ident)
                i.then_inc(ov_turned, 1)
                pe.wait_ge(ov_xT, 1)
                mm(bank(GATHER)[0:1, 0:1], ident[0:1, 0:1], ident[0:1, 0:1], start=True, stop=True).then_inc(ov_added, 1)
                with pe.Fori(0, EXPERTS) as e:
                    pe.wait_ge(ov_loaded, 48 * e + 48)
                    for h in range(NH):
                        n = NH * e + (h + 1)
                        for c in range(2):
                            for k in range(KC):
                                i = mm(bank(GATHER + c), ov_x[:, k, P * h:P * h + P],
                                       ov_gu_w[k // CT][:, k % CT, 512 * c:512 * c + 512], start=k == 0, stop=k == KC - 1)
                        i.then_inc(ov_gu, 1)
                        pe.wait_ge(ov_hid, n)
                        for k in range(CT):
                            i = tr(bank(HY)[:, P * k:P * k + P], ov_h[:, P * k:P * k + P], ident)
                        i.then_inc(ov_hidT_done, 1)
                        pe.wait_ge(ov_hidT, n)
                        for c in range(2):
                            for k in range(CT):
                                i = mm(bank(GATHER + c), ov_ht[:, P * k:P * k + P],
                                       ov_down_w[:, k, 512 * c:512 * c + 512], start=k == 0, stop=k == CT - 1)
                        i.then_inc(ov_y, 1)
                        pe.wait_ge(ov_scaled, n)
                        for c in range(2):
                            i = mm(bank(ACC_BANKS[2 * h + c]), ident, ov_ysc[:, 512 * c:512 * c + 512], start=False,
                                   stop=True, skip_group_check=True)
                        i.then_inc(ov_added, 1)

        @block.scalar
        def _(act):
            steps = [0]

            def link(ins):
                steps[0] += 1
                ins.then_inc(act_step, 1)
                act.wait_ge(act_step, steps[0])

            def copy(dst, src, scale=1.0, bias=0.0):
                return nc.scalar.activation(dst, src, ACT.Identity, scale=scale, bias=bias)

            def release(ins, job):
                ins.then_inc(freed[BANK_OF[job]], 1)

            act.dma_start(ctab, consts).then_inc(consts_loaded, 16)
            for name, src in (("norm_mix", norm_mix), ("norm_mem", norm_mem), ("norm_cross", norm_cross),
                              ("norm_ffn", norm_ffn), ("norm_lru_out", norm_lru_out),
                              ("norm_attn_out", norm_attn_out), ("conv_b", conv_b), ("b_rg", b_rg),
                              ("b_ig", b_ig), ("lru_lambda", lru_lambda), ("conv_w", conv_w[0])):
                a, n = ROWS[name]
                act.dma_start(prow[a:a + n], src.rearrange("w (c p) -> (w c) p", p=P)).then_inc(rows_loaded, 16)
            act.wait_ge(zeroed, 1)
            for n, w in enumerate((w_rg, w_ig)):
                for par in range(2):
                    r = slice(HD * par, HD * par + HD)
                    act.dma_start(bd[r, CT * n:CT * n + CT, HD * par:HD * par + HD],
                                  w[0].rearrange("(c two) i j -> two i c j", two=2)[par]).then_inc(bd_loaded, 16)
            act.dma_start(router[:, :, 0:GROUPS], w_router_group[0].rearrange("(c p) n -> p c n", p=P)
                          ).then_inc(router_loaded, 16)
            act.dma_start(router[:, :, GROUPS:], w_router_expert[0].rearrange("(c p) n -> p c n", p=P)
                          ).then_inc(router_loaded, 16)
            act.dma_start(brow[:, 0:GROUPS], b_router_group).then_inc(router_loaded, 16)
            act.dma_start(brow[:, GROUPS:], b_router_expert).then_inc(router_loaded, 16)

            def norm(stage, src, dst):
                for h in range(NH):
                    col = SS + 2 * (stage - 1) + h
                    nc.scalar.activation(sq, src[:, h], ACT.Square, accum_out=stat[:, col:col + 1]
                                         ).then_inc(sumsq, 1)
                    act.wait_ge(sumsq, 2 * (stage - 1) + h + 1)
                act.wait_ge(rstd, stage)
                col = RS + 2 * (stage - 1) + 1
                copy(dst[:, 1], src[:, 1], stat[:, col:col + 1]).then_inc(normed_act, 1)

            def evacuate_turned(prefix, dst, gain):
                for c in (0, 2):
                    await_fill(act, f"{prefix}{c}")
                    for k in range(2):
                        release(copy(dst[:, 2 * c + k], pb(f"{prefix}{c}")[:, 256 * k:256 * k + 256],
                                     param(gain, 2 * c + k)), f"{prefix}{c}")

            act.wait_ge(x_loaded, 16)
            norm(1, res, xtok)
            await_fill(act, "params")
            release(copy(params, pb("params")[:, 0:N_ROWS]), "params")
            await_read(act, "params")
            evacuate_turned("Tx", xT, "norm_mix")
            act.wait_ge(lambda_abs, 1)
            nc.scalar.activation(lru[:, 12:16], lru[:, 12:16], ACT.Exp, scale=-1.0).then_inc(lambda_exp, 1)
            act.wait_ge(mem_loaded, 16)
            norm(2, memraw, memraw)
            await_fill(act, "xl0")
            release(copy(xlp[:, 0:2, CONV - 1:], pb("xl0").rearrange("p (c t) -> p c t", c=2)), "xl0")
            evacuate_turned("Tm", mT, "norm_mem")
            for n, name in enumerate(("q", "k")):
                for h in range(NH):
                    await_fill(act, f"{name}{h}")
                    release(copy(qk[:, h, 512 * n:512 * n + 512], pb(f"{name}{h}")), f"{name}{h}")
            act.wait_ge(lru_params, 1)
            for n, (gate, dst) in enumerate((("rg", gate_r), ("ig", gate_i))):
                for c in range(2):
                    await_fill(act, f"{gate}{c}")
                    for k in range(2):
                        t = 2 * c + k
                        release(nc.scalar.activation(dst[:, t], pb(f"{gate}{c}")[:, 256 * k:256 * k + 256], ACT.Tanh,
                                                     scale=0.5, bias=lru[:, 4 * n + t:4 * n + t + 1]), f"{gate}{c}")
            for c in range(2):
                await_read(act, f"rg{c}")
            for t in range(CT):
                i = nc.scalar.activation(gate_r[:, t], gate_r[:, t], ACT.Tanh, scale=lru[:, 8 + t:9 + t],
                                         bias=lru[:, 8 + t:9 + t])
            i.then_inc(t2_ready, 1)
            act.wait_ge(t2_ready, 1)
            nc.scalar.activation(root, gate_r, ACT.Sqrt).then_inc(root_ready, 1)
            for h in range(NH):
                await_fill(act, f"v{h}")
                release(copy(v[:, h], pb(f"v{h}")), f"v{h}")
            for c in (0, 2):
                await_fill(act, f"Tqk{c}")
                release(copy(qkT[:, 2 * c:2 * c + 2], pb(f"Tqk{c}").rearrange("p (c t) -> p c t", c=2)), f"Tqk{c}")
            for c in range(2):
                await_fill(act, f"gl{c}")
                release(copy(gx[:, 2 * c:2 * c + 2], pb(f"gl{c}").rearrange("p (c t) -> p c t", c=2)), f"gl{c}")
            for h, p in enumerate((p0, p1)):
                act.wait_ge(smax, h + 1)
                for n in range(HEADS):
                    i = nc.scalar.activation(p[:, n], p[:, n], ACT.Exp, bias=soft[:, 8 * h + n:8 * h + n + 1],
                                             accum_out=soft[:, 16 + 8 * h + n:17 + 8 * h + n])
                i.then_inc(sexp, 1)
            act.wait_ge(gelu_arg, 1)
            nc.scalar.activation(gate_i, gate_r, ACT.Tanh, scale=GELU_IN).then_inc(gelu_tanh, 1)
            for c in (0, 2):
                await_fill(act, f"xk{c}")
                release(copy(xkT[:, 2 * c:2 * c + 2], pb(f"xk{c}").rearrange("p (c t) -> p c t", c=2)), f"xk{c}")
            for c in (0, 2):
                await_fill(act, f"Tp{c}")
                release(copy(pTa[:, 2 * c:2 * c + 2], pb(f"Tp{c}").rearrange("p (n t) -> p n t", n=2)), f"Tp{c}")
            await_fill(act, "Tp4")
            release(copy(pTb[:, 0:4], pb("Tp4").rearrange("p (n t) -> p n t", n=4)), "Tp4")
            act.wait_ge(ylru_ready, 1)
            nc.scalar.activation(sqT[:, 0:CT], yT[:, 0:CT], ACT.Square).then_inc(ylru_squared, 1)
            for c in (0, 2):
                await_fill(act, f"xv{c}")
                release(copy(xv[:, 0, 256 * c:256 * c + 512], pb(f"xv{c}")), f"xv{c}")
            for c in range(2):
                await_fill(act, f"pv{c}")
                release(nc.scalar.activation(sqT[:, CT + 2 * c:CT + 2 * c + 2],
                                             pb(f"pv{c}").rearrange("p (c t) -> p c t", c=2), ACT.Square), f"pv{c}")
            for c in range(8):
                await_read(act, f"out{c}")
            await_fill(act, "ss")
            norm(3, res, xtok)
            evacuate_turned("Th", xT, "norm_cross")
            for c in (0, 2):
                await_fill(act, f"xq{c}")
                release(copy(xqT[:, 2 * c:2 * c + 2], pb(f"xq{c}").rearrange("p (c t) -> p c t", c=2)), f"xq{c}")
            for h in range(NH):
                for c in range(2):
                    job = f"xs{2 * h + c}"
                    act.wait_ge(xmax, 2 * h + c + 1)
                    for k in range(2):
                        n = 2 * c + k
                        i = nc.scalar.activation(xp[:, h, n], pb(job)[:, 256 * k:256 * k + 256], ACT.Exp,
                                                 scale=XHD ** -0.5, bias=soft[:, 32 + 4 * h + n:33 + 4 * h + n],
                                                 accum_out=soft[:, 40 + 4 * h + n:41 + 4 * h + n])
                    release(i, job)
            for c in (0, 2):
                await_fill(act, f"Txp{c}")
                release(copy(xpT[:, c // 2, 0:2], pb(f"Txp{c}").rearrange("p (n t) -> p n t", n=2)), f"Txp{c}")
            for c in (0, 2):
                await_fill(act, f"xpv{c}")
                release(copy(oT[:, 2 * c:2 * c + 2], pb(f"xpv{c}").rearrange("p (c t) -> p c t", c=2)), f"xpv{c}")
            for c in range(4):
                await_read(act, f"xo{c}")
            norm(4, res, xtok)
            evacuate_turned("Tf", xT, "norm_ffn")
            act.wait_ge(group_arg, 1)
            nc.scalar.activation(rt(9, GROUPS), rt(8, GROUPS), ACT.Exp).then_inc(group_exp, 1)
            act.wait_ge(chosen, 1)
            nc.scalar.activation(soft[:, 56:58], soft[:, 54:56], ACT.Exp).then_inc(expert_exp, 1)

            GU, HY = 7, 6
            with act.Fori(0, BATCHES) as g:
                act.wait_ge(turned, g + 1)
                copy(give, bank(HY)[:, 0:S]).then_inc(give_ready, 1)
                for j in range(BATCH):
                    n = BATCH * g + (j + 1)
                    act.wait_ge(gu_done, n)
                    nc.scalar.activation(th, bank(GU)[:, 256 * (j % 2):256 * (j % 2) + P], ACT.Tanh, scale=0.5
                                         ).then_inc(gu_tanh, 1)
                    act.wait_ge(hid_turned, n)
                    copy(hidT, bank(HY)[:, 256:256 + P]).then_inc(hidT_ready, 1)
                    act.wait_ge(y_done, n)
                    for strip in range(2):
                        r = slice(SLOTS * strip, SLOTS * strip + SLOTS)
                        i = copy(ybuf[SLOTS * j:SLOTS * j + SLOTS, 256 * strip:256 * strip + 256], bank(HY)[r, 0:256])
                    i.then_inc(y_act, 1)

            await_read(act, "over")
            over = act.value_load(flag[0:1, 0:1])
            with act.If(over > 0):
                with act.Fori(0, EXPERTS) as e:
                    for h in range(NH):
                        n = NH * e + (h + 1)
                        act.wait_ge(ov_gu, n)
                        nc.scalar.activation(ov_th, bank(4), ACT.Tanh, scale=0.5).then_inc(ov_tanh, 1)
                        act.wait_ge(ov_hidT_done, n)
                        copy(ov_ht, bank(HY)).then_inc(ov_hidT, 1)
                act.wait_ge(ov_added, NH * EXPERTS + 1)
            act.wait_ge(scattered, BATCHES)
            for h in range(NH):
                nc.scalar.activation(sq.rearrange("p (c n) -> p c n", c=2), psum[:, 2 * h:2 * h + 2, :], ACT.Square,
                                     accum_out=stat[:, SS + FINAL + h:SS + FINAL + h + 1]).then_inc(final_sq, 1)
                act.wait_ge(final_sq, h + 1)

        @block.gpsimd
        def _(pool):
            nc.gpsimd.memset(ybuf, 0.0).then_inc(zeroed, 1)
            nc.gpsimd.memset(xlp[:, :, 0:CONV - 1], 0.0).then_inc(zeroed, 1)
            pool.wait_ge(consts_loaded, 16)

            def power(col, n, done):
                nc.gpsimd.tensor_tensor(stat[:, RS + col:RS + col + n], stat[:, MS + col:MS + col + n],
                                        const("power")[:, 0:n], ALU.pow).then_inc(done, 1)

            for stage in (1, 2):
                pool.wait_ge(meansq, stage)
                power(2 * (stage - 1), 2, rstd)
            await_read(pool, "ss")
            power(SUB, 4, sub_rstd)
            for stage in (3, 4):
                pool.wait_ge(meansq, stage)
                power(2 * (stage - 1), 2, rstd)
            pool.wait_ge(final_ms, 1)
            power(FINAL, 2, final_rstd)

        @block.vector
        def _(dve):
            steps = [0]
            V = nc.vector

            def link(ins):
                steps[0] += 1
                ins.then_inc(dve_step, 1)
                dve.wait_ge(dve_step, steps[0])

            def release(ins, job):
                ins.then_inc(freed[BANK_OF[job]], 1)

            def mean(col, n, width):
                return V.tensor_scalar(stat[:, MS + col:MS + col + n], stat[:, SS + col:SS + col + n],
                                       1.0 / width, EPS, ALU.mult, ALU.add)

            def norm(stage, src, dst):
                dve.wait_ge(sumsq, 2 * stage)
                mean(2 * (stage - 1), 2, D).then_inc(meansq, 1)
                dve.wait_ge(rstd, stage)
                col = RS + 2 * (stage - 1)
                V.tensor_scalar(dst[:, 0], src[:, 0], stat[:, col:col + 1], None, ALU.mult).then_inc(normed_dve, 1)

            def evacuate_turned(prefix, dst, gain):
                for c in (1, 3):
                    await_fill(dve, f"{prefix}{c}")
                    for k in range(2):
                        release(V.tensor_scalar(dst[:, 2 * c + k], pb(f"{prefix}{c}")[:, 256 * k:256 * k + 256],
                                                param(gain, 2 * c + k), None, ALU.mult), f"{prefix}{c}")

            norm(1, res, xtok)
            await_read(dve, "params")
            evacuate_turned("Tx", xT, "norm_mix")
            V.scalar_tensor_tensor(lru[:, 12:16], param("lru_lambda"), -1.0, param("lru_lambda"), ALU.mult, ALU.max
                                   ).then_inc(lambda_abs, 1)
            norm(2, memraw, memraw)
            dve.wait_ge(lambda_exp, 1)
            z, s, s2, ser = lru[:, 12:16], lru[:, 16:20], lru[:, 20:24], lru[:, 24:28]
            link(V.tensor_scalar(s, z, 2.0, None, ALU.add))
            link(V.reciprocal(s, s))
            link(V.tensor_tensor(s, s, z, ALU.mult))
            link(V.tensor_tensor(s2, s, s, ALU.mult))
            link(V.tensor_scalar(ser, s2, 1.0 / 17, 1.0 / 15, ALU.mult, ALU.add))
            for odd in (13, 11, 9, 7, 5, 3, 1):
                link(V.tensor_tensor(ser, ser, s2, ALU.mult))
                link(V.tensor_scalar(ser, ser, 1.0 / odd, None, ALU.add))
            link(V.tensor_tensor(ser, ser, s, ALU.mult))
            link(V.tensor_scalar(s2, param("lru_lambda"), -1.0, 0.0, ALU.mult, ALU.max))
            link(V.scalar_tensor_tensor(s, ser, 2.0, s2, ALU.mult, ALU.add))
            link(V.tensor_scalar(lru[:, 8:12], s, 8.0 / 4, None, ALU.mult))
            link(V.tensor_scalar(lru[:, 0:4], param("b_rg"), 0.5, None, ALU.mult))
            V.tensor_scalar(lru[:, 4:8], param("b_ig"), 0.5, None, ALU.mult).then_inc(lru_params, 1)
            await_fill(dve, "xl1")
            release(V.tensor_copy(xlp[:, 2:4, CONV - 1:], pb("xl1").rearrange("p (c t) -> p c t", c=2)), "xl1")
            evacuate_turned("Tm", mT, "norm_mem")
            await_read(dve, "xl0")
            await_read(dve, "xl1")
            dve.wait_ge(zeroed, 2)
            a, _ = ROWS["conv_w"]
            for w in range(CONV):
                for t in range(CT):
                    tap = params[:, a + CT * w + t:a + CT * w + t + 1]
                    src = xlp[:, t, w:w + S]
                    if w == 0:
                        i = V.tensor_scalar(xc[:, t], src, tap, param("conv_b", t), ALU.mult, ALU.add)
                    else:
                        i = V.scalar_tensor_tensor(xc[:, t], src, tap, xc[:, t], ALU.mult, ALU.add)
                if w < CONV - 1:
                    link(i)
            i.then_inc(conv_done, 1)
            for name in ("q", "k"):
                for h in range(NH):
                    await_read(dve, f"{name}{h}")
            for h in range(NH):
                heads = qk[:, h].rearrange("p (n d) -> p n d", n=2 * HEADS)
                x1, x2 = heads[:, :, 0:HALF_ROT], heads[:, :, HALF_ROT:2 * HALF_ROT]
                shape = [P, 2 * HEADS, HALF_ROT]
                c_, s_ = cos[:, h].unsqueeze(1).to_broadcast(shape), sin[:, h].unsqueeze(1).to_broadcast(shape)
                t = [rope[:, k, P * h:P * h + P].rearrange("p (n r) -> p n r", n=2 * HEADS) for k in range(4)]
                V.tensor_tensor(t[0], x1, c_, ALU.mult)
                V.tensor_tensor(t[1], x2, s_, ALU.mult)
                V.tensor_tensor(t[2], x2, c_, ALU.mult)
                link(V.tensor_tensor(t[3], x1, s_, ALU.mult))
                V.tensor_tensor(x1, t[0], t[1], ALU.subtract)
                i = V.tensor_tensor(x2, t[2], t[3], ALU.add)
            i.then_inc(rope_done, 1)
            dve.wait_ge(t2_ready, 1)
            link(V.tensor_scalar(decay, gate_r, 1.0, None, ALU.add))
            link(V.reciprocal(decay, decay))
            for c in range(2):
                await_read(dve, f"ig{c}")
            link(V.scalar_tensor_tensor(gate_i, gate_i, 1.0, xc, ALU.add, ALU.mult))
            dve.wait_ge(root_ready, 1)
            link(V.tensor_tensor(root, root, decay, ALU.mult))
            V.tensor_scalar(decay, decay, 2.0, -1.0, ALU.mult, ALU.add)
            link(V.tensor_tensor(root, root, gate_i, ALU.mult))
            for c in (1, 3):
                await_fill(dve, f"Tqk{c}")
                release(V.tensor_copy(qkT[:, 2 * c:2 * c + 2], pb(f"Tqk{c}").rearrange("p (c t) -> p c t", c=2)), f"Tqk{c}")
            for t in range(CT):
                i = V.tensor_tensor_scan(xc[:, t], decay[:, t], root[:, t], 0.0, ALU.mult, ALU.add)
            link(i)
            for job, par in (("s0e", 0), ("s0o", 1)):
                await_fill(dve, job)
                release(V.scalar_tensor_tensor(p0[:, par::2], pb(job).rearrange("p (n k) -> p n k", n=4), HD ** -0.5,
                                               const("causal")[:, P:S].unsqueeze(1).to_broadcast([P, 4, P]),
                                               ALU.mult, ALU.add), job)
            for job in ("s0e", "s0o"):
                await_read(dve, job)
            V.tensor_reduce(soft[:, 0:8], p0, AX.X, ALU.max, negate=True).then_inc(smax, 1)
            for c in range(4):
                await_fill(dve, f"s1{c}")
                first = 4 * (c // 2) + c % 2
                release(V.scalar_tensor_tensor(p1[:, first:first + 3:2],
                                               pb(f"s1{c}").rearrange("p (n k) -> p n k", n=2), HD ** -0.5,
                                               const("causal").unsqueeze(1).to_broadcast([P, 2, S]),
                                               ALU.mult, ALU.add), f"s1{c}")
            for c in range(4):
                await_read(dve, f"s1{c}")
            V.tensor_reduce(soft[:, 8:16], p1, AX.X, ALU.max, negate=True).then_inc(smax, 1)
            for c in range(2):
                await_read(dve, f"gl{c}")
            link(V.tensor_tensor(gate_r, gx, gx, ALU.mult))
            link(V.tensor_scalar(gate_r, gate_r, GELU_CUBE, 1.0, ALU.mult, ALU.add))
            V.tensor_tensor(gate_r, gate_r, gx, ALU.mult).then_inc(gelu_arg, 1)
            for h, p in enumerate((p0, p1)):
                dve.wait_ge(sexp, h + 1)
                keys = P * (h + 1)
                link(V.reciprocal(soft[:, 16 + 8 * h:24 + 8 * h], soft[:, 16 + 8 * h:24 + 8 * h]))
                V.tensor_tensor(p, p, soft[:, 16 + 8 * h:24 + 8 * h].unsqueeze(2).to_broadcast([P, HEADS, keys]),
                                ALU.mult).then_inc(snorm, 1)
            dve.wait_ge(gelu_tanh, 1)
            link(V.scalar_tensor_tensor(gate_i, gate_i, 1.0, gx, ALU.add, ALU.mult))
            V.scalar_tensor_tensor(yT[:, 0:CT], gate_i, 0.5, xc, ALU.mult, ALU.mult).then_inc(ylru_ready, 1)
            for c in (1, 3):
                await_fill(dve, f"xk{c}")
                release(V.tensor_copy(xkT[:, 2 * c:2 * c + 2], pb(f"xk{c}").rearrange("p (c t) -> p c t", c=2)), f"xk{c}")
            for c in (1, 3):
                await_fill(dve, f"Tp{c}")
                release(V.tensor_copy(pTa[:, 2 * c:2 * c + 2], pb(f"Tp{c}").rearrange("p (n t) -> p n t", n=2)), f"Tp{c}")
            await_fill(dve, "Tp5")
            release(V.tensor_copy(pTb[:, 4:8], pb("Tp5").rearrange("p (n t) -> p n t", n=4)), "Tp5")
            dve.wait_ge(ylru_squared, 1)
            for t in range(CT):
                i = V.tensor_scalar(yT[:, t], yT[:, t], param("norm_lru_out", t), None, ALU.mult)
            i.then_inc(ylru_scaled, 1)
            for c in (1, 3):
                await_fill(dve, f"xv{c}")
                release(V.tensor_copy(xv[:, 1, 256 * (c - 1):256 * (c - 1) + 512], pb(f"xv{c}")), f"xv{c}")
            for c in range(2):
                dve.wait_ge(freed[BANK_OF[f"pv{c}"]], FREED_BEFORE[f"pv{c}"] + 1)
                for k in range(2):
                    i = V.tensor_scalar(yT[:, CT + 2 * c + k], pb(f"pv{c}")[:, 256 * k:256 * k + 256],
                                        param("norm_attn_out", 2 * c + k), None, ALU.mult)
                release(i, f"pv{c}")
            await_fill(dve, "ss")
            release(V.tensor_scalar(stat[:, MS + SUB:MS + SUB + 4], pb("ss")[:, 0:4], 1.0 / DL, EPS, ALU.mult, ALU.add), "ss")
            await_read(dve, "ss")
            dve.wait_ge(sub_rstd, 1)
            for cb in range(2):
                for part in range(2):
                    for h in range(NH):
                        job = f"out{4 * cb + 2 * part + h}"
                        await_fill(dve, job)
                        o = res[:, h, 512 * cb:512 * cb + 512]
                        col = RS + SUB + 2 * part + h
                        if part:
                            await_read(dve, f"out{4 * cb + h}")
                        release(V.scalar_tensor_tensor(o, pb(job), stat[:, col:col + 1], o, ALU.mult, ALU.add), job)
            for c in range(8):
                await_read(dve, f"out{c}")
            norm(3, res, xtok)
            evacuate_turned("Th", xT, "norm_cross")
            for c in (1, 3):
                await_fill(dve, f"xq{c}")
                release(V.tensor_copy(xqT[:, 2 * c:2 * c + 2], pb(f"xq{c}").rearrange("p (c t) -> p c t", c=2)), f"xq{c}")
            for h in range(NH):
                for c in range(2):
                    job, col = f"xs{2 * h + c}", 32 + 4 * h + 2 * c
                    await_fill(dve, job)
                    release(V.tensor_reduce(soft[:, col:col + 2], pb(job).rearrange("p (n k) -> p n k", n=2), AX.X,
                                            ALU.max, negate=True), job)
                    dve.wait_ge(freed[BANK_OF[job]], FREED_BEFORE[job] + 1)
                    V.tensor_scalar(soft[:, col:col + 2], soft[:, col:col + 2], XHD ** -0.5, None, ALU.mult
                                    ).then_inc(xmax, 1)
            for h in range(NH):
                for c in range(2):
                    await_read(dve, f"xs{2 * h + c}")
                r = soft[:, 40 + 4 * h:44 + 4 * h]
                link(V.reciprocal(r, r))
                V.tensor_tensor(xp[:, h], xp[:, h], r.unsqueeze(2).to_broadcast([P, XH, S]), ALU.mult).then_inc(xnorm, 1)
            for c in (1, 3):
                await_fill(dve, f"Txp{c}")
                release(V.tensor_copy(xpT[:, c // 2, 2:4], pb(f"Txp{c}").rearrange("p (n t) -> p n t", n=2)), f"Txp{c}")
            for c in (1, 3):
                await_fill(dve, f"xpv{c}")
                release(V.tensor_copy(oT[:, 2 * c:2 * c + 2], pb(f"xpv{c}").rearrange("p (c t) -> p c t", c=2)), f"xpv{c}")
            for cb in range(2):
                for h in range(NH):
                    job = f"xo{2 * cb + h}"
                    await_fill(dve, job)
                    o = res[:, h, 512 * cb:512 * cb + 512]
                    release(V.tensor_tensor(o, pb(job), o, ALU.add), job)
            for c in range(4):
                await_read(dve, f"xo{c}")
            norm(4, res, xtok)
            evacuate_turned("Tf", xT, "norm_ffn")

            await_fill(dve, "route")
            lg = pb("route")[:, 0:128].rearrange("p (h e) -> p h e", h=NH)[:, :, 0:GROUPS + EXPERTS]
            release(V.tensor_copy(logit, lg), "route")
            await_read(dve, "route")

            def spread(ap, n):
                return ap.unsqueeze(2).to_broadcast([P, NH, n])

            def first_of_max(src, n, best, cand, index, pick):
                link(V.tensor_reduce(best, src, AX.X, ALU.max))
                link(V.tensor_tensor(cand, src, spread(best, n), ALU.is_equal))
                link(V.scalar_tensor_tensor(cand, cand, -64.0, iota[:, 0:n].unsqueeze(1).to_broadcast([P, NH, n]),
                                            ALU.mult, ALU.add))
                link(V.tensor_reduce(index, cand, AX.X, ALU.min))
                link(V.tensor_tensor(pick, cand, spread(index, n), ALU.is_equal))

            g_best, g_index, g_sum = soft[:, 48:50], soft[:, 50:52], soft[:, 52:54]
            g_pick, g_cand = rt(10, GROUPS), rt(11, GROUPS)
            first_of_max(logit[:, :, 0:GROUPS], GROUPS, g_best, g_cand, g_index, g_pick)
            V.tensor_tensor(rt(8, GROUPS), logit[:, :, 0:GROUPS], spread(g_best, GROUPS), ALU.subtract).then_inc(group_arg, 1)
            link(V.tensor_scalar(g_pick, g_pick, 1.0, BIG, ALU.subtract, ALU.mult))
            within = rt(0)
            link(V.tensor_tensor(within.rearrange("p h (g e) -> p h g e", g=GROUPS),
                                 logit[:, :, GROUPS:].rearrange("p h (g e) -> p h g e", g=GROUPS),
                                 g_pick.unsqueeze(3).to_broadcast([P, NH, GROUPS, PER_GROUP]), ALU.add))
            best1, best2, index = soft[:, 32:34], soft[:, 34:36], soft[:, 36:38]
            cand, pick1, pick2, picked, rest = rt(1), rt(2), rt(3), rt(4), rt(5)
            first_of_max(within, EXPERTS, best1, cand, index, pick1)
            link(V.scalar_tensor_tensor(rest, pick1, -3 * BIG, within, ALU.mult, ALU.add))
            first_of_max(rest, EXPERTS, best2, cand, index, pick2)
            link(V.tensor_tensor(soft[:, 54:56], best2, best1, ALU.subtract))
            V.tensor_tensor(picked, pick1, pick2, ALU.add).then_inc(chosen, 1)
            dve.wait_ge(chosen, 1)
            dve.wait_ge(group_exp, 1)
            link(V.tensor_reduce(g_sum, rt(9, GROUPS), AX.X, ALU.add))
            dve.wait_ge(expert_exp, 1)
            e21, gate1 = soft[:, 56:58], soft[:, 58:60]
            link(V.scalar_tensor_tensor(gate1, e21, 1.0, g_sum, ALU.add, ALU.mult))
            link(V.reciprocal(gate1, gate1))
            link(V.tensor_tensor(e21, e21, gate1, ALU.mult))
            link(V.tensor_tensor(pick1, pick1, spread(gate1, EXPERTS), ALU.mult))
            link(V.tensor_tensor(pick2, pick2, spread(e21, EXPERTS), ALU.mult))
            link(V.tensor_tensor(gates, pick1, pick2, ALU.add))
            await_fill(dve, "rank")
            release(V.scalar_tensor_tensor(rankm, pb("rank")[:, 0:2 * EXPERTS].rearrange("p (h e) -> p h e", h=NH), 1.0,
                                           picked, ALU.add, ALU.mult), "rank")
            await_read(dve, "rank")
            link(V.tensor_scalar(rankm, rankm, -1.0, None, ALU.add))
            over = rt(6)
            link(V.tensor_scalar(over, rankm, float(SLOTS), None, ALU.is_ge))
            V.tensor_reduce(soft[:, 0:1], over, AX.XY, ALU.add).then_inc(rank_ready, 1)
            await_fill(dve, "over")
            release(V.tensor_copy(flag, pb("over")[:, 0:1]), "over")
            await_read(dve, "over")

            with dve.Fori(0, BATCHES) as g:
                shape = [P, BATCH, SLOTS]
                for h in range(NH):
                    i = V.tensor_tensor(take[:, h], rankm[:, h, bass.ds(BATCH * g, BATCH)].unsqueeze(2).to_broadcast(shape),
                                        iota[:, 0:SLOTS].unsqueeze(1).to_broadcast(shape), ALU.is_equal)
                i.then_inc(taken, 1)
                dve.wait_ge(taken, g + 1)
                for h in range(NH):
                    i = V.tensor_tensor(gtake[:, h], take[:, h],
                                        gates[:, h, bass.ds(BATCH * g, BATCH)].unsqueeze(2).to_broadcast(shape), ALU.mult)
                i.then_inc(gtaken, 1)
                dve.wait_ge(gathered, g + 1)
                for half in range(2):
                    i = V.tensor_tensor(xg[:, 0, 4 * half:4 * half + 4], bank(4 + half).rearrange("p (c n) -> p c n", c=4),
                                        param("norm_ffn")[:, 4 * half:4 * half + 4].unsqueeze(2).to_broadcast([P, 4, P]),
                                        ALU.mult)
                i.then_inc(xg_ready, 1)
                for j in range(BATCH):
                    n = BATCH * g + (j + 1)
                    half = bank(7)[:, 256 * (j % 2):256 * (j % 2) + 256]
                    dve.wait_ge(gu_tanh, n)
                    V.scalar_tensor_tensor(th, th, 1.0, half[:, 0:P], ALU.add, ALU.mult).then_inc(gu_half, 1)
                    dve.wait_ge(gu_half, n)
                    V.scalar_tensor_tensor(hid, th, 0.5, half[:, P:2 * P], ALU.mult, ALU.mult).then_inc(hid_ready, 1)
                    dve.wait_ge(y_done, n)
                    for strip in range(2, 4):
                        r = slice(SLOTS * strip, SLOTS * strip + SLOTS)
                        i = V.tensor_copy(ybuf[SLOTS * j:SLOTS * j + SLOTS, 256 * strip:256 * strip + 256], bank(6)[r, 0:256])
                    i.then_inc(y_dve, 1)

            many = dve.value_load(flag[0:1, 0:1])
            with dve.If(many > 0):
                dve.wait_ge(scattered, BATCHES)
                V.tensor_scalar(ov_gates, rankm, float(SLOTS), None, ALU.is_ge).then_inc(ov_gate, 1)
                dve.wait_ge(ov_gate, 1)
                V.tensor_tensor(ov_gates, ov_gates, gates, ALU.mult).then_inc(ov_gate, 1)
                dve.wait_ge(ov_gate, 2)
                dve.wait_ge(ov_turned, 1)
                for k in range(KC):
                    i = V.tensor_scalar(ov_x[:, k], bank(4 + k // 2)[:, 256 * (k % 2):256 * (k % 2) + 256],
                                        param("norm_ffn", k), None, ALU.mult)
                i.then_inc(ov_xT, 1)
                with dve.Fori(0, EXPERTS) as e:
                    for h in range(NH):
                        n = NH * e + (h + 1)
                        dve.wait_ge(ov_tanh, n)
                        V.scalar_tensor_tensor(ov_th, ov_th, 1.0, bank(4), ALU.add, ALU.mult).then_inc(ov_half, 1)
                        dve.wait_ge(ov_half, n)
                        V.scalar_tensor_tensor(ov_h, ov_th, 0.5, bank(5), ALU.mult, ALU.mult).then_inc(ov_hid, 1)
                        V.tensor_copy(ov_g, ov_gates[:, h, bass.ds(e, 1)]).then_inc(ov_gate, 1)
                        dve.wait_ge(ov_gate, n + 2)
                        dve.wait_ge(ov_y, n)
                        V.tensor_scalar(ov_ysc.rearrange("p (c n) -> p c n", c=2), psum[:, 4:6, :], ov_g, None,
                                        ALU.mult).then_inc(ov_scaled, 1)
                dve.wait_ge(ov_added, NH * EXPERTS + 1)

            dve.wait_ge(final_sq, NH)
            mean(FINAL, 2, D).then_inc(final_ms, 1)
            dve.wait_ge(final_rstd, 1)
            dve.wait_ge(gain_loaded, 16)
            for h in range(NH):
                V.scalar_tensor_tensor(fin[:, h].rearrange("p (c n) -> p c n", c=2), psum[:, 2 * h:2 * h + 2, :],
                                       stat[:, RS + FINAL + h:RS + FINAL + h + 1],
                                       gain_final.rearrange("p (c n) -> p c n", c=2), ALU.mult, ALU.mult
                                       ).then_inc(final_out, 1)


_INS = ["x", "mem", "norm_mix", "w_in", "conv_w", "conv_b", "w_rg", "b_rg", "w_ig", "b_ig", "lru_lambda",
        "norm_lru_out", "norm_attn_out", "w_out", "norm_cross", "norm_mem", "w_xq", "w_xkv", "w_xo",
        "norm_ffn", "w_router_group", "b_router_group", "w_router_expert", "b_router_expert",
        "w_gate_up", "w_down", "norm_final"]


def kernel(**inputs):
    import concourse.bacc as bacc
    from concourse.bass_utils import run_bass_kernel_spmd

    nc = bacc.Bacc("TRN2", target_bir_lowering=False, num_devices=1, dynamic_dma_scratch_size=1024)
    arrays = {f"in_{name}": np.ascontiguousarray(inputs[name]) for name in _INS}
    arrays["in_consts"] = constants()
    args = [nc.dram_tensor(name, a.shape, F32, kind="ExternalInput").ap() for name, a in arrays.items()]
    args.append(nc.dram_tensor("out_0", (1, S, D), F32, kind="ExternalOutput").ap())
    block_kernel(nc, *args)
    r = run_bass_kernel_spmd(nc, [arrays], core_ids=[0])
    return r.results[0]["out_0"]
```

```python
from contextlib import ExitStack

import concourse.bass as bass
import numpy as np
from concourse import mybir

F32 = mybir.dt.float32
F32R = mybir.dt.float32r
I32 = mybir.dt.int32
ALU = mybir.AluOpType
ACT = mybir.ActivationFunctionType
AX = mybir.AxisListType

P = 128
D = 1024
S = 256
NH = S // P
KC = D // P
DL = 512
CT = DL // P
CONV = 4
HEADS = 8
HD = 64
HALF_ROT = 8
XH = 4
XHD = 256
GROUPS = 4
EXPERTS = 32
PER_GROUP = EXPERTS // GROUPS
FF = 512
EPS = 1e-6
UNIT = 4096
UNITS = 12
SLOTS = 32
BATCH = P // SLOTS
BATCHES = EXPERTS // BATCH
BIG = 1e30
GELU_IN = 0.7978845608028654
GELU_CUBE = 0.044715

EXPERT_UNITS = [(7, 8, 6), (9, 10, 11), (1, 2, 0), (3, 4, 5)]

STREAM = ["x_lru", "q", "k", "v", "g_lru", "xk0", "xk1", "out0", "out1", "xv0",
          "xq0", "xq1", "xv1", "xo0", "xo1"]
BY_COLUMNS = {"x_lru", "g_lru", "xk0", "xk1", "xq0", "xq1"}
HALVES = 2 * len(STREAM)
HALF = UNIT // 2
RAW = 4
MIXER_DONE_AT = 24
SLOTS_W = 3
LAST_JOB = ["xl0", "xl1", None, "q1", None, "k1", None, "v1", "gl0", "gl1", "xk0", "xk1", "xk2", "xk3",
            "out1", "out3", "out5", "out7", None, "xv1", "xq0", "xq1", "xq2", "xq3", None, "xv3",
            None, "xo1", None, "xo3"]
POOL_LO = (6, 8, 10, 12)

PARAMS = {}
for _name, _cols in (("norm_mix", KC), ("norm_mem", KC), ("norm_cross", KC), ("norm_ffn", KC),
                     ("norm_lru_out", CT), ("norm_attn_out", CT), ("conv_b", CT), ("b_rg", CT),
                     ("b_ig", CT), ("lru_lambda", CT), ("conv_w", CONV * CT)):
    PARAMS[_name] = (sum(n for _, n in PARAMS.values()), _cols)
N_PARAMS = sum(n for _, n in PARAMS.values())
N_ROUTES = GROUPS + EXPERTS

CONSTS = {}
for _name, _cols in (("ident", P), ("before", P), ("causal", S), ("ones", P), ("iota", EXPERTS),
                     ("cos", NH * HALF_ROT), ("sin", NH * HALF_ROT), ("power", 4)):
    CONSTS[_name] = (sum(n for _, n in CONSTS.values()), _cols)
N_CONSTS = sum(n for _, n in CONSTS.values())


def constants():
    t = np.zeros((P, N_CONSTS), np.float32)

    def put(name, value):
        a, n = CONSTS[name]
        t[:, a:a + n] = value

    i = np.arange(P)
    put("ident", np.eye(P))
    put("before", i[:, None] < i[None, :])
    put("causal", np.where(np.arange(S)[None, :] - P <= i[:, None], 0.0, -BIG))
    put("ones", 1.0)
    put("iota", np.arange(EXPERTS)[None, :])
    rot = 2 * HALF_ROT
    inv_freq = np.float32(500000.0) ** (-np.arange(0, rot, 2, dtype=np.float32) / np.float32(rot))
    angle = np.arange(S, dtype=np.float32)[:, None] * inv_freq[None, :].astype(np.float32)
    for name, f in (("cos", np.cos), ("sin", np.sin)):
        put(name, f(angle).astype(np.float32).reshape(NH, P, HALF_ROT).transpose(1, 0, 2).reshape(P, -1))
    put("power", -0.5)
    return t


def lay_out_params(inputs):
    return np.concatenate([np.asarray(inputs[name]).reshape(n, P) for name, (_, n) in PARAMS.items()]).T


def lay_out_late(inputs):
    router = np.concatenate([np.asarray(inputs["w_router_group"])[0], np.asarray(inputs["w_router_expert"])[0]], axis=1)
    bias = np.concatenate([np.asarray(inputs["b_router_group"]), np.asarray(inputs["b_router_expert"])], axis=1)
    blocks = np.zeros((P, 2, CT, P), np.float32)
    for n, name in enumerate(("w_rg", "w_ig")):
        w = np.asarray(inputs[name])[0]
        for b in range(w.shape[0]):
            r = HD * (b % 2)
            blocks[r:r + HD, n, b // 2, r:r + HD] = w[b]
    return np.concatenate([router.reshape(KC, P, N_ROUTES).transpose(1, 0, 2).reshape(P, -1),
                           np.broadcast_to(bias, (P, N_ROUTES)), blocks.reshape(P, -1)], axis=1)


JOBS = []
JOBS += [(f"Tx{c}", 2) for c in range(4)]
JOBS += [(f"xl{c}", 1) for c in range(2)]
JOBS += [(f"Tm{c}", 2) for c in range(4)]
JOBS += [(f"q{h}", 1) for h in range(2)] + [(f"k{h}", 1) for h in range(2)]
JOBS += [(f"rg{c}", 2) for c in range(2)] + [(f"ig{c}", 2) for c in range(2)]
JOBS += [(f"v{h}", 1) for h in range(2)]
JOBS += [(f"Tqk{c}", 1) for c in range(4)]
JOBS += [(f"gl{c}", 1) for c in range(2)]
JOBS += [("s0e", 1), ("s0o", 1)] + [(f"s1{c}", 1) for c in range(4)]
JOBS += [(f"xk{c}", 1) for c in range(4)]
JOBS += [(f"Tp{c}", 1) for c in range(6)]
JOBS += [(f"pv{c}", 2) for c in range(2)]
JOBS += [(f"out{c}", 1) for c in range(4)] + [("ss", 1)]
JOBS += [(f"out{c}", 1) for c in (4, 5)] + [(f"Th{c}", 2) for c in range(2)]
JOBS += [(f"out{c}", 1) for c in (6, 7)] + [(f"xv{c}", 1) for c in (0, 1)] + [(f"Th{c}", 2) for c in (2, 3)]
JOBS += [(f"xq{c}", 1) for c in range(4)] + [(f"xv{c}", 1) for c in (2, 3)]
JOBS += [(f"xs{c}", 2) for c in range(4)]
JOBS += [(f"Txp{c}", 1) for c in range(4)]
JOBS += [(f"xpv{c}", 2) for c in range(4)]
JOBS += [(f"xo{c}", 1) for c in range(4)]
JOBS += [(f"Tf{c}", 1) for c in range(4)]
JOBS += [("route0", 1), ("route1", 1), ("rank", 1), ("over", 1)]
BANKS = 8
ACC_BANKS = (0, 1, 2, 3)
LATE = {"xo0": 4, "xo1": 5, "xo2": 6, "xo3": 7, "Tf0": 4, "Tf1": 5, "Tf2": 6, "Tf3": 7,
        "route0": 4, "route1": 7, "rank": 5, "over": 6}
BANK_OF, FILLS, FREED_BEFORE, FREED_AFTER = {}, {}, {}, {}
_fills, _reads = [0] * BANKS, [0] * BANKS
for _n, (_name, _parts) in enumerate(JOBS):
    _b = LATE.get(_name, _n % BANKS)
    BANK_OF[_name], FREED_BEFORE[_name] = _b, _reads[_b]
    _fills[_b] += 1
    _reads[_b] += _parts
    FILLS[_name], FREED_AFTER[_name] = _fills[_b], _reads[_b]
READS_IN_A = list(_reads)

def block_kernel(nc, x, mem, w_in, w_out, w_xq, w_xkv, w_xo, w_gate_up, w_down, norm_final, early, late, out):
    with ExitStack() as ctx:
        def sb(name, shape, dt=F32):
            return ctx.enter_context(nc.sbuf_tensor(name, shape, dt))[:]

        def sem(name):
            return ctx.enter_context(nc.semaphore(name))

        with (nc.sbuf_tensor("landing", [P, 2 * UNIT], F32) as landing,
              nc.sbuf_tensor("split_w", [P, 3 * UNIT], F32R) as split_w,
              nc.sbuf_tensor("split_act", [P, 2 * UNIT], F32R) as split_act,
              nc.sbuf_tensor("work", [P, 5 * UNIT], F32) as work):
            landing, split_w, split_act, work = landing[:], split_w[:], split_act[:], work[:]
        ring = sb("ring", [P, UNITS * UNIT])
        ctab = sb("ctab", [P, N_CONSTS + N_PARAMS])
        latetab = sb("latetab", [P, (KC + 1) * N_ROUTES])
        res = sb("res", [P, NH, D])
        xg = sb("xg", [P, KC, P])
        ybuf = sb("ybuf", [P, D])
        small = sb("small", [P, 9 * P])
        take, gtake = (small[:, a:a + NH * P].rearrange("p (h e s) -> p h e s", h=NH, e=BATCH) for a in (0, 2 * P))
        give = small[:, 4 * P:6 * P]
        th, hid, hidT = (small[:, a:a + P] for a in (6 * P, 7 * P, 8 * P))
        rankm = sb("rankm", [P, NH, EXPERTS])
        gates = sb("gates", [P, NH, EXPERTS])
        stat = sb("stat", [P, 64])
        soft = sb("soft", [P, 64])
        lru = sb("lru", [P, 32])
        flag = sb("flag", [P, 1], I32)
        psum = ctx.enter_context(nc.psum_tensor("psum", [P, BANKS, 512], F32))[:]

        def unit(u):
            return ring[:, u * UNIT:(u + 1) * UNIT]

        def scratch(u, off, n):
            return work[:, (u - 7) * UNIT + off:(u - 7) * UNIT + off + n]

        def spare(u, off, n):
            return ring[:, u * UNIT + off:u * UNIT + off + n]

        def const(name):
            a, n = CONSTS[name]
            return ctab[:, a:a + n]

        def param(name, c=None):
            a, n = PARAMS[name][0] + N_CONSTS, PARAMS[name][1]
            return ctab[:, a:a + n] if c is None else ctab[:, a + c:a + c + 1]

        def bank(b):
            return psum[:, b, :]

        def pb(job):
            return bank(BANK_OF[job])

        ident, ones, iota = const("ident"), const("ones"), const("iota")
        cos = const("cos").rearrange("p (h r) -> p h r", h=NH)
        sin = const("sin").rearrange("p (h r) -> p h r", h=NH)

        def tiles(ap, c=CT):
            return ap.rearrange("p (c t) -> p c t", c=c)

        xc = tiles(scratch(7, 0, 1024))
        gate_r = tiles(scratch(7, 1024, 1024))
        gate_i = tiles(scratch(7, 2048, 1024))
        gx = tiles(scratch(7, 3072, 1024))
        xtok = tiles(scratch(7, 0, 2048), NH)
        sqT = tiles(scratch(7, 1024, 2048), KC)
        PAD = S + CONV - 1
        xlp = tiles(scratch(8, 0, CT * PAD))
        root = tiles(scratch(8, 1040, 1024))
        ylru = root
        decay = tiles(scratch(8, 2064, 1024))
        qk = tiles(scratch(9, 0, 2048), NH)
        xkT = tiles(scratch(9, 0, 2048), KC)
        qkT = tiles(scratch(9, 2048, 2048), 2 * CT)
        memraw = tiles(scratch(10, 0, 2048), NH)
        v = tiles(scratch(10, 0, 1024), NH)
        p0 = tiles(scratch(10, 1024, 1024), HEADS)
        xv = tiles(scratch(10, 0, 2048), NH)
        p1 = tiles(scratch(10, 2048, 2048), HEADS)
        xqT = tiles(scratch(10, 2048, 2048), KC)
        pTa = tiles(scratch(11, 0, 2048), HEADS)
        pTb = tiles(scratch(11, 2048, 1024), HEADS)
        rope = scratch(11, 3072, 1024).rearrange("p (k n) -> p k n", k=4)
        xp = scratch(11, 0, 2048).rearrange("p (h n k) -> p h n k", h=NH, n=XH)
        xpT = scratch(11, 2048, 2048).rearrange("p (m n q) -> p m n q", m=NH, n=XH)
        sq = small[:, 0:D]
        xT = [tiles(t) for t in (xg.rearrange("p c t -> p (c t)"), ybuf)]
        bd = tiles(ybuf, 2 * CT)
        router = latetab[:, 0:KC * N_ROUTES].rearrange("p (c n) -> p c n", c=KC)
        route_bias = latetab[:, KC * N_ROUTES:]

        def pair(src, off, c):
            return tuple(src[:, off + HALF * part:off + HALF * part + HALF].rearrange("p (c t) -> p c t", c=c)
                         for part in range(2))

        def slot(m, c):
            return pair(split_w, UNIT * (m % SLOTS_W), c)

        xs_ = pair(split_act, 0, KC)
        ys_ = xs_
        hs_ = xs_
        ms_ = pair(split_act, UNIT, KC)

        def raw(m, c):
            return landing[:, HALF * (m % RAW):HALF * (m % RAW) + HALF].rearrange("p (c t) -> p c t", c=c)

        def chunks_of(m):
            return KC if STREAM[m // 2] in BY_COLUMNS else CT

        def rt(n, m=EXPERTS):
            return ybuf[:, 80 + 64 * n:80 + 64 * n + NH * m].rearrange("p (h e) -> p h e", h=NH)

        logit = ybuf[:, 0:72].rearrange("p (h e) -> p h e", h=NH)

        x_in = x[0].rearrange("(h p) d -> p h d", p=P)
        mem_in = mem[0].rearrange("(h p) d -> p h d", p=P)
        out_d = out[0].rearrange("(h p) d -> p h d", p=P)

        def columns(w, a):
            return w[0].rearrange("(c p) n -> p c n", p=P)[:, :, a:a + 512]

        def half_source(m):
            name, part = STREAM[m // 2], m % 2
            if name in BY_COLUMNS:
                return SOURCE[name][:, :, 256 * part:256 * part + 256]
            return SOURCE[name][:, CT * part:CT * part + CT, :]

        SOURCE = {
            "x_lru": columns(w_in, 0), "g_lru": columns(w_in, 512), "q": columns(w_in, 1024),
            "k": columns(w_in, 1536), "v": columns(w_in, 2048),
            "xk0": columns(w_xkv, 0), "xk1": columns(w_xkv, 512),
            "xv0": columns(w_xkv, 1024), "xv1": columns(w_xkv, 1536),
            "out0": columns(w_out, 0), "out1": columns(w_out, 512),
            "xq0": columns(w_xq, 0), "xq1": columns(w_xq, 512),
            "xo0": columns(w_xo, 0), "xo1": columns(w_xo, 512),
        }

        loaded = [sem(f"loaded{u}") for u in range(UNITS)]
        filled = [sem(f"filled{b}") for b in range(BANKS)]
        freed = [sem(f"freed{b}") for b in range(BANKS)]
        raw_loaded = [sem(f"raw_loaded{r}") for r in range(RAW)]
        w_hi, w_lo, w_lo_pool = sem("w_hi"), sem("w_lo"), sem("w_lo_pool")
        half_used = sem("half_used")
        x_loaded = [sem(f"x_loaded{h}") for h in range(NH)]
        mem_loaded, early_loaded = sem("mem_loaded"), sem("early_loaded")
        router_loaded, bd_loaded = sem("router_loaded"), sem("bd_loaded")
        zeroed = sem("zeroed")
        dve_step, act_step, pool_step = sem("dve_step"), sem("act_step"), sem("pool_step")
        sumsq, meansq, rstd = sem("sumsq"), sem("meansq"), sem("rstd")
        sub_rstd = sem("sub_rstd")
        normed_act, normed_dve = sem("normed_act"), sem("normed_dve")
        conv_done = sem("conv_done")
        lambda_abs, lambda_exp, lru_params = sem("lambda_abs"), sem("lambda_exp"), sem("lru_params")
        decay_ready, t2_ready, root_ready = sem("decay_ready"), sem("t2_ready"), sem("root_ready")
        scanned = sem("scanned")
        gelu_arg, gelu_tanh = sem("gelu_arg"), sem("gelu_tanh")
        ylru_ready, ylru_squared, ylru_hi, ylru_lo = sem("ylru_ready"), sem("ylru_squared"), sem("ylru_hi"), sem("ylru_lo")
        squares_added = sem("squares_added")
        rope_done = sem("rope_done")
        smax, sexp, snorm = sem("smax"), sem("sexp"), sem("snorm")
        xmax, xexp, xnorm = sem("xmax"), sem("xexp"), sem("xnorm")
        xscale = sem("xscale")
        acc_set = sem("acc_set")
        group_arg, group_exp, expert_exp = sem("group_arg"), sem("group_exp"), sem("expert_exp")
        chosen, rank_ready = sem("chosen"), sem("rank_ready")
        taken, gtaken = sem("taken"), sem("gtaken")
        gathered, xg_ready = sem("gathered"), sem("xg_ready")
        turned, give_ready = sem("turned"), sem("give_ready")
        gu_done, gu_tanh, gu_half, hid_ready = sem("gu_done"), sem("gu_tanh"), sem("gu_half"), sem("hid_ready")
        hid_turned, hidT_ready = sem("hid_turned"), sem("hidT_ready")
        y_done, y_act, y_dve = sem("y_done"), sem("y_act"), sem("y_dve")
        scattered = sem("scattered")
        ov_turned, ov_xT = sem("ov_turned"), sem("ov_xT")
        ov_loaded, ov_gu, ov_tanh, ov_half, ov_hid = (
            sem("ov_loaded"), sem("ov_gu"), sem("ov_tanh"), sem("ov_half"), sem("ov_hid"))
        ov_hidT_done, ov_hidT, ov_y, ov_gate, ov_scaled, ov_added = (
            sem("ov_hidT_done"), sem("ov_hidT"), sem("ov_y"), sem("ov_gate"), sem("ov_scaled"), sem("ov_added"))
        gain_loaded, final_sq, final_ms, final_rstd, final_out, stored = (
            sem("gain_loaded"), sem("final_sq"), sem("final_ms"), sem("final_rstd"), sem("final_out"), sem("stored"))

        gain_final = unit(EXPERT_UNITS[0][0])[:, 0:D]
        fin = unit(EXPERT_UNITS[0][1])[:, 0:2048].rearrange("p (h n) -> p h n", h=NH)

        ov_gu_w = [unit(u).rearrange("p (c n) -> p c n", c=CT) for u in (0, 1)]
        ov_down_w = unit(2).rearrange("p (c n) -> p c n", c=CT)
        ov_x = tiles(spare(9, 0, 2048), KC)
        ov_th, ov_h, ov_ht = spare(9, 2048, 512), spare(9, 2560, 512), spare(9, 3072, 512)
        ov_ysc = spare(10, 0, 1024)
        ov_g = spare(10, 1024, 1)
        ov_gates = spare(10, 1088, NH * EXPERTS).rearrange("p (h e) -> p h e", h=NH)

        SS, MS, RS = 0, 16, 32
        SUB, FINAL = 8, 12

        def expert_gu(j, part):
            return unit(EXPERT_UNITS[j][part]).rearrange("p (c n) -> p c n", c=CT)

        def expert_down(j):
            return unit(EXPERT_UNITS[j][2]).rearrange("p (c n) -> p c n", c=CT)

        def await_fill(eng, job):
            eng.wait_ge(filled[BANK_OF[job]], FILLS[job])

        def await_read(eng, job):
            eng.wait_ge(freed[BANK_OF[job]], FREED_AFTER[job])

        def await_first_read(eng, job):
            eng.wait_ge(freed[BANK_OF[job]], FREED_BEFORE[job] + 1)

        def await_split(eng, m):
            by_pool = sum(n in POOL_LO for n in range(m + 1))
            eng.wait_ge(w_lo, m + 1 - by_pool)
            if by_pool:
                eng.wait_ge(w_lo_pool, by_pool)

        def await_half_used(eng, m):
            if LAST_JOB[m]:
                await_fill(eng, LAST_JOB[m])
            else:
                eng.wait_ge(half_used, sum(j is None for j in LAST_JOB[:m + 1]))

        block = ctx.enter_context(nc.Block())

        @block.sync
        def _(sp):
            def load_expert(e, j, part):
                u = EXPERT_UNITS[j][part]
                if part < 2:
                    src = w_gate_up[0, e].rearrange("(two c p) n -> two p c n", p=P, two=2)[part]
                else:
                    src = w_down[0, e].rearrange("(c p) n -> p c n", p=P)
                sp.dma_start(unit(u).rearrange("p (c n) -> p c n", c=CT), src).then_inc(loaded[u], 16)

            def load_half(m):
                if m >= RAW:
                    await_split(sp, m - RAW)
                sp.dma_start(raw(m, chunks_of(m)), half_source(m)).then_inc(raw_loaded[m % RAW], 16)

            for h in range(NH):
                sp.dma_start(res[:, h], x_in[:, h]).then_inc(x_loaded[h], 16)
            sp.dma_start(ctab, early).then_inc(early_loaded, 16)
            load_half(0)
            load_half(1)
            sp.dma_start(memraw, mem_in).then_inc(mem_loaded, 16)
            load_half(2)
            sp.dma_start(bd.rearrange("p c n -> p (c n)"), late[:, (KC + 1) * N_ROUTES:]).then_inc(bd_loaded, 16)
            load_half(3)
            sp.dma_start(latetab, late[:, 0:(KC + 1) * N_ROUTES]).then_inc(router_loaded, 16)
            for m in range(4, HALVES):
                if m == MIXER_DONE_AT:
                    await_fill(sp, "out7")
                    load_expert(0, 0, 0)
                    load_expert(0, 0, 1)
                load_half(m)

            await_fill(sp, "xs3")
            load_expert(1, 1, 0)
            await_fill(sp, "xv3")
            load_expert(0, 0, 2)
            await_fill(sp, "xpv3")
            load_expert(1, 1, 1)
            load_expert(1, 1, 2)
            await_split(sp, HALVES - 3)
            load_expert(2, 2, 0)
            await_half_used(sp, HALVES - 3)
            load_expert(2, 2, 1)
            await_split(sp, HALVES - 1)
            load_expert(2, 2, 2)
            await_half_used(sp, HALVES - 2)
            load_expert(3, 3, 0)
            await_half_used(sp, HALVES - 1)
            load_expert(3, 3, 1)
            load_expert(3, 3, 2)
            with sp.Fori(1, BATCHES) as g:
                for j in range(BATCH):
                    sp.wait_ge(gu_done, BATCH * g + (j + 1 - BATCH))
                    load_expert(BATCH * g + j, j, 0)
                    load_expert(BATCH * g + j, j, 1)
                    sp.wait_ge(y_done, BATCH * g + (j + 1 - BATCH))
                    load_expert(BATCH * g + j, j, 2)
            sp.wait_ge(gu_done, EXPERTS - BATCH + 1)
            sp.dma_start(gain_final, norm_final.partition_broadcast(P)).then_inc(gain_loaded, 16)
            await_read(sp, "over")
            over = sp.value_load(flag[0:1, 0:1])
            with sp.If(over > 0):
                sp.wait_ge(scattered, BATCHES)
                with sp.Fori(0, EXPERTS) as e:
                    sp.wait_ge(ov_added, NH * e + 1)
                    for part in range(2):
                        sp.dma_start(ov_gu_w[part], w_gate_up[0, e].rearrange("(two c p) n -> two p c n", p=P, two=2)[part]
                                     ).then_inc(ov_loaded, 16)
                    sp.dma_start(ov_down_w, w_down[0, e].rearrange("(c p) n -> p c n", p=P)).then_inc(ov_loaded, 16)
            for h in range(NH):
                sp.wait_ge(final_out, h + 1)
                sp.dma_start(out_d[:, h], fin[:, h]).then_inc(stored, 16)
            sp.wait_ge(stored, 16 * NH)

        @block.tensor
        def _(pe):
            mm, tr = nc.tensor.matmul, nc.tensor.transpose

            def begin(job):
                if FREED_BEFORE[job]:
                    pe.wait_ge(freed[BANK_OF[job]], FREED_BEFORE[job])
                return pb(job)

            def end(ins, job):
                ins.then_inc(filled[BANK_OF[job]], 1)

            def turn(prefix, src, cs=range(4)):
                for c in cs:
                    b = begin(f"{prefix}{c}")
                    for k in range(2):
                        for h in range(NH):
                            i = tr(b[:, 256 * k + P * h:256 * k + P * h + P],
                                   src[:, h, (2 * c + k) * P:(2 * c + k + 1) * P], ident)
                    end(i, f"{prefix}{c}")

            def channels(m, job, src):
                await_split(pe, m)
                w = slot(m, KC)
                b = begin(job)
                for c in range(2):
                    for k in range(KC):
                        for n, (a, t) in enumerate(((1, 0), (0, 1), (0, 0))):
                            i = mm(b[:, 256 * c:256 * c + 256], w[a][:, k, P * c:P * c + P], src[t][:, k, :],
                                   start=k == 0 and n == 0, stop=k == KC - 1 and n == 2)
                end(i, job)

            def tokens(m, jobs, src, k0, first=True, last=True):
                await_split(pe, m)
                w = slot(m, CT)
                for h in range(NH):
                    b = begin(jobs[h]) if first else pb(jobs[h])
                    for k in range(CT):
                        for n, (t, a) in enumerate(((1, 0), (0, 1), (0, 0))):
                            i = mm(b, src[t][:, k0 + k, P * h:P * h + P], w[a][:, k, :],
                                   start=first and k == 0 and n == 0, stop=last and k == CT - 1 and n == 2)
                    if last:
                        end(i, jobs[h])
                if not last:
                    i.then_inc(half_used, 1)

            def tokens_whole(m, jobs, src):
                tokens(m, jobs, src, 0, last=False)
                tokens(m + 1, jobs, src, CT, first=False)

            pe.wait_ge(early_loaded, 16)
            pe.wait_ge(normed_act, 1)
            pe.wait_ge(normed_dve, 1)
            turn("Tx", xtok)
            for c in range(4):
                await_read(pe, f"Tx{c}")
            channels(0, "xl0", xs_)
            channels(1, "xl1", xs_)
            pe.wait_ge(normed_act, 2)
            pe.wait_ge(normed_dve, 2)
            turn("Tm", memraw)
            tokens_whole(2, ["q0", "q1"], xs_)
            tokens_whole(4, ["k0", "k1"], xs_)
            pe.wait_ge(bd_loaded, 16)
            pe.wait_ge(conv_done, 1)
            for n, gate in enumerate(("rg", "ig")):
                for c in range(2):
                    b = begin(f"{gate}{c}")
                    for k in range(2):
                        i = mm(b[:, 256 * k:256 * k + 256], bd[:, CT * n + 2 * c + k, :], xc[:, 2 * c + k, :],
                               start=True, stop=True)
                    end(i, f"{gate}{c}")
            tokens_whole(6, ["v0", "v1"], xs_)
            pe.wait_ge(rope_done, 1)
            turn("Tqk", qk)
            channels(8, "gl0", xs_)
            channels(9, "gl1", xs_)
            for c in range(4):
                await_read(pe, f"Tqk{c}")

            def score(n, tok, keys, out_ap):
                r = slice(HD * (n % 2), HD * (n % 2) + HD)
                return mm(out_ap, qkT[r, n // 2, tok], qkT[r, CT + n // 2, keys], start=True, stop=True)

            for job in ("s0e", "s0o"):
                begin(job)
            for n in range(HEADS):
                job = ("s0e", "s0o")[n % 2]
                i = score(n, slice(0, P), slice(0, P), pb(job)[:, P * (n // 2):P * (n // 2) + P])
                if n >= HEADS - 2:
                    end(i, job)
            for c in range(4):
                begin(f"s1{c}")
            for n in range(HEADS):
                job, k = f"s1{2 * (n // 4) + n % 2}", n // 2 % 2
                i = score(n, slice(P, S), slice(0, S), pb(job)[:, 256 * k:256 * k + 256])
                if k:
                    end(i, job)
            for c in range(4):
                await_read(pe, f"Tm{c}")
            for n in range(4):
                channels(10 + n, f"xk{n}", ms_)
            pe.wait_ge(snorm, 2)
            for c in range(4):
                b = begin(f"Tp{c}")
                for k in range(2):
                    n = 2 * c + k
                    tr(b[:, 256 * k:256 * k + P], p0[:, n, :], ident)
                    i = tr(b[:, 256 * k + P:256 * k + 256], p1[:, n, 0:P], ident)
                end(i, f"Tp{c}")
            for c in range(2):
                b = begin(f"Tp{4 + c}")
                for k in range(4):
                    i = tr(b[:, P * k:P * k + P], p1[:, 4 * c + k, P:S], ident)
                end(i, f"Tp{4 + c}")
            for c in range(6):
                await_read(pe, f"Tp{c}")
            for h in range(NH):
                await_read(pe, f"v{h}")
            for c in range(2):
                b = begin(f"pv{c}")
                for n in range(4 * c, 4 * c + 4):
                    r = slice(HD * (n % 2), HD * (n % 2) + HD)
                    k = n // 2 % 2
                    mm(b[r, 256 * k:256 * k + 256], v[:, 0, HD * n:HD * n + HD], pTa[:, n, :],
                       start=True, stop=False, skip_group_check=True)
                    i = mm(b[r, 256 * k + P:256 * k + 256], v[:, 1, HD * n:HD * n + HD], pTb[:, n, :],
                           start=False, stop=True, skip_group_check=True)
                end(i, f"pv{c}")
            pe.wait_ge(ylru_lo, 1)
            tokens(14, ["out0", "out1"], ys_, 0)
            for c in range(2):
                await_read(pe, f"pv{c}")
            tokens(15, ["out2", "out3"], ys_, CT)
            pe.wait_ge(squares_added, 2)
            b = begin("ss")
            for part in range(2):
                for h in range(NH):
                    i = mm(b[:, 2 * part + h:2 * part + h + 1], sqT[:, CT * part, P * h:P * h + P], ones[:, 0:1],
                           start=True, stop=True)
            end(i, "ss")
            tokens(16, ["out4", "out5"], ys_, 0)
            for c in range(4):
                await_read(pe, f"out{c}")
            turn("Th", res, (0, 1))
            tokens(17, ["out6", "out7"], ys_, CT)
            tokens(18, ["xv0", "xv1"], ms_, 0, last=False)
            for c in range(4, 8):
                await_read(pe, f"out{c}")
            turn("Th", res, (2, 3))
            tokens(19, ["xv0", "xv1"], ms_, CT, first=False)
            for c in range(4):
                await_read(pe, f"Th{c}")
            for n in range(4):
                channels(20 + n, f"xq{n}", hs_)
            tokens(24, ["xv2", "xv3"], ms_, 0, last=False)
            for c in range(4):
                await_read(pe, f"xk{c}")
                await_read(pe, f"xq{c}")
            for h in range(NH):
                for c in range(2):
                    b = begin(f"xs{2 * h + c}")
                    for k in range(2):
                        n = 2 * c + k
                        for m in range(2):
                            i = mm(b[:, 256 * k:256 * k + 256], xqT[:, 2 * n + m, P * h:P * h + P],
                                   xkT[:, 2 * n + m, :], start=m == 0, stop=m == 1)
                    end(i, f"xs{2 * h + c}")
            tokens(25, ["xv2", "xv3"], ms_, CT, first=False)
            pe.wait_ge(xnorm, 2)
            for m in range(2):
                for c in range(2):
                    b = begin(f"Txp{2 * m + c}")
                    for k in range(2):
                        for h in range(NH):
                            i = tr(b[:, 256 * k + P * h:256 * k + P * h + P],
                                   xp[:, h, 2 * c + k, P * m:P * m + P], ident)
                    end(i, f"Txp{2 * m + c}")
            for c in range(4):
                await_read(pe, f"Txp{c}")
                await_read(pe, f"xv{c}")
            for n in range(XH):
                b = begin(f"xpv{n}")
                for k in range(2):
                    for m in range(2):
                        i = mm(b[:, 256 * k:256 * k + 256], xv[:, m, XHD * n + P * k:XHD * n + P * k + P],
                               xpT[:, m, n, :], start=m == 0, stop=m == 1)
                end(i, f"xpv{n}")
            for n in range(XH):
                await_read(pe, f"xpv{n}")

            def open_sum(cb):
                for h in range(NH):
                    b = ACC_BANKS[2 * h + cb]
                    pe.wait_ge(freed[b], READS_IN_A[b])
                    i = mm(bank(b), ident, res[:, h, 512 * cb:512 * cb + 512], start=True, stop=True,
                           skip_group_check=True)
                i.then_inc(acc_set, 1)

            tokens_whole(26, ["xo0", "xo1"], ys_)
            tokens(28, ["xo2", "xo3"], ys_, 0, last=False)
            for c in (0, 1):
                await_read(pe, f"xo{c}")
            turn("Tf", res, (0, 1))
            open_sum(0)
            tokens(29, ["xo2", "xo3"], ys_, CT, first=False)
            for c in (2, 3):
                await_read(pe, f"xo{c}")
            turn("Tf", res, (2, 3))
            pe.wait_ge(router_loaded, 16)
            for h in range(NH):
                begin(f"route{h}")
            for part in range(2):
                for c in (2 * part, 2 * part + 1):
                    await_read(pe, f"Tf{c}")
                for h in range(NH):
                    for k in range(CT):
                        i = mm(pb(f"route{h}")[:, 0:N_ROUTES], xT[part][:, k, P * h:P * h + P],
                               router[:, CT * part + k, :], start=part == 0 and k == 0, stop=part == 1 and k == CT - 1)
                    if part:
                        end(i, f"route{h}")
            open_sum(1)
            pe.wait_ge(chosen, 1)
            picked = rt(4)
            b = begin("rank")
            mm(b[:, 0:EXPERTS], const("before"), picked[:, 0], start=True, stop=True)
            mm(b[:, EXPERTS:2 * EXPERTS], const("before"), picked[:, 1], start=True, stop=False)
            end(mm(b[:, EXPERTS:2 * EXPERTS], ones, picked[:, 0], start=False, stop=True), "rank")
            pe.wait_ge(rank_ready, 1)
            b = begin("over")
            end(mm(b[:, 0:1], ones, soft[:, 0:1], start=True, stop=True), "over")

            GATHER, HY, GU = 4, 6, 7
            await_read(pe, "rank")
            await_read(pe, "over")
            pe.wait_ge(normed_act, 3)
            pe.wait_ge(normed_dve, 3)
            with pe.Fori(0, BATCHES) as g:
                pe.wait_ge(taken, g + 1)
                for k in range(KC):
                    for h in range(NH):
                        i = mm(bank(GATHER + k // 4)[:, P * (k % 4):P * (k % 4) + P], res[:, h, P * k:P * k + P],
                               take[:, h].rearrange("p e s -> p (e s)"), start=h == 0, stop=h == NH - 1)
                i.then_inc(gathered, 1)
                pe.wait_ge(gtaken, g + 1)
                for h in range(NH):
                    i = tr(bank(HY)[:, P * h:P * h + P], gtake[:, h].rearrange("p e s -> p (e s)"), ident)
                i.then_inc(turned, 1)
                pe.wait_ge(xg_ready, g + 1)
                for j in range(BATCH):
                    n = BATCH * g + (j + 1)
                    half = bank(GU)[:, 256 * (j % 2):256 * (j % 2) + 256]
                    for part in range(2):
                        u = EXPERT_UNITS[j][part]
                        pe.wait_ge(loaded[u], 16 * g + 16)
                        w = expert_gu(j, part).rearrange("p c (two n) -> p c two n", two=2)
                        for k in range(CT):
                            for strip in range(BATCH):
                                i = mm(half[SLOTS * strip:SLOTS * strip + SLOTS],
                                       xg[:, CT * part + k, SLOTS * j:SLOTS * j + SLOTS],
                                       w[:, k, :, P * strip:P * strip + P],
                                       start=part == 0 and k == 0, stop=part == 1 and k == CT - 1,
                                       tile_position=(0, SLOTS * strip))
                    i.then_inc(gu_done, 1)
                    if j:
                        pe.wait_ge(y_act, n - 1)
                        pe.wait_ge(y_dve, n - 1)
                    else:
                        pe.wait_ge(give_ready, g + 1)
                    pe.wait_ge(hid_ready, n)
                    tr(bank(HY)[:, 256:256 + P], hid, ident).then_inc(hid_turned, 1)
                    u = EXPERT_UNITS[j][2]
                    pe.wait_ge(loaded[u], 16 * g + 16)
                    w = expert_down(j)
                    pe.wait_ge(hidT_ready, n)
                    for k in range(CT):
                        for strip in range(BATCH):
                            i = mm(bank(HY)[SLOTS * strip:SLOTS * strip + SLOTS, 0:256],
                                   hidT[:, SLOTS * k:SLOTS * k + SLOTS], w[:, k, 256 * strip:256 * strip + 256],
                                   start=k == 0, stop=k == CT - 1, tile_position=(0, SLOTS * strip))
                    i.then_inc(y_done, 1)
                pe.wait_ge(y_act, BATCH * g + BATCH)
                pe.wait_ge(y_dve, BATCH * g + BATCH)
                for n, b in enumerate(ACC_BANKS):
                    i = mm(bank(b), give[:, P * (n // 2):P * (n // 2) + P], ybuf[:, 512 * (n % 2):512 * (n % 2) + 512],
                           start=False, stop=True, skip_group_check=True)
                i.then_inc(scattered, 1)

            over = pe.value_load(flag[0:1, 0:1])
            with pe.If(over > 0):
                for half in range(2):
                    for k in range(4):
                        for h in range(NH):
                            i = tr(bank(GATHER + k // 2 + 2 * half)[:, 256 * (k % 2) + P * h:256 * (k % 2) + P * h + P],
                                   res[:, h, P * (4 * half + k):P * (4 * half + k) + P], ident)
                i.then_inc(ov_turned, 1)
                pe.wait_ge(ov_xT, 1)
                mm(bank(GATHER)[0:1, 0:1], ident[0:1, 0:1], ident[0:1, 0:1], start=True, stop=True).then_inc(ov_added, 1)
                with pe.Fori(0, EXPERTS) as e:
                    pe.wait_ge(ov_loaded, 48 * e + 48)
                    for h in range(NH):
                        n = NH * e + (h + 1)
                        for c in range(2):
                            for k in range(KC):
                                i = mm(bank(GATHER + c), ov_x[:, k, P * h:P * h + P],
                                       ov_gu_w[k // CT][:, k % CT, 512 * c:512 * c + 512], start=k == 0, stop=k == KC - 1)
                        i.then_inc(ov_gu, 1)
                        pe.wait_ge(ov_hid, n)
                        for k in range(CT):
                            i = tr(bank(HY)[:, P * k:P * k + P], ov_h[:, P * k:P * k + P], ident)
                        i.then_inc(ov_hidT_done, 1)
                        pe.wait_ge(ov_hidT, n)
                        for c in range(2):
                            for k in range(CT):
                                i = mm(bank(GATHER + c), ov_ht[:, P * k:P * k + P],
                                       ov_down_w[:, k, 512 * c:512 * c + 512], start=k == 0, stop=k == CT - 1)
                        i.then_inc(ov_y, 1)
                        pe.wait_ge(ov_scaled, n)
                        for c in range(2):
                            i = mm(bank(ACC_BANKS[2 * h + c]), ident, ov_ysc[:, 512 * c:512 * c + 512], start=False,
                                   stop=True, skip_group_check=True)
                        i.then_inc(ov_added, 1)

        @block.scalar
        def _(act):
            steps = [0]

            def link(ins):
                steps[0] += 1
                ins.then_inc(act_step, 1)
                act.wait_ge(act_step, steps[0])

            def copy(dst, src, scale=1.0, bias=0.0):
                return nc.scalar.activation(dst, src, ACT.Identity, scale=scale, bias=bias)

            def release(ins, job):
                ins.then_inc(freed[BANK_OF[job]], 1)

            def split_hi(m):
                act.wait_ge(raw_loaded[m % RAW], 16 * (m // RAW + 1))
                if m >= SLOTS_W:
                    await_half_used(act, m - SLOTS_W)
                copy(slot(m, chunks_of(m))[0], raw(m, chunks_of(m))).then_inc(w_hi, 1)

            def sum_squares(src, stage, halves=range(NH)):
                for h in halves:
                    col = SS + 2 * (stage - 1) + h
                    nc.scalar.activation(sq, src[:, h], ACT.Square, accum_out=stat[:, col:col + 1]
                                         ).then_inc(sumsq, 1)
                    act.wait_ge(sumsq, 2 * (stage - 1) + h + 1)

            def scale_half(stage, src, dst):
                act.wait_ge(rstd, stage)
                col = RS + 2 * (stage - 1) + 1
                copy(dst[:, 1], src[:, 1], stat[:, col:col + 1]).then_inc(normed_act, 1)

            def turned_hi(prefix, dst, gain, cs=range(4)):
                for c in cs:
                    await_fill(act, f"{prefix}{c}")
                    for k in range(2):
                        i = copy(dst[0][:, 2 * c + k], pb(f"{prefix}{c}")[:, 256 * k:256 * k + 256],
                                 param(gain, 2 * c + k))
                    release(i, f"{prefix}{c}")

            def plain(job, dst, c=2):
                await_fill(act, job)
                src = pb(job).rearrange("p (c t) -> p c t", c=c) if c else pb(job)
                release(copy(dst, src), job)

            for h in range(NH):
                act.wait_ge(x_loaded[h], 16)
                sum_squares(res, 1, (h,))
            scale_half(1, res, xtok)
            split_hi(0)
            act.wait_ge(early_loaded, 16)
            turned_hi("Tx", xs_, "norm_mix")
            split_hi(1)
            act.wait_ge(lambda_abs, 1)
            nc.scalar.activation(lru[:, 12:16], lru[:, 12:16], ACT.Exp, scale=-1.0).then_inc(lambda_exp, 1)
            split_hi(2)
            act.wait_ge(mem_loaded, 16)
            sum_squares(memraw, 2)
            scale_half(2, memraw, memraw)
            split_hi(3)
            plain("xl0", xlp[:, 0:2, CONV - 1:])
            split_hi(4)
            turned_hi("Tm", ms_, "norm_mem")
            split_hi(5)
            split_hi(6)
            for h in range(NH):
                plain(f"q{h}", qk[:, h, 0:512], None)
            split_hi(7)
            split_hi(8)
            for h in range(NH):
                plain(f"k{h}", qk[:, h, 512:], None)
            act.wait_ge(lru_params, 1)
            for n, (gate, dst) in enumerate((("rg", gate_r), ("ig", gate_i))):
                for c in range(2):
                    await_fill(act, f"{gate}{c}")
                    for k in range(2):
                        t = 2 * c + k
                        release(nc.scalar.activation(dst[:, t], pb(f"{gate}{c}")[:, 256 * k:256 * k + 256], ACT.Tanh,
                                                     scale=0.5, bias=lru[:, 4 * n + t:4 * n + t + 1]), f"{gate}{c}")
            for c in range(2):
                await_read(act, f"rg{c}")
            for t in range(CT):
                i = nc.scalar.activation(decay[:, t], gate_r[:, t], ACT.Exp, scale=lru[:, 28 + t:29 + t],
                                         bias=lru[:, 28 + t:29 + t])
            i.then_inc(decay_ready, 1)
            for t in range(CT):
                i = nc.scalar.activation(gate_r[:, t], gate_r[:, t], ACT.Tanh, scale=lru[:, 8 + t:9 + t],
                                         bias=lru[:, 8 + t:9 + t])
            i.then_inc(t2_ready, 1)
            act.wait_ge(t2_ready, 1)
            nc.scalar.activation(root, gate_r, ACT.Sqrt, scale=0.25).then_inc(root_ready, 1)
            split_hi(9)
            split_hi(10)
            for h in range(NH):
                plain(f"v{h}", v[:, h], None)
            for c in (0, 2):
                plain(f"Tqk{c}", qkT[:, 2 * c:2 * c + 2])
            split_hi(11)
            plain("gl0", gx[:, 0:2])
            split_hi(12)
            plain("gl1", gx[:, 2:4])
            for h, p in enumerate((p0, p1)):
                act.wait_ge(smax, h + 1)
                for n in range(HEADS):
                    i = nc.scalar.activation(p[:, n], p[:, n], ACT.Exp, bias=soft[:, 8 * h + n:8 * h + n + 1],
                                             accum_out=soft[:, 16 + 8 * h + n:17 + 8 * h + n])
                i.then_inc(sexp, 1)
                if h == 0:
                    split_hi(13)
            plain("xk0", xkT[:, 0:2])
            split_hi(14)
            plain("xk2", xkT[:, 4:6])
            for c in (0, 2):
                plain(f"Tp{c}", pTa[:, 2 * c:2 * c + 2])
            plain("Tp4", pTb[:, 0:4], 4)
            act.wait_ge(gelu_arg, 1)
            nc.scalar.activation(gate_i, gate_r, ACT.Tanh, scale=GELU_IN).then_inc(gelu_tanh, 1)
            split_hi(15)
            act.wait_ge(ylru_ready, 1)
            for t in range(CT):
                i = copy(ys_[0][:, t], ylru[:, t], param("norm_lru_out", t))
            i.then_inc(ylru_hi, 1)
            nc.scalar.activation(sqT[:, 0:CT], ylru, ACT.Square).then_inc(ylru_squared, 1)
            for c in range(2):
                await_fill(act, f"pv{c}")
                nc.scalar.activation(sqT[:, CT + 2 * c:CT + 2 * c + 2],
                                     pb(f"pv{c}").rearrange("p (c t) -> p c t", c=2), ACT.Square)
                for k in range(2):
                    i = copy(ys_[0][:, CT + 2 * c + k], pb(f"pv{c}")[:, 256 * k:256 * k + 256],
                             param("norm_attn_out", 2 * c + k))
                release(i, f"pv{c}")
            for m in (16, 17, 18, 19):
                split_hi(m)
            turned_hi("Th", hs_, "norm_cross", (0, 1))
            split_hi(20)
            split_hi(21)
            turned_hi("Th", hs_, "norm_cross", (2, 3))
            sum_squares(res, 3)
            split_hi(22)
            plain("xv0", xv[:, 0, 0:512], None)
            split_hi(23)
            plain("xq0", xqT[:, 0:2])
            split_hi(24)
            split_hi(25)
            plain("xq2", xqT[:, 4:6])
            split_hi(26)
            act.wait_ge(xscale, 1)
            for h in range(NH):
                for c in range(2):
                    job = f"xs{2 * h + c}"
                    act.wait_ge(xmax, 2 * h + c + 1)
                    for k in range(2):
                        n = 2 * c + k
                        i = nc.scalar.activation(xp[:, h, n], pb(job)[:, 256 * k:256 * k + 256], ACT.Exp,
                                                 scale=soft[:, 48 + h:49 + h], bias=soft[:, 32 + 4 * h + n:33 + 4 * h + n],
                                                 accum_out=soft[:, 40 + 4 * h + n:41 + 4 * h + n])
                    release(i, job)
            split_hi(27)
            plain("xv2", xv[:, 0, 512:], None)
            for c in (0, 2):
                plain(f"Txp{c}", xpT[:, c // 2, 0:2])
            split_hi(28)
            for c in range(4):
                plain(f"xpv{c}", ys_[0][:, 2 * c:2 * c + 2])
            split_hi(29)

            def turned_tokens(c):
                await_fill(act, f"Tf{c}")
                for k in range(2):
                    i = copy(xT[c // 2][:, 2 * (c % 2) + k], pb(f"Tf{c}")[:, 256 * k:256 * k + 256],
                             param("norm_ffn", 2 * c + k))
                release(i, f"Tf{c}")

            turned_tokens(0)
            for c in (2, 3):
                await_read(act, f"xo{c}")
            sum_squares(res, 4)
            turned_tokens(2)
            act.wait_ge(acc_set, 2)
            act.wait_ge(rstd, 4)
            copy(res[:, 1], res[:, 1], stat[:, RS + 7:RS + 8]).then_inc(normed_act, 1)
            act.wait_ge(group_arg, 1)
            nc.scalar.activation(rt(9, GROUPS), rt(8, GROUPS), ACT.Exp).then_inc(group_exp, 1)
            act.wait_ge(chosen, 1)
            nc.scalar.activation(soft[:, 56:58], soft[:, 54:56], ACT.Exp).then_inc(expert_exp, 1)

            GU, HY = 7, 6
            with act.Fori(0, BATCHES) as g:
                act.wait_ge(turned, g + 1)
                copy(give, bank(HY)[:, 0:S]).then_inc(give_ready, 1)
                for j in range(BATCH):
                    n = BATCH * g + (j + 1)
                    act.wait_ge(gu_done, n)
                    nc.scalar.activation(th, bank(GU)[:, 256 * (j % 2):256 * (j % 2) + P], ACT.Tanh, scale=0.5
                                         ).then_inc(gu_tanh, 1)
                    act.wait_ge(hid_turned, n)
                    copy(hidT, bank(HY)[:, 256:256 + P]).then_inc(hidT_ready, 1)
                    act.wait_ge(y_done, n)
                    for strip in range(2):
                        r = slice(SLOTS * strip, SLOTS * strip + SLOTS)
                        i = copy(ybuf[SLOTS * j:SLOTS * j + SLOTS, 256 * strip:256 * strip + 256], bank(HY)[r, 0:256])
                    i.then_inc(y_act, 1)

            await_read(act, "over")
            over = act.value_load(flag[0:1, 0:1])
            with act.If(over > 0):
                with act.Fori(0, EXPERTS) as e:
                    for h in range(NH):
                        n = NH * e + (h + 1)
                        act.wait_ge(ov_gu, n)
                        nc.scalar.activation(ov_th, bank(4), ACT.Tanh, scale=0.5).then_inc(ov_tanh, 1)
                        act.wait_ge(ov_hidT_done, n)
                        copy(ov_ht, bank(HY)).then_inc(ov_hidT, 1)
                act.wait_ge(ov_added, NH * EXPERTS + 1)
            act.wait_ge(scattered, BATCHES)
            for h in range(NH):
                nc.scalar.activation(sq.rearrange("p (c n) -> p c n", c=2), psum[:, 2 * h:2 * h + 2, :], ACT.Square,
                                     accum_out=stat[:, SS + FINAL + h:SS + FINAL + h + 1]).then_inc(final_sq, 1)
                act.wait_ge(final_sq, h + 1)

        @block.gpsimd
        def _(pool):
            nc.gpsimd.memset(xlp[:, :, 0:CONV - 1], 0.0).then_inc(zeroed, 1)
            pool.wait_ge(early_loaded, 16)

            def power(col, n, done):
                nc.gpsimd.tensor_tensor(stat[:, RS + col:RS + col + n], stat[:, MS + col:MS + col + n],
                                        const("power")[:, 0:n], ALU.pow).then_inc(done, 1)

            def split_lo(m):
                pool.wait_ge(w_hi, m + 1)
                hi, lo = slot(m, chunks_of(m))
                nc.gpsimd.tensor_tensor(lo, raw(m, chunks_of(m)), hi.bitcast(F32), ALU.subtract).then_inc(w_lo_pool, 1)

            for stage in (1, 2):
                pool.wait_ge(meansq, stage)
                power(2 * (stage - 1), 2, rstd)
            split_lo(6)
            split_lo(8)
            split_lo(10)
            pool.wait_ge(root_ready, 1)
            for c in range(2):
                await_read(pool, f"gl{c}")
            nc.gpsimd.tensor_tensor(gate_r, gx, gx, ALU.mult).then_inc(pool_step, 1)
            pool.wait_ge(pool_step, 1)
            nc.gpsimd.tensor_scalar(gate_r, gate_r, GELU_CUBE, 1.0, ALU.mult, ALU.add).then_inc(pool_step, 1)
            pool.wait_ge(pool_step, 2)
            nc.gpsimd.tensor_tensor(gate_r, gate_r, gx, ALU.mult).then_inc(gelu_arg, 1)
            split_lo(12)
            for part in range(2):
                if part:
                    for c in range(2):
                        await_first_read(pool, f"pv{c}")
                else:
                    pool.wait_ge(ylru_squared, 1)
                t = CT * part
                nc.gpsimd.tensor_tensor(sqT[:, t:t + 2], sqT[:, t:t + 2], sqT[:, t + 2:t + 4], ALU.add).then_inc(pool_step, 1)
                pool.wait_ge(pool_step, 3 + part)
                nc.gpsimd.tensor_tensor(sqT[:, t], sqT[:, t], sqT[:, t + 1], ALU.add).then_inc(squares_added, 1)
            await_read(pool, "ss")
            power(SUB, 4, sub_rstd)
            for stage in (3, 4):
                pool.wait_ge(meansq, stage)
                power(2 * (stage - 1), 2, rstd)
            pool.wait_ge(final_ms, 1)
            power(FINAL, 2, final_rstd)

        @block.vector
        def _(dve):
            steps = [0]
            V = nc.vector

            def link(ins):
                steps[0] += 1
                ins.then_inc(dve_step, 1)
                dve.wait_ge(dve_step, steps[0])

            def release(ins, job):
                ins.then_inc(freed[BANK_OF[job]], 1)

            def mean(col, n, width):
                return V.tensor_scalar(stat[:, MS + col:MS + col + n], stat[:, SS + col:SS + col + n],
                                       1.0 / width, EPS, ALU.mult, ALU.add)

            def split_lo(m):
                dve.wait_ge(w_hi, m + 1)
                hi, lo = slot(m, chunks_of(m))
                V.tensor_tensor(lo, raw(m, chunks_of(m)), hi.bitcast(F32), ALU.subtract).then_inc(w_lo, 1)

            def mean_squares(stage):
                dve.wait_ge(sumsq, 2 * stage)
                mean(2 * (stage - 1), 2, D).then_inc(meansq, 1)

            def scale_half(stage, src, dst):
                dve.wait_ge(rstd, stage)
                col = RS + 2 * (stage - 1)
                V.tensor_scalar(dst[:, 0], src[:, 0], stat[:, col:col + 1], None, ALU.mult).then_inc(normed_dve, 1)

            def rest(dst, src, gain, hi):
                return V.scalar_tensor_tensor(dst, src, gain, hi.bitcast(F32), ALU.mult, ALU.subtract)

            def turned_lo(prefix, dst, gain, cs=range(4)):
                for c in cs:
                    await_first_read(dve, f"{prefix}{c}")
                    for k in range(2):
                        t = 2 * c + k
                        i = rest(dst[1][:, t], pb(f"{prefix}{c}")[:, 256 * k:256 * k + 256], param(gain, t), dst[0][:, t])
                    release(i, f"{prefix}{c}")

            def plain(job, dst, c=2):
                await_fill(dve, job)
                src = pb(job).rearrange("p (c t) -> p c t", c=c) if c else pb(job)
                release(V.tensor_copy(dst, src), job)

            mean_squares(1)
            scale_half(1, res, xtok)
            split_lo(0)
            dve.wait_ge(early_loaded, 16)
            turned_lo("Tx", xs_, "norm_mix")
            split_lo(1)
            V.scalar_tensor_tensor(lru[:, 12:16], param("lru_lambda"), -1.0, param("lru_lambda"), ALU.mult, ALU.max
                                   ).then_inc(lambda_abs, 1)
            split_lo(2)
            mean_squares(2)
            scale_half(2, memraw, memraw)
            dve.wait_ge(lambda_exp, 1)
            z, s, s2, ser = lru[:, 12:16], lru[:, 16:20], lru[:, 20:24], lru[:, 24:28]
            link(V.tensor_scalar(s, z, 2.0, None, ALU.add))
            link(V.reciprocal(s, s))
            link(V.tensor_tensor(s, s, z, ALU.mult))
            link(V.tensor_tensor(s2, s, s, ALU.mult))
            link(V.tensor_scalar(ser, s2, 1.0 / 17, 1.0 / 15, ALU.mult, ALU.add))
            for odd in (13, 11, 9, 7, 5, 3, 1):
                link(V.tensor_tensor(ser, ser, s2, ALU.mult))
                link(V.tensor_scalar(ser, ser, 1.0 / odd, None, ALU.add))
            link(V.tensor_tensor(ser, ser, s, ALU.mult))
            link(V.tensor_scalar(s2, param("lru_lambda"), -1.0, 0.0, ALU.mult, ALU.max))
            link(V.scalar_tensor_tensor(s, ser, 2.0, s2, ALU.mult, ALU.add))
            link(V.tensor_scalar(lru[:, 8:12], s, 8.0 / 4, None, ALU.mult))
            link(V.tensor_scalar(lru[:, 28:32], s, -8.0 / 2, None, ALU.mult))
            link(V.tensor_scalar(lru[:, 0:4], param("b_rg"), 0.5, None, ALU.mult))
            V.tensor_scalar(lru[:, 4:8], param("b_ig"), 0.5, None, ALU.mult).then_inc(lru_params, 1)
            split_lo(3)
            plain("xl1", xlp[:, 2:4, CONV - 1:])
            await_read(dve, "xl0")
            await_read(dve, "xl1")
            dve.wait_ge(zeroed, 1)
            conv_w, _ = PARAMS["conv_w"]
            conv_w += N_CONSTS
            for w in range(CONV):
                for t in range(CT):
                    tap = ctab[:, conv_w + CT * w + t:conv_w + CT * w + t + 1]
                    src = xlp[:, t, w:w + S]
                    if w == 0:
                        i = V.tensor_scalar(xc[:, t], src, tap, param("conv_b", t), ALU.mult, ALU.add)
                    else:
                        i = V.scalar_tensor_tensor(xc[:, t], src, tap, xc[:, t], ALU.mult, ALU.add)
                if w < CONV - 1:
                    link(i)
            i.then_inc(conv_done, 1)
            split_lo(4)
            turned_lo("Tm", ms_, "norm_mem")
            split_lo(5)
            split_lo(7)
            for name in ("q", "k"):
                for h in range(NH):
                    await_read(dve, f"{name}{h}")
            for h in range(NH):
                heads = qk[:, h].rearrange("p (n d) -> p n d", n=2 * HEADS)
                x1, x2 = heads[:, :, 0:HALF_ROT], heads[:, :, HALF_ROT:2 * HALF_ROT]
                shape = [P, 2 * HEADS, HALF_ROT]
                c_, s_ = cos[:, h].unsqueeze(1).to_broadcast(shape), sin[:, h].unsqueeze(1).to_broadcast(shape)
                t = [rope[:, k, P * h:P * h + P].rearrange("p (n r) -> p n r", n=2 * HEADS) for k in range(4)]
                V.tensor_tensor(t[0], x1, c_, ALU.mult)
                V.tensor_tensor(t[1], x2, s_, ALU.mult)
                V.tensor_tensor(t[2], x2, c_, ALU.mult)
                link(V.tensor_tensor(t[3], x1, s_, ALU.mult))
                V.tensor_tensor(x1, t[0], t[1], ALU.subtract)
                i = V.tensor_tensor(x2, t[2], t[3], ALU.add)
            i.then_inc(rope_done, 1)
            for c in range(2):
                await_read(dve, f"ig{c}")
            link(V.scalar_tensor_tensor(gate_i, gate_i, 1.0, xc, ALU.add, ALU.mult))
            split_lo(9)
            dve.wait_ge(decay_ready, 1)
            dve.wait_ge(root_ready, 1)
            link(V.scalar_tensor_tensor(root, decay, 1.0, root, ALU.add, ALU.mult))
            link(V.tensor_tensor(root, root, gate_i, ALU.mult))
            for c in (1, 3):
                plain(f"Tqk{c}", qkT[:, 2 * c:2 * c + 2])
            split_lo(11)
            for t in range(CT):
                i = V.tensor_tensor_scan(xc[:, t], decay[:, t], root[:, t], 0.0, ALU.mult, ALU.add)
            i.then_inc(scanned, 1)
            for job, par in (("s0e", 0), ("s0o", 1)):
                await_fill(dve, job)
                release(V.scalar_tensor_tensor(p0[:, par::2], pb(job).rearrange("p (n k) -> p n k", n=4), HD ** -0.5,
                                               const("causal")[:, P:S].unsqueeze(1).to_broadcast([P, 4, P]),
                                               ALU.mult, ALU.add), job)
            for job in ("s0e", "s0o"):
                await_read(dve, job)
            V.tensor_reduce(soft[:, 0:8], p0, AX.X, ALU.max, negate=True).then_inc(smax, 1)
            for c in range(4):
                await_fill(dve, f"s1{c}")
                first = 4 * (c // 2) + c % 2
                release(V.scalar_tensor_tensor(p1[:, first:first + 3:2],
                                               pb(f"s1{c}").rearrange("p (n k) -> p n k", n=2), HD ** -0.5,
                                               const("causal").unsqueeze(1).to_broadcast([P, 2, S]),
                                               ALU.mult, ALU.add), f"s1{c}")
            for c in range(4):
                await_read(dve, f"s1{c}")
            V.tensor_reduce(soft[:, 8:16], p1, AX.X, ALU.max, negate=True).then_inc(smax, 1)
            split_lo(13)

            def normalize(h, p):
                dve.wait_ge(sexp, h + 1)
                link(V.reciprocal(soft[:, 16 + 8 * h:24 + 8 * h], soft[:, 16 + 8 * h:24 + 8 * h]))
                V.tensor_tensor(p, p, soft[:, 16 + 8 * h:24 + 8 * h].unsqueeze(2).to_broadcast([P, HEADS, P * (h + 1)]),
                                ALU.mult).then_inc(snorm, 1)

            normalize(0, p0)
            normalize(1, p1)
            split_lo(14)
            plain("xk1", xkT[:, 2:4])
            plain("xk3", xkT[:, 6:8])
            for c in (1, 3):
                plain(f"Tp{c}", pTa[:, 2 * c:2 * c + 2])
            plain("Tp5", pTb[:, 4:8], 4)
            dve.wait_ge(scanned, 1)
            dve.wait_ge(gelu_tanh, 1)
            link(V.scalar_tensor_tensor(gate_i, gate_i, 1.0, gx, ALU.add, ALU.mult))
            V.scalar_tensor_tensor(ylru, gate_i, 0.5, xc, ALU.mult, ALU.mult).then_inc(ylru_ready, 1)
            split_lo(15)
            dve.wait_ge(ylru_ready, 1)
            dve.wait_ge(ylru_hi, 1)
            for t in range(CT):
                i = rest(ys_[1][:, t], ylru[:, t], param("norm_lru_out", t), ys_[0][:, t])
            i.then_inc(ylru_lo, 1)
            for c in range(2):
                await_first_read(dve, f"pv{c}")
                for k in range(2):
                    t = CT + 2 * c + k
                    i = rest(ys_[1][:, t], pb(f"pv{c}")[:, 256 * k:256 * k + 256], param("norm_attn_out", 2 * c + k),
                             ys_[0][:, t])
                release(i, f"pv{c}")
            split_lo(16)
            split_lo(17)
            await_fill(dve, "ss")
            release(V.tensor_scalar(stat[:, MS + SUB:MS + SUB + 4], pb("ss")[:, 0:4], 1.0 / DL, EPS, ALU.mult, ALU.add), "ss")
            split_lo(18)
            dve.wait_ge(sub_rstd, 1)

            def add_out(cb, part):
                for h in range(NH):
                    job = f"out{4 * cb + 2 * part + h}"
                    await_fill(dve, job)
                    if part:
                        await_read(dve, f"out{4 * cb + h}")
                    o = res[:, h, 512 * cb:512 * cb + 512]
                    col = RS + SUB + 2 * part + h
                    release(V.scalar_tensor_tensor(o, pb(job), stat[:, col:col + 1], o, ALU.mult, ALU.add), job)

            add_out(0, 0)
            add_out(0, 1)
            split_lo(19)
            add_out(1, 0)
            turned_lo("Th", hs_, "norm_cross", (0, 1))
            split_lo(20)
            add_out(1, 1)
            split_lo(21)
            turned_lo("Th", hs_, "norm_cross", (2, 3))
            mean_squares(3)
            split_lo(22)
            dve.wait_ge(rstd, 3)
            V.tensor_scalar(soft[:, 48:50], stat[:, RS + 4:RS + 6], XHD ** -0.5, None, ALU.mult).then_inc(xscale, 1)
            plain("xv1", xv[:, 1, 0:512], None)
            split_lo(23)
            split_lo(24)
            plain("xq1", xqT[:, 2:4])
            split_lo(25)
            plain("xq3", xqT[:, 6:8])
            split_lo(26)
            dve.wait_ge(xscale, 1)
            for h in range(NH):
                for c in range(2):
                    job, col = f"xs{2 * h + c}", 32 + 4 * h + 2 * c
                    await_fill(dve, job)
                    release(V.tensor_reduce(soft[:, col:col + 2], pb(job).rearrange("p (n k) -> p n k", n=2), AX.X,
                                            ALU.max, negate=True), job)
                    await_first_read(dve, job)
                    V.tensor_scalar(soft[:, col:col + 2], soft[:, col:col + 2], soft[:, 48 + h:49 + h], None, ALU.mult
                                    ).then_inc(xmax, 1)
            for h in range(NH):
                for c in range(2):
                    await_read(dve, f"xs{2 * h + c}")
                r = soft[:, 40 + 4 * h:44 + 4 * h]
                link(V.reciprocal(r, r))
                V.tensor_tensor(xp[:, h], xp[:, h], r.unsqueeze(2).to_broadcast([P, XH, S]), ALU.mult).then_inc(xnorm, 1)
            split_lo(27)
            plain("xv3", xv[:, 1, 512:], None)
            for c in (1, 3):
                plain(f"Txp{c}", xpT[:, c // 2, 2:4])
            split_lo(28)
            for c in range(4):
                await_first_read(dve, f"xpv{c}")
                release(V.tensor_tensor(ys_[1][:, 2 * c:2 * c + 2], pb(f"xpv{c}").rearrange("p (c t) -> p c t", c=2),
                                        ys_[0][:, 2 * c:2 * c + 2].bitcast(F32), ALU.subtract), f"xpv{c}")
            split_lo(29)

            def add_xo(cb):
                for h in range(NH):
                    job = f"xo{2 * cb + h}"
                    await_fill(dve, job)
                    o = res[:, h, 512 * cb:512 * cb + 512]
                    release(V.tensor_tensor(o, pb(job), o, ALU.add), job)

            def turned_tokens(c):
                await_fill(dve, f"Tf{c}")
                for k in range(2):
                    i = V.tensor_scalar(xT[c // 2][:, 2 * (c % 2) + k], pb(f"Tf{c}")[:, 256 * k:256 * k + 256],
                                        param("norm_ffn", 2 * c + k), None, ALU.mult)
                release(i, f"Tf{c}")

            add_xo(0)
            turned_tokens(1)
            add_xo(1)
            mean_squares(4)
            turned_tokens(3)

            dve.wait_ge(rstd, 4)
            for h in range(NH):
                await_fill(dve, f"route{h}")
                release(V.scalar_tensor_tensor(logit[:, h], pb(f"route{h}")[:, 0:N_ROUTES],
                                               stat[:, RS + 6 + h:RS + 7 + h], route_bias, ALU.mult, ALU.add), f"route{h}")
            for h in range(NH):
                await_read(dve, f"route{h}")

            def spread(ap, n):
                return ap.unsqueeze(2).to_broadcast([P, NH, n])

            def first_of_max(src, n, best, cand, index, pick):
                link(V.tensor_reduce(best, src, AX.X, ALU.max))
                link(V.tensor_tensor(cand, src, spread(best, n), ALU.is_equal))
                link(V.scalar_tensor_tensor(cand, cand, -64.0, iota[:, 0:n].unsqueeze(1).to_broadcast([P, NH, n]),
                                            ALU.mult, ALU.add))
                link(V.tensor_reduce(index, cand, AX.X, ALU.min))
                link(V.tensor_tensor(pick, cand, spread(index, n), ALU.is_equal))

            g_best, g_index, g_sum = soft[:, 48:50], soft[:, 50:52], soft[:, 52:54]
            g_pick, g_cand = rt(10, GROUPS), rt(11, GROUPS)
            first_of_max(logit[:, :, 0:GROUPS], GROUPS, g_best, g_cand, g_index, g_pick)
            V.tensor_tensor(rt(8, GROUPS), logit[:, :, 0:GROUPS], spread(g_best, GROUPS), ALU.subtract).then_inc(group_arg, 1)
            link(V.tensor_scalar(g_pick, g_pick, 1.0, BIG, ALU.subtract, ALU.mult))
            within = rt(0)
            link(V.tensor_tensor(within.rearrange("p h (g e) -> p h g e", g=GROUPS),
                                 logit[:, :, GROUPS:].rearrange("p h (g e) -> p h g e", g=GROUPS),
                                 g_pick.unsqueeze(3).to_broadcast([P, NH, GROUPS, PER_GROUP]), ALU.add))
            best1, best2, index = soft[:, 32:34], soft[:, 34:36], soft[:, 36:38]
            cand, pick1, pick2, picked, rest = rt(1), rt(2), rt(3), rt(4), rt(5)
            first_of_max(within, EXPERTS, best1, cand, index, pick1)
            link(V.scalar_tensor_tensor(rest, pick1, -3 * BIG, within, ALU.mult, ALU.add))
            first_of_max(rest, EXPERTS, best2, cand, index, pick2)
            link(V.tensor_tensor(soft[:, 54:56], best2, best1, ALU.subtract))
            V.tensor_tensor(picked, pick1, pick2, ALU.add).then_inc(chosen, 1)
            dve.wait_ge(chosen, 1)
            dve.wait_ge(acc_set, 2)
            V.tensor_scalar(res[:, 0], res[:, 0], stat[:, RS + 6:RS + 7], None, ALU.mult).then_inc(normed_dve, 1)
            dve.wait_ge(group_exp, 1)
            link(V.tensor_reduce(g_sum, rt(9, GROUPS), AX.X, ALU.add))
            dve.wait_ge(expert_exp, 1)
            e21, gate1 = soft[:, 56:58], soft[:, 58:60]
            link(V.scalar_tensor_tensor(gate1, e21, 1.0, g_sum, ALU.add, ALU.mult))
            link(V.reciprocal(gate1, gate1))
            link(V.tensor_tensor(e21, e21, gate1, ALU.mult))
            link(V.tensor_tensor(pick1, pick1, spread(gate1, EXPERTS), ALU.mult))
            link(V.tensor_tensor(pick2, pick2, spread(e21, EXPERTS), ALU.mult))
            link(V.tensor_tensor(gates, pick1, pick2, ALU.add))
            await_fill(dve, "rank")
            release(V.scalar_tensor_tensor(rankm, pb("rank")[:, 0:2 * EXPERTS].rearrange("p (h e) -> p h e", h=NH), 1.0,
                                           picked, ALU.add, ALU.mult), "rank")
            await_read(dve, "rank")
            link(V.tensor_scalar(rankm, rankm, -1.0, None, ALU.add))
            over = rt(6)
            link(V.tensor_scalar(over, rankm, float(SLOTS), None, ALU.is_ge))
            V.tensor_reduce(soft[:, 0:1], over, AX.XY, ALU.add).then_inc(rank_ready, 1)
            await_fill(dve, "over")
            release(V.tensor_copy(flag, pb("over")[:, 0:1]), "over")
            await_read(dve, "over")

            with dve.Fori(0, BATCHES) as g:
                shape = [P, BATCH, SLOTS]
                for h in range(NH):
                    i = V.tensor_tensor(take[:, h], rankm[:, h, bass.ds(BATCH * g, BATCH)].unsqueeze(2).to_broadcast(shape),
                                        iota[:, 0:SLOTS].unsqueeze(1).to_broadcast(shape), ALU.is_equal)
                i.then_inc(taken, 1)
                dve.wait_ge(taken, g + 1)
                for h in range(NH):
                    i = V.tensor_tensor(gtake[:, h], take[:, h],
                                        gates[:, h, bass.ds(BATCH * g, BATCH)].unsqueeze(2).to_broadcast(shape), ALU.mult)
                i.then_inc(gtaken, 1)
                dve.wait_ge(gathered, g + 1)
                for half in range(2):
                    i = V.tensor_tensor(xg[:, 4 * half:4 * half + 4], bank(4 + half).rearrange("p (c n) -> p c n", c=4),
                                        param("norm_ffn")[:, 4 * half:4 * half + 4].unsqueeze(2).to_broadcast([P, 4, P]),
                                        ALU.mult)
                i.then_inc(xg_ready, 1)
                for j in range(BATCH):
                    n = BATCH * g + (j + 1)
                    half = bank(7)[:, 256 * (j % 2):256 * (j % 2) + 256]
                    dve.wait_ge(gu_tanh, n)
                    V.scalar_tensor_tensor(th, th, 1.0, half[:, 0:P], ALU.add, ALU.mult).then_inc(gu_half, 1)
                    dve.wait_ge(gu_half, n)
                    V.scalar_tensor_tensor(hid, th, 0.5, half[:, P:2 * P], ALU.mult, ALU.mult).then_inc(hid_ready, 1)
                    dve.wait_ge(y_done, n)
                    for strip in range(2, 4):
                        r = slice(SLOTS * strip, SLOTS * strip + SLOTS)
                        i = V.tensor_copy(ybuf[SLOTS * j:SLOTS * j + SLOTS, 256 * strip:256 * strip + 256], bank(6)[r, 0:256])
                    i.then_inc(y_dve, 1)

            many = dve.value_load(flag[0:1, 0:1])
            with dve.If(many > 0):
                dve.wait_ge(scattered, BATCHES)
                V.tensor_scalar(ov_gates, rankm, float(SLOTS), None, ALU.is_ge).then_inc(ov_gate, 1)
                dve.wait_ge(ov_gate, 1)
                V.tensor_tensor(ov_gates, ov_gates, gates, ALU.mult).then_inc(ov_gate, 1)
                dve.wait_ge(ov_gate, 2)
                dve.wait_ge(ov_turned, 1)
                for k in range(KC):
                    i = V.tensor_scalar(ov_x[:, k], bank(4 + k // 2)[:, 256 * (k % 2):256 * (k % 2) + 256],
                                        param("norm_ffn", k), None, ALU.mult)
                i.then_inc(ov_xT, 1)
                with dve.Fori(0, EXPERTS) as e:
                    for h in range(NH):
                        n = NH * e + (h + 1)
                        dve.wait_ge(ov_tanh, n)
                        V.scalar_tensor_tensor(ov_th, ov_th, 1.0, bank(4), ALU.add, ALU.mult).then_inc(ov_half, 1)
                        dve.wait_ge(ov_half, n)
                        V.scalar_tensor_tensor(ov_h, ov_th, 0.5, bank(5), ALU.mult, ALU.mult).then_inc(ov_hid, 1)
                        V.tensor_copy(ov_g, ov_gates[:, h, bass.ds(e, 1)]).then_inc(ov_gate, 1)
                        dve.wait_ge(ov_gate, n + 2)
                        dve.wait_ge(ov_y, n)
                        V.tensor_scalar(ov_ysc.rearrange("p (c n) -> p c n", c=2), psum[:, 4:6, :], ov_g, None,
                                        ALU.mult).then_inc(ov_scaled, 1)
                dve.wait_ge(ov_added, NH * EXPERTS + 1)

            dve.wait_ge(final_sq, NH)
            mean(FINAL, 2, D).then_inc(final_ms, 1)
            dve.wait_ge(final_rstd, 1)
            dve.wait_ge(gain_loaded, 16)
            for h in range(NH):
                V.scalar_tensor_tensor(fin[:, h].rearrange("p (c n) -> p c n", c=2), psum[:, 2 * h:2 * h + 2, :],
                                       stat[:, RS + FINAL + h:RS + FINAL + h + 1],
                                       gain_final.rearrange("p (c n) -> p c n", c=2), ALU.mult, ALU.mult
                                       ).then_inc(final_out, 1)


_WEIGHTS = ["w_in", "w_out", "w_xq", "w_xkv", "w_xo", "w_gate_up", "w_down", "norm_final"]


def kernel(**inputs):
    import concourse.bacc as bacc
    from concourse.bass_utils import run_bass_kernel_spmd

    nc = bacc.Bacc("TRN2", target_bir_lowering=False, num_devices=1, dynamic_dma_scratch_size=1024)
    arrays = {f"in_{name}": np.ascontiguousarray(inputs[name]) for name in ["x", "mem"] + _WEIGHTS}
    arrays["in_early"] = np.ascontiguousarray(np.concatenate([constants(), lay_out_params(inputs)], axis=1))
    arrays["in_late"] = np.ascontiguousarray(lay_out_late(inputs))
    args = [nc.dram_tensor(name, a.shape, F32, kind="ExternalInput").ap() for name, a in arrays.items()]
    args.append(nc.dram_tensor("out_0", (1, S, D), F32, kind="ExternalOutput").ap())
    block_kernel(nc, *args)
    r = run_bass_kernel_spmd(nc, [arrays], core_ids=[0])
    return r.results[0]["out_0"]
```

```python
from contextlib import ExitStack

import concourse.bass as bass
import numpy as np
from concourse import mybir

F32 = mybir.dt.float32
F32R = mybir.dt.float32r
I32 = mybir.dt.int32
ALU = mybir.AluOpType
ACT = mybir.ActivationFunctionType
AX = mybir.AxisListType

P = 128
D = 1024
S = 256
NH = S // P
KC = D // P
DL = 512
CT = DL // P
CONV = 4
HEADS = 8
HD = 64
HALF_ROT = 8
XH = 4
XHD = 256
GROUPS = 4
EXPERTS = 32
PER_GROUP = EXPERTS // GROUPS
FF = 512
EPS = 1e-6
UNIT = 4096
UNITS = 12
SLOTS = 32
BATCH = P // SLOTS
BATCHES = EXPERTS // BATCH
BIG = 1e30
GELU_IN = 0.7978845608028654
GELU_CUBE = 0.044715

EXPERT_UNITS = [(11, 7, 8), (10, 6, 9), (1, 2, 0), (3, 4, 5)]

STREAM = ["x_lru", "q", "k", "v", "g_lru", "xk0", "xk1", "out_lru", "out_attn", "xv0",
          "xq0", "xq1", "xv1", "xo0", "xo1"]
BY_COLUMNS = {"x_lru", "g_lru", "xk0", "xk1", "xq0", "xq1"}
HALVES = 2 * len(STREAM)
HALF = UNIT // 2
RAW = 4
UNIT_11_AT = 14
MIXER_DONE_AT = 24
SLOTS_W = 3
LAST_JOB = ["xl0", "xl1", None, "q1", None, "k1", None, "v1", "gl0", "gl1", "xk0", "xk1", "xk2", "xk3",
            "out1", "out5", "out3", "out7", None, "xv1", "xq0", "xq1", "xq2", "xq3", None, "xv3",
            None, "xo1", None, "xo3"]
POOL_LO = (6, 8, 10, 12)

PARAMS = {}
for _name, _cols in (("norm_mix", KC), ("norm_mem", KC), ("norm_cross", KC), ("norm_ffn", KC),
                     ("norm_lru_out", CT), ("norm_attn_out", CT), ("conv_b", CT), ("b_rg", CT),
                     ("b_ig", CT), ("lru_lambda", CT), ("conv_w", CONV * CT)):
    PARAMS[_name] = (sum(n for _, n in PARAMS.values()), _cols)
N_PARAMS = sum(n for _, n in PARAMS.values())
N_ROUTES = GROUPS + EXPERTS

CONSTS = {}
for _name, _cols in (("ident", P), ("before", P), ("causal", S), ("ones", P), ("iota", EXPERTS),
                     ("cos", NH * HALF_ROT), ("sin", NH * HALF_ROT), ("power", 4)):
    CONSTS[_name] = (sum(n for _, n in CONSTS.values()), _cols)
N_CONSTS = sum(n for _, n in CONSTS.values())


def constants():
    t = np.zeros((P, N_CONSTS), np.float32)

    def put(name, value):
        a, n = CONSTS[name]
        t[:, a:a + n] = value

    i = np.arange(P)
    put("ident", np.eye(P))
    put("before", i[:, None] < i[None, :])
    put("causal", np.where(np.arange(S)[None, :] - P <= i[:, None], 0.0, -BIG))
    put("ones", 1.0)
    put("iota", np.arange(EXPERTS)[None, :])
    rot = 2 * HALF_ROT
    inv_freq = np.float32(500000.0) ** (-np.arange(0, rot, 2, dtype=np.float32) / np.float32(rot))
    angle = np.arange(S, dtype=np.float32)[:, None] * inv_freq[None, :].astype(np.float32)
    for name, f in (("cos", np.cos), ("sin", np.sin)):
        put(name, f(angle).astype(np.float32).reshape(NH, P, HALF_ROT).transpose(1, 0, 2).reshape(P, -1))
    put("power", -0.5)
    return t


def lay_out_params(inputs):
    return np.concatenate([np.asarray(inputs[name]).reshape(n, P) for name, (_, n) in PARAMS.items()]).T


def lay_out_late(inputs):
    router = np.concatenate([np.asarray(inputs["w_router_group"])[0], np.asarray(inputs["w_router_expert"])[0]], axis=1)
    bias = np.concatenate([np.asarray(inputs["b_router_group"]), np.asarray(inputs["b_router_expert"])], axis=1)
    blocks = np.zeros((P, 2, CT, P), np.float32)
    for n, name in enumerate(("w_rg", "w_ig")):
        w = np.asarray(inputs[name])[0]
        for b in range(w.shape[0]):
            r = HD * (b % 2)
            blocks[r:r + HD, n, b // 2, r:r + HD] = w[b]
    return np.concatenate([router.reshape(KC, P, N_ROUTES).transpose(1, 0, 2).reshape(P, -1),
                           np.broadcast_to(bias, (P, N_ROUTES)), blocks.reshape(P, -1)], axis=1)


JOBS = []
JOBS += [(f"Tx{c}", 2) for c in range(4)]
JOBS += [(f"xl{c}", 1) for c in range(2)]
JOBS += [(f"Tm{c}", 2) for c in range(4)]
JOBS += [(f"q{h}", 1) for h in range(2)] + [(f"k{h}", 1) for h in range(2)]
JOBS += [(f"rg{c}", 2) for c in range(2)] + [(f"ig{c}", 2) for c in range(2)]
JOBS += [(f"v{h}", 1) for h in range(2)]
JOBS += [(f"Tqk{c}", 1) for c in range(4)]
JOBS += [(f"gl{c}", 1) for c in range(2)]
JOBS += [("s0e", 1), ("s0o", 1)] + [(f"s1{c}", 1) for c in range(4)]
JOBS += [(f"xk{c}", 1) for c in range(4)]
JOBS += [(f"Tp{c}", 1) for c in range(6)]
JOBS += [(f"out{c}", 1) for c in (0, 1)] + [(f"pv{c}", 2) for c in range(2)]
JOBS += [(f"out{c}", 1) for c in (4, 5)] + [("ss", 1)] + [(f"out{c}", 1) for c in (2, 3, 6, 7)]
JOBS += [(f"Th{c}", 2) for c in (0, 1)] + [(f"xv{c}", 1) for c in (0, 1)] + [(f"Th{c}", 2) for c in (2, 3)]
JOBS += [(f"xq{c}", 1) for c in range(4)] + [("xv2", 1)]
JOBS += [(f"xs{c}", 2) for c in range(4)] + [("xv3", 1)]
JOBS += [(f"Txp{c}", 1) for c in range(4)]
JOBS += [(f"xpv{c}", 2) for c in range(4)]
JOBS += [(f"xo{c}", 1) for c in range(4)]
JOBS += [("Tf0", 1), ("Tf1", 1), ("route0", 1), ("route1", 1), ("Tf2", 1), ("Tf3", 1), ("rank", 1), ("over", 1)]
BANKS = 8
OVER = 384
ACC_BANKS = (0, 1, 2, 3)
LATE = {"xo0": 6, "xo1": 7, "xo2": 4, "xo3": 5, "Tf0": 6, "Tf1": 7, "Tf2": 4, "Tf3": 5,
        "route0": 6, "route1": 7, "rank": 5, "over": 6}
BANK_OF, FILLS, FREED_BEFORE, FREED_AFTER = {}, {}, {}, {}
_fills, _reads = [0] * BANKS, [0] * BANKS
for _n, (_name, _parts) in enumerate(JOBS):
    _b = LATE.get(_name, _n % BANKS)
    BANK_OF[_name], FREED_BEFORE[_name] = _b, _reads[_b]
    _fills[_b] += 1
    _reads[_b] += _parts
    FILLS[_name], FREED_AFTER[_name] = _fills[_b], _reads[_b]
READS_IN_A = list(_reads)

def block_kernel(nc, x, mem, w_in, w_out, w_xq, w_xkv, w_xo, w_gate_up, w_down, norm_final, early, late, out):
    with ExitStack() as ctx:
        def sb(name, shape, dt=F32):
            return ctx.enter_context(nc.sbuf_tensor(name, shape, dt))[:]

        def sem(name):
            return ctx.enter_context(nc.semaphore(name))

        with (nc.sbuf_tensor("landing", [P, 2 * UNIT], F32) as landing,
              nc.sbuf_tensor("split_w", [P, 3 * UNIT], F32R) as split_w,
              nc.sbuf_tensor("split_act", [P, 2 * UNIT], F32R) as split_act,
              nc.sbuf_tensor("work", [P, 4 * UNIT], F32) as work):
            landing, split_w, split_act, work = landing[:], split_w[:], split_act[:], work[:]
        ring = sb("ring", [P, UNITS * UNIT])
        ctab = sb("ctab", [P, N_CONSTS + N_PARAMS])
        latetab = sb("latetab", [P, (KC + 1) * N_ROUTES])
        res = sb("res", [P, NH, D])
        xg = sb("xg", [P, KC, P])
        ybuf = sb("ybuf", [P, D])
        small = sb("small", [P, 9 * P])
        take, gtake = (small[:, a:a + NH * P].rearrange("p (h e s) -> p h e s", h=NH, e=BATCH) for a in (0, 2 * P))
        ntake = sb("ntake", [P, NH, P])
        give = small[:, 4 * P:6 * P]
        th, hid, hidT = (small[:, a:a + P] for a in (6 * P, 7 * P, 8 * P))
        rankm_more = sb("rankm", [P, NH, EXPERTS + BATCH])
        rankm = rankm_more[:, :, 0:EXPERTS]
        gates = sb("gates", [P, NH, EXPERTS])
        stat = sb("stat", [P, 64])
        soft = sb("soft", [P, 64])
        lru = sb("lru", [P, 32])
        flag = sb("flag", [P, 1], I32)
        psum = ctx.enter_context(nc.psum_tensor("psum", [P, BANKS, 512], F32))[:]

        def unit(u):
            return ring[:, u * UNIT:(u + 1) * UNIT]

        def scratch(u, off, n):
            return work[:, (u - 7) * UNIT + off:(u - 7) * UNIT + off + n]

        def spare(u, off, n):
            return ring[:, u * UNIT + off:u * UNIT + off + n]

        def const(name):
            a, n = CONSTS[name]
            return ctab[:, a:a + n]

        def param(name, c=None):
            a, n = PARAMS[name][0] + N_CONSTS, PARAMS[name][1]
            return ctab[:, a:a + n] if c is None else ctab[:, a + c:a + c + 1]

        def bank(b):
            return psum[:, b, :]

        def pb(job):
            return bank(BANK_OF[job])

        ident, ones, iota = const("ident"), const("ones"), const("iota")
        cos = const("cos").rearrange("p (h r) -> p h r", h=NH)
        sin = const("sin").rearrange("p (h r) -> p h r", h=NH)

        def tiles(ap, c=CT):
            return ap.rearrange("p (c t) -> p c t", c=c)

        xc = tiles(scratch(7, 0, 1024))
        gate_r = tiles(scratch(7, 1024, 1024))
        gate_i = tiles(scratch(7, 2048, 1024))
        gx = tiles(scratch(7, 3072, 1024))
        xtok = tiles(scratch(7, 0, 2048), NH)
        sqT = tiles(scratch(7, 1024, 2048), KC)
        PAD = S + CONV - 1
        xlp = tiles(scratch(8, 0, CT * PAD))
        root = tiles(scratch(8, 1040, 1024))
        ylru = root
        decay = tiles(scratch(8, 2064, 1024))
        qk = tiles(scratch(9, 0, 2048), NH)
        xkT = tiles(scratch(9, 0, 2048), KC)
        qkT = tiles(scratch(9, 2048, 2048), 2 * CT)
        memraw = tiles(scratch(10, 0, 2048), NH)
        v = tiles(scratch(10, 0, 1024), NH)
        p0 = tiles(scratch(10, 1024, 1024), HEADS)
        xv = tiles(scratch(10, 0, 2048), NH)
        p1 = tiles(scratch(10, 2048, 2048), HEADS)
        xqT = tiles(scratch(10, 2048, 2048), KC)
        pTa = tiles(scratch(9, 2048, 2048), HEADS)
        pTb = tiles(scratch(8, 2064, 1024), HEADS)
        rope = scratch(10, 1024, 1024).rearrange("p (k n) -> p k n", k=4)
        xp = scratch(9, 2048, 2048).rearrange("p (h n k) -> p h n k", h=NH, n=XH)
        xpT = scratch(9, 0, 2048).rearrange("p (m n q) -> p m n q", m=NH, n=XH)
        sq = small[:, 0:D]
        xT = [tiles(t) for t in (xg.rearrange("p c t -> p (c t)"), ybuf)]
        bd = tiles(ybuf, 2 * CT)
        router = latetab[:, 0:KC * N_ROUTES].rearrange("p (c n) -> p c n", c=KC)
        route_bias = latetab[:, KC * N_ROUTES:]

        def pair(src, off, c):
            return tuple(src[:, off + HALF * part:off + HALF * part + HALF].rearrange("p (c t) -> p c t", c=c)
                         for part in range(2))

        def slot(m, c):
            return pair(split_w, UNIT * (m % SLOTS_W), c)

        xs_ = pair(split_act, 0, KC)
        ys_ = xs_
        hs_ = xs_
        ms_ = pair(split_act, UNIT, KC)

        def raw(m, c):
            return landing[:, HALF * (m % RAW):HALF * (m % RAW) + HALF].rearrange("p (c t) -> p c t", c=c)

        def chunks_of(m):
            return KC if STREAM[m // 2] in BY_COLUMNS else CT

        def rt(n, m=EXPERTS):
            return small[:, 256 + 64 * n:256 + 64 * n + NH * m].rearrange("p (h e) -> p h e", h=NH)

        logit = small[:, 0:72].rearrange("p (h e) -> p h e", h=NH)

        x_in = x[0].rearrange("(h p) d -> p h d", p=P)
        mem_in = mem[0].rearrange("(h p) d -> p h d", p=P)
        out_d = out[0].rearrange("(h p) d -> p h d", p=P)

        def columns(w, a):
            return w[0].rearrange("(c p) n -> p c n", p=P)[:, :, a:a + 512]

        def half_source(m):
            name, part = STREAM[m // 2], m % 2
            if name in ("out_lru", "out_attn"):
                row = CT * (name == "out_attn")
                return columns(w_out, 512 * part)[:, row:row + CT, :]
            if name in BY_COLUMNS:
                return SOURCE[name][:, :, 256 * part:256 * part + 256]
            return SOURCE[name][:, CT * part:CT * part + CT, :]

        SOURCE = {
            "x_lru": columns(w_in, 0), "g_lru": columns(w_in, 512), "q": columns(w_in, 1024),
            "k": columns(w_in, 1536), "v": columns(w_in, 2048),
            "xk0": columns(w_xkv, 0), "xk1": columns(w_xkv, 512),
            "xv0": columns(w_xkv, 1024), "xv1": columns(w_xkv, 1536),
            "xq0": columns(w_xq, 0), "xq1": columns(w_xq, 512),
            "xo0": columns(w_xo, 0), "xo1": columns(w_xo, 512),
        }

        loaded = [[sem(f"loaded{u}_{side}") for side in range(2)] for u in range(UNITS)]
        filled = [sem(f"filled{b}") for b in range(BANKS)]
        freed = [sem(f"freed{b}") for b in range(BANKS)]
        raw_loaded = [sem(f"raw_loaded{r}") for r in range(RAW)]
        w_hi, w_lo, w_lo_pool = sem("w_hi"), sem("w_lo"), sem("w_lo_pool")
        w_lo_first = sem("w_lo_first")
        half_used = sem("half_used")
        x_loaded = [sem(f"x_loaded{h}") for h in range(NH)]
        mem_loaded, early_loaded = sem("mem_loaded"), sem("early_loaded")
        router_loaded, bd_loaded = sem("router_loaded"), sem("bd_loaded")
        zeroed = sem("zeroed")
        dve_step, act_step, pool_step = sem("dve_step"), sem("act_step"), sem("pool_step")
        sumsq, meansq, rstd = sem("sumsq"), sem("meansq"), sem("rstd")
        sub_rstd = sem("sub_rstd")
        normed_act, normed_dve = sem("normed_act"), sem("normed_dve")
        conv_done = sem("conv_done")
        lambda_abs, lambda_exp, lru_params = sem("lambda_abs"), sem("lambda_exp"), sem("lru_params")
        decay_ready, t2_ready, root_ready = sem("decay_ready"), sem("t2_ready"), sem("root_ready")
        scanned = sem("scanned")
        gelu_arg, gelu_tanh = sem("gelu_arg"), sem("gelu_tanh")
        ylru_ready, ylru_squared, ylru_hi, ylru_lo = sem("ylru_ready"), sem("ylru_squared"), sem("ylru_hi"), sem("ylru_lo")
        squares_added = sem("squares_added")
        rope_done = sem("rope_done")
        smax, sexp, snorm = sem("smax"), sem("sexp"), sem("snorm")
        xmax, xexp, xnorm = sem("xmax"), sem("xexp"), sem("xnorm")
        xscale = sem("xscale")
        group_arg, group_exp, expert_exp = sem("group_arg"), sem("group_exp"), sem("expert_exp")
        chosen, rank_known, over_ready = sem("chosen"), sem("rank_known"), sem("over_ready")
        slots_found, taken, gtaken = sem("slots_found"), sem("taken"), sem("gtaken")
        gathered, xg_ready = sem("gathered"), sem("xg_ready")
        turned, give_ready = sem("turned"), sem("give_ready")
        gu_used = sem("gu_used")
        gu_tanh, gu_half, hid_ready = sem("gu_tanh"), sem("gu_half"), sem("hid_ready")
        hid_turned, hidT_ready = sem("hid_turned"), sem("hidT_ready")
        y_done, y_act, y_dve = sem("y_done"), sem("y_act"), sem("y_dve")
        scattered = sem("scattered")
        ov_normed, ov_turned, ov_xT = sem("ov_normed"), sem("ov_turned"), sem("ov_xT")
        ov_loaded, ov_gu, ov_tanh, ov_half, ov_hid = (
            sem("ov_loaded"), sem("ov_gu"), sem("ov_tanh"), sem("ov_half"), sem("ov_hid"))
        ov_hidT_done, ov_hidT, ov_y, ov_gate, ov_scaled, ov_added = (
            sem("ov_hidT_done"), sem("ov_hidT"), sem("ov_y"), sem("ov_gate"), sem("ov_scaled"), sem("ov_added"))
        gain_loaded, final_sq, final_ms, final_rstd, final_out, stored = (
            sem("gain_loaded"), sem("final_sq"), sem("final_ms"), sem("final_rstd"), sem("final_out"), sem("stored"))

        gain_final = unit(EXPERT_UNITS[0][0])[:, 0:D]
        fin = unit(EXPERT_UNITS[0][1])[:, 0:2048].rearrange("p (h n) -> p h n", h=NH)

        final_squares = unit(EXPERT_UNITS[0][1])[:, 2048:3072]

        ov_gu_w = [unit(u).rearrange("p (c n) -> p c n", c=CT) for u in (0, 1)]
        ov_down_w = unit(2).rearrange("p (c n) -> p c n", c=CT)
        ov_x = tiles(spare(9, 0, 2048), KC)
        ov_th, ov_h, ov_ht = spare(9, 2048, 512), spare(9, 2560, 512), spare(9, 3072, 512)
        ov_ysc = spare(10, 0, 1024)
        ov_g = spare(10, 1024, 1)
        ov_gates = spare(10, 1088, NH * EXPERTS).rearrange("p (h e) -> p h e", h=NH)

        SS, MS, RS = 0, 16, 32
        SUB, FINAL = 8, 12

        def expert_gu(j, part):
            return unit(EXPERT_UNITS[j][part]).rearrange("p (c n) -> p c n", c=CT)

        def expert_down(j):
            return unit(EXPERT_UNITS[j][2]).rearrange("p (c n) -> p c n", c=CT)

        def await_fill(eng, job):
            eng.wait_ge(filled[BANK_OF[job]], FILLS[job])

        def await_read(eng, job):
            eng.wait_ge(freed[BANK_OF[job]], FREED_AFTER[job])

        def await_first_read(eng, job):
            eng.wait_ge(freed[BANK_OF[job]], FREED_BEFORE[job] + 1)

        def await_split(eng, m):
            by_pool = sum(n in POOL_LO for n in range(m + 1))
            eng.wait_ge(w_lo, m + 1 - by_pool)
            if by_pool:
                eng.wait_ge(w_lo_pool, by_pool)

        def await_half_used(eng, m):
            if LAST_JOB[m]:
                await_fill(eng, LAST_JOB[m])
            else:
                eng.wait_ge(half_used, sum(j is None for j in LAST_JOB[:m + 1]))

        block = ctx.enter_context(nc.Block())

        @block.sync
        def _(sp):
            def load_expert(e, j, part, sides=range(2)):
                u = EXPERT_UNITS[j][part]
                if part < 2:
                    src = w_gate_up[0, e].rearrange("(two c p) n -> two p c n", p=P, two=2)[part]
                else:
                    src = w_down[0, e].rearrange("(c p) n -> p c n", p=P)
                for side in sides:
                    c = slice(CT // 2 * side, CT // 2 * side + CT // 2)
                    sp.dma_start(unit(u).rearrange("p (c n) -> p c n", c=CT)[:, c], src[:, c]
                                 ).then_inc(loaded[u][side], 16)

            def load_half(m):
                if m >= RAW:
                    await_split(sp, m - RAW)
                sp.dma_start(raw(m, chunks_of(m)), half_source(m)).then_inc(raw_loaded[m % RAW], 16)

            for h in range(NH):
                sp.dma_start(res[:, h], x_in[:, h]).then_inc(x_loaded[h], 16)
            sp.dma_start(ctab, early).then_inc(early_loaded, 16)
            load_half(0)
            load_half(1)
            sp.dma_start(memraw, mem_in).then_inc(mem_loaded, 16)
            load_half(2)
            sp.dma_start(bd.rearrange("p c n -> p (c n)"), late[:, (KC + 1) * N_ROUTES:]).then_inc(bd_loaded, 16)
            load_half(3)
            sp.dma_start(latetab, late[:, 0:(KC + 1) * N_ROUTES]).then_inc(router_loaded, 16)
            sp.wait_ge(w_lo_first, 1)
            for m in range(4, HALVES):
                if m == UNIT_11_AT:
                    load_expert(0, 0, 0)
                if m == MIXER_DONE_AT:
                    await_fill(sp, "out7")
                    load_expert(0, 0, 1)
                    load_expert(0, 0, 2)
                load_half(m)

            await_split(sp, HALVES - 4)
            load_expert(2, 2, 0, (0,))
            await_fill(sp, "xs3")
            load_expert(1, 1, 0, (1,))
            for c in range(4):
                await_fill(sp, f"Txp{c}")
            load_expert(1, 1, 2, (1,))
            await_fill(sp, "xv3")
            load_expert(1, 1, 1)
            await_split(sp, HALVES - 3)
            load_expert(2, 2, 0, (1,))
            await_fill(sp, "xpv3")
            load_expert(1, 1, 0, (0,))
            load_expert(1, 1, 2, (0,))
            for side in range(2):
                await_split(sp, HALVES - 2 + side)
                load_expert(2, 2, 2, (side,))
            await_half_used(sp, HALVES - 3)
            load_expert(2, 2, 1)
            await_half_used(sp, HALVES - 2)
            load_expert(3, 3, 0)
            await_half_used(sp, HALVES - 1)
            load_expert(3, 3, 1)
            load_expert(3, 3, 2)
            with sp.Fori(1, BATCHES) as g:
                for j in range(BATCH):
                    for part in range(2):
                        for side in range(2):
                            sp.wait_ge(gu_used, 4 * BATCH * g + (4 * (j - BATCH) + 2 * part + side + 1))
                            load_expert(BATCH * g + j, j, part, (side,))
                    sp.wait_ge(y_done, BATCH * g + (j + 1 - BATCH))
                    load_expert(BATCH * g + j, j, 2)
            sp.wait_ge(gu_used, 4 * (EXPERTS - BATCH + 1))
            sp.dma_start(gain_final, norm_final.partition_broadcast(P)).then_inc(gain_loaded, 16)
            await_read(sp, "over")
            over = sp.value_load(flag[0:1, 0:1])
            with sp.If(over > 0):
                sp.wait_ge(scattered, NH * BATCHES)
                with sp.Fori(0, EXPERTS) as e:
                    sp.wait_ge(ov_added, NH * e + 1)
                    for part in range(2):
                        sp.dma_start(ov_gu_w[part], w_gate_up[0, e].rearrange("(two c p) n -> two p c n", p=P, two=2)[part]
                                     ).then_inc(ov_loaded, 16)
                    sp.dma_start(ov_down_w, w_down[0, e].rearrange("(c p) n -> p c n", p=P)).then_inc(ov_loaded, 16)
            for h in range(NH):
                for cb in range(2):
                    sp.wait_ge(final_out, 2 * h + cb + 1)
                    sp.dma_start(out_d[:, h, 512 * cb:512 * cb + 512], fin[:, h, 512 * cb:512 * cb + 512]
                                 ).then_inc(stored, 16)
            sp.wait_ge(stored, 2 * 16 * NH)

        @block.tensor
        def _(pe):
            mm, tr = nc.tensor.matmul, nc.tensor.transpose

            def begin(job):
                if FREED_BEFORE[job]:
                    pe.wait_ge(freed[BANK_OF[job]], FREED_BEFORE[job])
                return pb(job)

            def end(ins, job):
                ins.then_inc(filled[BANK_OF[job]], 1)

            def turn(prefix, src, cs=range(4)):
                for c in cs:
                    b = begin(f"{prefix}{c}")
                    for k in range(2):
                        for h in range(NH):
                            i = tr(b[:, 256 * k + P * h:256 * k + P * h + P],
                                   src[:, h, (2 * c + k) * P:(2 * c + k + 1) * P], ident)
                    end(i, f"{prefix}{c}")

            def channels(m, job, src, turned=None):
                await_split(pe, m)
                w = slot(m, KC)
                b = begin(job)
                for c in range(2):
                    for k in range(KC):
                        if turned and c == 0 and k % 2 == 0:
                            await_read(pe, f"{turned}{k // 2}")
                        if m == 0 and c == 0 and k == CT:
                            pe.wait_ge(w_lo_first, 1)
                        for n, (a, t) in enumerate(((1, 0), (0, 1), (0, 0))):
                            i = mm(b[:, 256 * c:256 * c + 256], w[a][:, k, P * c:P * c + P], src[t][:, k, :],
                                   start=k == 0 and n == 0, stop=k == KC - 1 and n == 2)
                end(i, job)

            def tokens(m, jobs, src, k0, first=True, last=True, turned=None, halves=range(NH)):
                await_split(pe, m)
                w = slot(m, CT)
                for h in halves:
                    b = begin(jobs[h]) if first else pb(jobs[h])
                    for k in range(CT):
                        if turned and h == 0 and k % 2 == 0:
                            await_read(pe, f"{turned}{(k0 + k) // 2}")
                        for n, (t, a) in enumerate(((1, 0), (0, 1), (0, 0))):
                            i = mm(b, src[t][:, k0 + k, P * h:P * h + P], w[a][:, k, :],
                                   start=first and k == 0 and n == 0, stop=last and k == CT - 1 and n == 2)
                    if last:
                        end(i, jobs[h])
                if not last and halves[-1] == NH - 1:
                    i.then_inc(half_used, 1)

            def tokens_whole(m, jobs, src, turned=None):
                tokens(m, jobs, src, 0, last=False, turned=turned)
                tokens(m + 1, jobs, src, CT, first=False, turned=turned)

            pe.wait_ge(early_loaded, 16)
            pe.wait_ge(normed_act, 1)
            pe.wait_ge(normed_dve, 1)
            turn("Tx", xtok)
            channels(0, "xl0", xs_, "Tx")
            channels(1, "xl1", xs_)
            pe.wait_ge(normed_act, 2)
            pe.wait_ge(normed_dve, 2)
            turn("Tm", memraw)
            tokens_whole(2, ["q0", "q1"], xs_)
            tokens_whole(4, ["k0", "k1"], xs_)
            pe.wait_ge(bd_loaded, 16)
            pe.wait_ge(conv_done, 1)
            for n, gate in enumerate(("rg", "ig")):
                for c in range(2):
                    b = begin(f"{gate}{c}")
                    for k in range(2):
                        i = mm(b[:, 256 * k:256 * k + 256], bd[:, CT * n + 2 * c + k, :], xc[:, 2 * c + k, :],
                               start=True, stop=True)
                    end(i, f"{gate}{c}")
            tokens_whole(6, ["v0", "v1"], xs_)
            pe.wait_ge(rope_done, 1)
            turn("Tqk", qk)
            channels(8, "gl0", xs_)
            channels(9, "gl1", xs_)
            for c in range(4):
                await_read(pe, f"Tqk{c}")

            def score(n, tok, keys, out_ap):
                r = slice(HD * (n % 2), HD * (n % 2) + HD)
                return mm(out_ap, qkT[r, n // 2, tok], qkT[r, CT + n // 2, keys], start=True, stop=True)

            for job in ("s0e", "s0o"):
                begin(job)
            for n in range(HEADS):
                job = ("s0e", "s0o")[n % 2]
                i = score(n, slice(0, P), slice(0, P), pb(job)[:, P * (n // 2):P * (n // 2) + P])
                if n >= HEADS - 2:
                    end(i, job)
            for c in range(4):
                begin(f"s1{c}")
            for n in range(HEADS):
                job, k = f"s1{2 * (n // 4) + n % 2}", n // 2 % 2
                i = score(n, slice(P, S), slice(0, S), pb(job)[:, 256 * k:256 * k + 256])
                if k:
                    end(i, job)
            for c in range(4):
                await_read(pe, f"Tm{c}")
            for n in range(4):
                channels(10 + n, f"xk{n}", ms_)
            pe.wait_ge(snorm, 2)
            for c in range(4):
                b = begin(f"Tp{c}")
                for k in range(2):
                    n = 2 * c + k
                    tr(b[:, 256 * k:256 * k + P], p0[:, n, :], ident)
                    i = tr(b[:, 256 * k + P:256 * k + 256], p1[:, n, 0:P], ident)
                end(i, f"Tp{c}")
            for c in range(2):
                b = begin(f"Tp{4 + c}")
                for k in range(4):
                    i = tr(b[:, P * k:P * k + P], p1[:, 4 * c + k, P:S], ident)
                end(i, f"Tp{4 + c}")
            pe.wait_ge(ylru_lo, 1)
            tokens(14, ["out0", "out1"], ys_, 0)
            for c in range(6):
                await_read(pe, f"Tp{c}")
            for h in range(NH):
                await_read(pe, f"v{h}")
            for c in range(2):
                b = begin(f"pv{c}")
                for n in range(4 * c, 4 * c + 4):
                    r = slice(HD * (n % 2), HD * (n % 2) + HD)
                    k = n // 2 % 2
                    mm(b[r, 256 * k:256 * k + 256], v[:, 0, HD * n:HD * n + HD], pTa[:, n, :],
                       start=True, stop=False, skip_group_check=True)
                    i = mm(b[r, 256 * k + P:256 * k + 256], v[:, 1, HD * n:HD * n + HD], pTb[:, n, :],
                           start=False, stop=True, skip_group_check=True)
                end(i, f"pv{c}")
            tokens(15, ["out4", "out5"], ys_, 0)
            pe.wait_ge(squares_added, 2)
            b = begin("ss")
            for part in range(2):
                for h in range(NH):
                    i = mm(b[:, 2 * part + h:2 * part + h + 1], sqT[:, CT * part, P * h:P * h + P], ones[:, 0:1],
                           start=True, stop=True)
            end(i, "ss")
            for c in range(2):
                await_read(pe, f"pv{c}")
            tokens(16, ["out2", "out3"], ys_, CT)
            tokens(17, ["out6", "out7"], ys_, CT)
            for c in range(4):
                await_read(pe, f"out{c}")
            turn("Th", res, (0, 1))
            tokens(18, ["xv0", "xv1"], ms_, 0, last=False)
            for c in range(4, 8):
                await_read(pe, f"out{c}")
            turn("Th", res, (2, 3))
            tokens(19, ["xv0", "xv1"], ms_, CT, first=False)
            for n in range(4):
                channels(20 + n, f"xq{n}", hs_, "Th")
            tokens(24, ["xv2", "xv3"], ms_, 0, last=False, halves=(0,))
            for c in range(4):
                await_read(pe, f"xk{c}")
                await_read(pe, f"xq{c}")
            for h in range(NH):
                for c in range(2):
                    b = begin(f"xs{2 * h + c}")
                    for k in range(2):
                        n = 2 * c + k
                        for m in range(2):
                            i = mm(b[:, 256 * k:256 * k + 256], xqT[:, 2 * n + m, P * h:P * h + P],
                                   xkT[:, 2 * n + m, :], start=m == 0, stop=m == 1)
                    end(i, f"xs{2 * h + c}")
            tokens(25, ["xv2", "xv3"], ms_, CT, first=False, halves=(0,))
            tokens(24, ["xv2", "xv3"], ms_, 0, last=False, halves=(1,))
            pe.wait_ge(xnorm, 2)
            for m in range(2):
                for c in range(2):
                    b = begin(f"Txp{2 * m + c}")
                    for k in range(2):
                        for h in range(NH):
                            i = tr(b[:, 256 * k + P * h:256 * k + P * h + P],
                                   xp[:, h, 2 * c + k, P * m:P * m + P], ident)
                    end(i, f"Txp{2 * m + c}")
            tokens(25, ["xv2", "xv3"], ms_, CT, first=False, halves=(1,))
            for c in range(4):
                await_read(pe, f"Txp{c}")
            for n in range(XH):
                for h in range(NH):
                    await_read(pe, f"xv{2 * (n // 2) + h}")
                b = begin(f"xpv{n}")
                for k in range(2):
                    for m in range(2):
                        i = mm(b[:, 256 * k:256 * k + 256], xv[:, m, XHD * n + P * k:XHD * n + P * k + P],
                               xpT[:, m, n, :], start=m == 0, stop=m == 1)
                end(i, f"xpv{n}")
            def open_sum(cb):
                for h in range(NH):
                    b = ACC_BANKS[2 * h + cb]
                    pe.wait_ge(freed[b], READS_IN_A[b])
                    mm(bank(b), ident, res[:, h, 512 * cb:512 * cb + 512], start=True, stop=True,
                           skip_group_check=True)

            tokens_whole(26, ["xo0", "xo1"], ys_, "xpv")
            tokens(28, ["xo2", "xo3"], ys_, 0, last=False)
            for c in (0, 1):
                await_read(pe, f"xo{c}")
            turn("Tf", res, (0, 1))
            tokens(29, ["xo2", "xo3"], ys_, CT, first=False)

            def route(part):
                for h in range(NH):
                    if part == 0:
                        begin(f"route{h}")
                    for c in (2 * part, 2 * part + 1):
                        await_read(pe, f"Tf{c}")
                    for k in range(CT):
                        i = mm(pb(f"route{h}")[:, 0:N_ROUTES], xT[part][:, k, P * h:P * h + P],
                               router[:, CT * part + k, :], start=part == 0 and k == 0, stop=part == 1 and k == CT - 1)
                    if part:
                        end(i, f"route{h}")

            pe.wait_ge(router_loaded, 16)
            route(0)
            for c in (2, 3):
                await_read(pe, f"xo{c}")
            turn("Tf", res, (2, 3))
            route(1)
            open_sum(0)
            pe.wait_ge(chosen, 1)
            picked = rt(4)
            b = begin("rank")
            mm(b[:, 0:EXPERTS], const("before"), picked[:, 0], start=True, stop=True)
            mm(b[:, EXPERTS:2 * EXPERTS], const("before"), picked[:, 1], start=True, stop=False)
            end(mm(b[:, EXPERTS:2 * EXPERTS], ones, picked[:, 0], start=False, stop=True), "rank")
            open_sum(1)
            GATHER, HY, GU = 4, 6, 7
            for h in range(NH):
                await_read(pe, f"route{h}")
            await_read(pe, "rank")
            pe.wait_ge(over_ready, 1)
            begin("over")
            end(mm(pb("over")[:, OVER:OVER + NH * EXPERTS], ones, rt(12).rearrange("p h e -> p (h e)"), start=True,
                   stop=True), "over")
            with pe.Fori(0, BATCHES) as g:
                pe.wait_ge(taken, g + 1)
                for part in range(2):
                    for k in range(CT):
                        for h in range(NH):
                            c = CT * part + k
                            i = mm(bank(GATHER + part)[:, P * k:P * k + P], res[:, h, P * c:P * c + P],
                                   ntake[:, h], start=h == 0, stop=h == NH - 1)
                    i.then_inc(gathered, 1)
                for j in range(BATCH):
                    n = BATCH * g + (j + 1)
                    half = bank(GU)[:, 256 * (j % 2):256 * (j % 2) + 256]
                    for part in range(2):
                        u = EXPERT_UNITS[j][part]
                        if j == 0:
                            pe.wait_ge(xg_ready, 2 * g + (1 + part))
                        w = expert_gu(j, part).rearrange("p c (two n) -> p c two n", two=2)
                        for k in range(CT):
                            if k % 2 == 0:
                                pe.wait_ge(loaded[u][k // 2], 16 * g + 16)
                            for strip in range(BATCH):
                                i = mm(half[SLOTS * strip:SLOTS * strip + SLOTS],
                                       xg[:, CT * part + k, SLOTS * j:SLOTS * j + SLOTS],
                                       w[:, k, :, P * strip:P * strip + P],
                                       start=part == 0 and k == 0, stop=part == 1 and k == CT - 1,
                                       tile_position=(0, SLOTS * strip))
                            if k % 2:
                                i.then_inc(gu_used, 1)
                    if j:
                        pe.wait_ge(y_act, n - 1)
                        pe.wait_ge(y_dve, n - 1)
                    else:
                        pe.wait_ge(gtaken, g + 1)
                        for h in range(NH):
                            i = tr(bank(HY)[:, P * h:P * h + P], gtake[:, h].rearrange("p e s -> p (e s)"), ident)
                        i.then_inc(turned, 1)
                        pe.wait_ge(give_ready, g + 1)
                    pe.wait_ge(hid_ready, n)
                    tr(bank(HY)[:, 256:256 + P], hid, ident).then_inc(hid_turned, 1)
                    u = EXPERT_UNITS[j][2]
                    w = expert_down(j)
                    pe.wait_ge(hidT_ready, n)
                    for k in range(CT):
                        if k % 2 == 0:
                            pe.wait_ge(loaded[u][k // 2], 16 * g + 16)
                        for strip in range(BATCH):
                            i = mm(bank(HY)[SLOTS * strip:SLOTS * strip + SLOTS, 0:256],
                                   hidT[:, SLOTS * k:SLOTS * k + SLOTS], w[:, k, 256 * strip:256 * strip + 256],
                                   start=k == 0, stop=k == CT - 1, tile_position=(0, SLOTS * strip))
                    i.then_inc(y_done, 1)
                pe.wait_ge(y_act, BATCH * g + BATCH)
                pe.wait_ge(y_dve, BATCH * g + BATCH)
                for h in range(NH):
                    for cb in range(2):
                        i = mm(bank(ACC_BANKS[2 * h + cb]), give[:, P * h:P * h + P], ybuf[:, 512 * cb:512 * cb + 512],
                               start=False, stop=True, skip_group_check=True)
                    i.then_inc(scattered, 1)

            await_read(pe, "over")
            over = pe.value_load(flag[0:1, 0:1])
            with pe.If(over > 0):
                pe.wait_ge(ov_normed, 1)
                for half in range(2):
                    for k in range(4):
                        for h in range(NH):
                            i = tr(bank(GATHER + k // 2 + 2 * half)[:, 256 * (k % 2) + P * h:256 * (k % 2) + P * h + P],
                                   res[:, h, P * (4 * half + k):P * (4 * half + k) + P], ident)
                i.then_inc(ov_turned, 1)
                pe.wait_ge(ov_xT, 1)
                mm(bank(GATHER)[0:1, 0:1], ident[0:1, 0:1], ident[0:1, 0:1], start=True, stop=True).then_inc(ov_added, 1)
                with pe.Fori(0, EXPERTS) as e:
                    pe.wait_ge(ov_loaded, 48 * e + 48)
                    for h in range(NH):
                        n = NH * e + (h + 1)
                        for c in range(2):
                            for k in range(KC):
                                i = mm(bank(GATHER + c), ov_x[:, k, P * h:P * h + P],
                                       ov_gu_w[k // CT][:, k % CT, 512 * c:512 * c + 512], start=k == 0, stop=k == KC - 1)
                        i.then_inc(ov_gu, 1)
                        pe.wait_ge(ov_hid, n)
                        for k in range(CT):
                            i = tr(bank(HY)[:, P * k:P * k + P], ov_h[:, P * k:P * k + P], ident)
                        i.then_inc(ov_hidT_done, 1)
                        pe.wait_ge(ov_hidT, n)
                        for c in range(2):
                            for k in range(CT):
                                i = mm(bank(GATHER + c), ov_ht[:, P * k:P * k + P],
                                       ov_down_w[:, k, 512 * c:512 * c + 512], start=k == 0, stop=k == CT - 1)
                        i.then_inc(ov_y, 1)
                        pe.wait_ge(ov_scaled, n)
                        for c in range(2):
                            i = mm(bank(ACC_BANKS[2 * h + c]), ident, ov_ysc[:, 512 * c:512 * c + 512], start=False,
                                   stop=True, skip_group_check=True)
                        i.then_inc(ov_added, 1)

        @block.scalar
        def _(act):
            steps = [0]

            def link(ins):
                steps[0] += 1
                ins.then_inc(act_step, 1)
                act.wait_ge(act_step, steps[0])

            def copy(dst, src, scale=1.0, bias=0.0):
                return nc.scalar.activation(dst, src, ACT.Identity, scale=scale, bias=bias)

            def release(ins, job):
                ins.then_inc(freed[BANK_OF[job]], 1)

            def split_hi(m):
                act.wait_ge(raw_loaded[m % RAW], 16 * (m // RAW + 1))
                if m >= SLOTS_W:
                    await_half_used(act, m - SLOTS_W)
                copy(slot(m, chunks_of(m))[0], raw(m, chunks_of(m))).then_inc(w_hi, 1)

            def sum_squares(src, stage, halves=range(NH)):
                for h in halves:
                    col = SS + 2 * (stage - 1) + h
                    nc.scalar.activation(sq, src[:, h], ACT.Square, accum_out=stat[:, col:col + 1]
                                         ).then_inc(sumsq, 1)
                    act.wait_ge(sumsq, 2 * (stage - 1) + h + 1)

            def scale_half(stage, src, dst):
                act.wait_ge(rstd, stage)
                col = RS + 2 * (stage - 1) + 1
                copy(dst[:, 1], src[:, 1], stat[:, col:col + 1]).then_inc(normed_act, 1)

            def turned_hi(prefix, dst, gain, cs=range(4)):
                for c in cs:
                    await_fill(act, f"{prefix}{c}")
                    for k in range(2):
                        i = copy(dst[0][:, 2 * c + k], pb(f"{prefix}{c}")[:, 256 * k:256 * k + 256],
                                 param(gain, 2 * c + k))
                    release(i, f"{prefix}{c}")

            def plain(job, dst, c=2):
                await_fill(act, job)
                src = pb(job).rearrange("p (c t) -> p c t", c=c) if c else pb(job)
                release(copy(dst, src), job)

            for h in range(NH):
                act.wait_ge(x_loaded[h], 16)
                sum_squares(res, 1, (h,))
            scale_half(1, res, xtok)
            split_hi(0)
            act.wait_ge(early_loaded, 16)
            turned_hi("Tx", xs_, "norm_mix")
            split_hi(1)
            act.wait_ge(lambda_abs, 1)
            nc.scalar.activation(lru[:, 12:16], lru[:, 12:16], ACT.Exp, scale=-1.0).then_inc(lambda_exp, 1)
            split_hi(2)
            act.wait_ge(mem_loaded, 16)
            sum_squares(memraw, 2)
            scale_half(2, memraw, memraw)
            split_hi(3)
            plain("xl0", xlp[:, 0:2, CONV - 1:])
            split_hi(4)
            split_hi(5)
            turned_hi("Tm", ms_, "norm_mem")
            split_hi(6)
            for h in range(NH):
                plain(f"q{h}", qk[:, h, 0:512], None)
            split_hi(7)
            split_hi(8)
            for h in range(NH):
                plain(f"k{h}", qk[:, h, 512:], None)
            act.wait_ge(lru_params, 1)
            for n, (gate, dst) in enumerate((("rg", gate_r), ("ig", gate_i))):
                for c in range(2):
                    await_fill(act, f"{gate}{c}")
                    for k in range(2):
                        t = 2 * c + k
                        release(nc.scalar.activation(dst[:, t], pb(f"{gate}{c}")[:, 256 * k:256 * k + 256], ACT.Tanh,
                                                     scale=0.5, bias=lru[:, 4 * n + t:4 * n + t + 1]), f"{gate}{c}")
            for c in range(2):
                await_read(act, f"rg{c}")
            for t in range(CT):
                i = nc.scalar.activation(decay[:, t], gate_r[:, t], ACT.Exp, scale=lru[:, 28 + t:29 + t],
                                         bias=lru[:, 28 + t:29 + t])
            i.then_inc(decay_ready, 1)
            for t in range(CT):
                i = nc.scalar.activation(gate_r[:, t], gate_r[:, t], ACT.Tanh, scale=lru[:, 8 + t:9 + t],
                                         bias=lru[:, 8 + t:9 + t])
            i.then_inc(t2_ready, 1)
            act.wait_ge(t2_ready, 1)
            nc.scalar.activation(root, gate_r, ACT.Sqrt, scale=0.25).then_inc(root_ready, 1)
            split_hi(9)
            split_hi(10)
            for h in range(NH):
                plain(f"v{h}", v[:, h], None)
            for c in (0, 2):
                plain(f"Tqk{c}", qkT[:, 2 * c:2 * c + 2])
            split_hi(11)
            plain("gl0", gx[:, 0:2])
            split_hi(12)
            plain("gl1", gx[:, 2:4])
            for h, p in enumerate((p0, p1)):
                act.wait_ge(smax, h + 1)
                for n in range(HEADS):
                    i = nc.scalar.activation(p[:, n], p[:, n], ACT.Exp, bias=soft[:, 8 * h + n:8 * h + n + 1],
                                             accum_out=soft[:, 16 + 8 * h + n:17 + 8 * h + n])
                i.then_inc(sexp, 1)
                if h == 0:
                    split_hi(13)
            act.wait_ge(gelu_arg, 1)
            nc.scalar.activation(gate_i, gate_r, ACT.Tanh, scale=GELU_IN).then_inc(gelu_tanh, 1)
            plain("xk0", xkT[:, 0:2])
            split_hi(14)
            act.wait_ge(ylru_ready, 1)
            for t in range(CT):
                i = copy(ys_[0][:, t], ylru[:, t], param("norm_lru_out", t))
            i.then_inc(ylru_hi, 1)
            nc.scalar.activation(sqT[:, 0:CT], ylru, ACT.Square).then_inc(ylru_squared, 1)
            plain("xk2", xkT[:, 4:6])
            for c in (0, 2):
                plain(f"Tp{c}", pTa[:, 2 * c:2 * c + 2])
            plain("Tp4", pTb[:, 0:4], 4)
            split_hi(15)
            split_hi(16)
            for c in range(2):
                await_fill(act, f"pv{c}")
                nc.scalar.activation(sqT[:, CT + 2 * c:CT + 2 * c + 2],
                                     pb(f"pv{c}").rearrange("p (c t) -> p c t", c=2), ACT.Square)
                for k in range(2):
                    i = copy(ys_[0][:, CT + 2 * c + k], pb(f"pv{c}")[:, 256 * k:256 * k + 256],
                             param("norm_attn_out", 2 * c + k))
                release(i, f"pv{c}")
            for m in (17, 18, 19):
                split_hi(m)
            turned_hi("Th", hs_, "norm_cross", (0, 1))
            split_hi(20)
            split_hi(21)
            turned_hi("Th", hs_, "norm_cross", (2, 3))
            sum_squares(res, 3)
            split_hi(22)
            plain("xv0", xv[:, 0, 0:512], None)
            split_hi(23)
            plain("xq0", xqT[:, 0:2])
            split_hi(24)
            split_hi(25)
            plain("xq2", xqT[:, 4:6])
            split_hi(26)
            act.wait_ge(xscale, 1)
            for h in range(NH):
                for c in range(2):
                    job = f"xs{2 * h + c}"
                    act.wait_ge(xmax, 2 * h + c + 1)
                    for k in range(2):
                        n = 2 * c + k
                        i = nc.scalar.activation(xp[:, h, n], pb(job)[:, 256 * k:256 * k + 256], ACT.Exp,
                                                 scale=soft[:, 48 + h:49 + h], bias=soft[:, 32 + 4 * h + n:33 + 4 * h + n],
                                                 accum_out=soft[:, 40 + 4 * h + n:41 + 4 * h + n])
                    release(i, job)
            plain("xv2", xv[:, 0, 512:], None)
            for c in (0, 2):
                plain(f"Txp{c}", xpT[:, c // 2, 0:2])
            split_hi(27)
            for c in range(4):
                plain(f"xpv{c}", ys_[0][:, 2 * c:2 * c + 2])
            split_hi(28)
            split_hi(29)

            def turned_tokens(c):
                await_fill(act, f"Tf{c}")
                for k in range(2):
                    i = copy(xT[c // 2][:, 2 * (c % 2) + k], pb(f"Tf{c}")[:, 256 * k:256 * k + 256],
                             param("norm_ffn", 2 * c + k))
                release(i, f"Tf{c}")

            turned_tokens(0)
            for h in range(NH):
                await_read(act, f"xo{2 + h}")
                sum_squares(res, 4, (h,))
            turned_tokens(2)
            act.wait_ge(group_arg, 1)
            nc.scalar.activation(rt(9, GROUPS), rt(8, GROUPS), ACT.Exp).then_inc(group_exp, 1)
            act.wait_ge(chosen, 1)
            nc.scalar.activation(soft[:, 32:40], soft[:, 24:32], ACT.Exp).then_inc(expert_exp, 1)

            GU, HY = 7, 6
            with act.Fori(0, BATCHES) as g:
                for j in range(BATCH):
                    n = BATCH * g + (j + 1)
                    act.wait_ge(gu_used, 4 * BATCH * g + 4 * (j + 1))
                    nc.scalar.activation(th, bank(GU)[:, 256 * (j % 2):256 * (j % 2) + P], ACT.Tanh, scale=0.5
                                         ).then_inc(gu_tanh, 1)
                    if j == 0:
                        act.wait_ge(turned, g + 1)
                        copy(give, bank(HY)[:, 0:S]).then_inc(give_ready, 1)
                    act.wait_ge(hid_turned, n)
                    copy(hidT, bank(HY)[:, 256:256 + P]).then_inc(hidT_ready, 1)
                    act.wait_ge(y_done, n)
                    for strip in range(2):
                        r = slice(SLOTS * strip, SLOTS * strip + SLOTS)
                        i = copy(ybuf[SLOTS * j:SLOTS * j + SLOTS, 256 * strip:256 * strip + 256], bank(HY)[r, 0:256])
                    i.then_inc(y_act, 1)

            await_read(act, "over")
            over = act.value_load(flag[0:1, 0:1])
            with act.If(over > 0):
                with act.Fori(0, EXPERTS) as e:
                    for h in range(NH):
                        n = NH * e + (h + 1)
                        act.wait_ge(ov_gu, n)
                        nc.scalar.activation(ov_th, bank(4), ACT.Tanh, scale=0.5).then_inc(ov_tanh, 1)
                        act.wait_ge(ov_hidT_done, n)
                        copy(ov_ht, bank(HY)).then_inc(ov_hidT, 1)
                act.wait_ge(ov_added, NH * EXPERTS + 1)
            for h in range(NH):
                act.wait_ge(scattered, NH * (BATCHES - 1) + h + 1)
                nc.scalar.activation(final_squares.rearrange("p (c n) -> p c n", c=2), psum[:, 2 * h:2 * h + 2, :], ACT.Square,
                                     accum_out=stat[:, SS + FINAL + h:SS + FINAL + h + 1]).then_inc(final_sq, 1)
                act.wait_ge(final_sq, h + 1)

        @block.gpsimd
        def _(pool):
            nc.gpsimd.memset(xlp[:, :, 0:CONV - 1], 0.0).then_inc(zeroed, 1)
            pool.wait_ge(early_loaded, 16)

            def power(col, n, done):
                nc.gpsimd.tensor_tensor(stat[:, RS + col:RS + col + n], stat[:, MS + col:MS + col + n],
                                        const("power")[:, 0:n], ALU.pow).then_inc(done, 1)

            def split_lo(m):
                pool.wait_ge(w_hi, m + 1)
                hi, lo = slot(m, chunks_of(m))
                nc.gpsimd.tensor_tensor(lo, raw(m, chunks_of(m)), hi.bitcast(F32), ALU.subtract).then_inc(w_lo_pool, 1)

            for stage in (1, 2):
                pool.wait_ge(meansq, stage)
                power(2 * (stage - 1), 2, rstd)
                if stage == 1:
                    pool.wait_ge(w_hi, 1)
                    hi, lo = slot(0, KC)
                    nc.gpsimd.tensor_tensor(lo[:, CT:], raw(0, KC)[:, CT:], hi[:, CT:].bitcast(F32), ALU.subtract
                                            ).then_inc(w_lo_first, 1)
            split_lo(6)
            split_lo(8)
            split_lo(10)
            pool.wait_ge(root_ready, 1)
            for c in range(2):
                await_read(pool, f"gl{c}")
            nc.gpsimd.tensor_tensor(gate_r, gx, gx, ALU.mult).then_inc(pool_step, 1)
            pool.wait_ge(pool_step, 1)
            nc.gpsimd.tensor_scalar(gate_r, gate_r, GELU_CUBE, 1.0, ALU.mult, ALU.add).then_inc(pool_step, 1)
            pool.wait_ge(pool_step, 2)
            nc.gpsimd.tensor_tensor(gate_r, gate_r, gx, ALU.mult).then_inc(gelu_arg, 1)
            split_lo(12)
            for part in range(2):
                if part:
                    for c in range(2):
                        await_first_read(pool, f"pv{c}")
                else:
                    pool.wait_ge(ylru_squared, 1)
                t = CT * part
                nc.gpsimd.tensor_tensor(sqT[:, t:t + 2], sqT[:, t:t + 2], sqT[:, t + 2:t + 4], ALU.add).then_inc(pool_step, 1)
                pool.wait_ge(pool_step, 3 + part)
                nc.gpsimd.tensor_tensor(sqT[:, t], sqT[:, t], sqT[:, t + 1], ALU.add).then_inc(squares_added, 1)
            await_read(pool, "ss")
            power(SUB, 4, sub_rstd)
            for stage in (3, 4):
                pool.wait_ge(meansq, stage)
                power(2 * (stage - 1), 2, rstd)
            pool.wait_ge(rank_known, 1)
            over = rt(12)
            nc.gpsimd.tensor_scalar(over, rankm, float(SLOTS), None, ALU.is_ge).then_inc(over_ready, 1)
            for h in range(NH):
                pool.wait_ge(final_ms, h + 1)
                power(FINAL + h, 1, final_rstd)

        @block.vector
        def _(dve):
            steps = [0]
            V = nc.vector

            def link(ins):
                steps[0] += 1
                ins.then_inc(dve_step, 1)
                dve.wait_ge(dve_step, steps[0])

            def release(ins, job):
                ins.then_inc(freed[BANK_OF[job]], 1)

            def mean(col, n, width):
                return V.tensor_scalar(stat[:, MS + col:MS + col + n], stat[:, SS + col:SS + col + n],
                                       1.0 / width, EPS, ALU.mult, ALU.add)

            def split_lo(m):
                dve.wait_ge(w_hi, m + 1)
                hi, lo = slot(m, chunks_of(m))
                V.tensor_tensor(lo, raw(m, chunks_of(m)), hi.bitcast(F32), ALU.subtract).then_inc(w_lo, 1)

            def mean_squares(stage):
                dve.wait_ge(sumsq, 2 * stage)
                mean(2 * (stage - 1), 2, D).then_inc(meansq, 1)

            def scale_half(stage, src, dst):
                dve.wait_ge(rstd, stage)
                col = RS + 2 * (stage - 1)
                V.tensor_scalar(dst[:, 0], src[:, 0], stat[:, col:col + 1], None, ALU.mult).then_inc(normed_dve, 1)

            def rest(dst, src, gain, hi):
                return V.scalar_tensor_tensor(dst, src, gain, hi.bitcast(F32), ALU.mult, ALU.subtract)

            def turned_lo(prefix, dst, gain, cs=range(4)):
                for c in cs:
                    await_first_read(dve, f"{prefix}{c}")
                    for k in range(2):
                        t = 2 * c + k
                        i = rest(dst[1][:, t], pb(f"{prefix}{c}")[:, 256 * k:256 * k + 256], param(gain, t), dst[0][:, t])
                    release(i, f"{prefix}{c}")

            def plain(job, dst, c=2):
                await_fill(dve, job)
                src = pb(job).rearrange("p (c t) -> p c t", c=c) if c else pb(job)
                release(V.tensor_copy(dst, src), job)

            mean_squares(1)
            scale_half(1, res, xtok)
            dve.wait_ge(w_hi, 1)
            hi, lo = slot(0, KC)
            V.tensor_tensor(lo[:, 0:CT], raw(0, KC)[:, 0:CT], hi[:, 0:CT].bitcast(F32), ALU.subtract).then_inc(w_lo, 1)
            dve.wait_ge(early_loaded, 16)
            turned_lo("Tx", xs_, "norm_mix")
            split_lo(1)
            V.scalar_tensor_tensor(lru[:, 12:16], param("lru_lambda"), -1.0, param("lru_lambda"), ALU.mult, ALU.max
                                   ).then_inc(lambda_abs, 1)
            split_lo(2)
            mean_squares(2)
            scale_half(2, memraw, memraw)
            dve.wait_ge(lambda_exp, 1)
            z, s, s2, ser = lru[:, 12:16], lru[:, 16:20], lru[:, 20:24], lru[:, 24:28]
            link(V.tensor_scalar(s, z, 2.0, None, ALU.add))
            link(V.reciprocal(s, s))
            link(V.tensor_tensor(s, s, z, ALU.mult))
            link(V.tensor_tensor(s2, s, s, ALU.mult))
            link(V.tensor_scalar(ser, s2, 1.0 / 17, 1.0 / 15, ALU.mult, ALU.add))
            for odd in (13, 11, 9, 7, 5, 3, 1):
                link(V.tensor_tensor(ser, ser, s2, ALU.mult))
                link(V.tensor_scalar(ser, ser, 1.0 / odd, None, ALU.add))
            link(V.tensor_tensor(ser, ser, s, ALU.mult))
            link(V.tensor_scalar(s2, param("lru_lambda"), -1.0, 0.0, ALU.mult, ALU.max))
            link(V.scalar_tensor_tensor(s, ser, 2.0, s2, ALU.mult, ALU.add))
            link(V.tensor_scalar(lru[:, 8:12], s, 8.0 / 4, None, ALU.mult))
            link(V.tensor_scalar(lru[:, 28:32], s, -8.0 / 2, None, ALU.mult))
            link(V.tensor_scalar(lru[:, 0:4], param("b_rg"), 0.5, None, ALU.mult))
            V.tensor_scalar(lru[:, 4:8], param("b_ig"), 0.5, None, ALU.mult).then_inc(lru_params, 1)
            split_lo(3)
            plain("xl1", xlp[:, 2:4, CONV - 1:])
            split_lo(4)
            await_read(dve, "xl0")
            await_read(dve, "xl1")
            dve.wait_ge(zeroed, 1)
            conv_w, _ = PARAMS["conv_w"]
            conv_w += N_CONSTS
            for w in range(CONV):
                for t in range(CT):
                    tap = ctab[:, conv_w + CT * w + t:conv_w + CT * w + t + 1]
                    src = xlp[:, t, w:w + S]
                    if w == 0:
                        i = V.tensor_scalar(xc[:, t], src, tap, param("conv_b", t), ALU.mult, ALU.add)
                    else:
                        i = V.scalar_tensor_tensor(xc[:, t], src, tap, xc[:, t], ALU.mult, ALU.add)
                if w < CONV - 1:
                    link(i)
            i.then_inc(conv_done, 1)
            split_lo(5)
            turned_lo("Tm", ms_, "norm_mem")
            split_lo(7)
            for name in ("q", "k"):
                for h in range(NH):
                    await_read(dve, f"{name}{h}")
            for h in range(NH):
                heads = qk[:, h].rearrange("p (n d) -> p n d", n=2 * HEADS)
                x1, x2 = heads[:, :, 0:HALF_ROT], heads[:, :, HALF_ROT:2 * HALF_ROT]
                shape = [P, 2 * HEADS, HALF_ROT]
                c_, s_ = cos[:, h].unsqueeze(1).to_broadcast(shape), sin[:, h].unsqueeze(1).to_broadcast(shape)
                t = [rope[:, k, P * h:P * h + P].rearrange("p (n r) -> p n r", n=2 * HEADS) for k in range(4)]
                V.tensor_tensor(t[0], x1, c_, ALU.mult)
                V.tensor_tensor(t[1], x2, s_, ALU.mult)
                V.tensor_tensor(t[2], x2, c_, ALU.mult)
                link(V.tensor_tensor(t[3], x1, s_, ALU.mult))
                V.tensor_tensor(x1, t[0], t[1], ALU.subtract)
                i = V.tensor_tensor(x2, t[2], t[3], ALU.add)
            i.then_inc(rope_done, 1)
            for c in range(2):
                await_read(dve, f"ig{c}")
            link(V.scalar_tensor_tensor(gate_i, gate_i, 1.0, xc, ALU.add, ALU.mult))
            split_lo(9)
            dve.wait_ge(decay_ready, 1)
            dve.wait_ge(root_ready, 1)
            link(V.scalar_tensor_tensor(root, decay, 1.0, root, ALU.add, ALU.mult))
            link(V.tensor_tensor(root, root, gate_i, ALU.mult))
            for c in (1, 3):
                plain(f"Tqk{c}", qkT[:, 2 * c:2 * c + 2])
            split_lo(11)
            for t in range(CT):
                i = V.tensor_tensor_scan(xc[:, t], decay[:, t], root[:, t], 0.0, ALU.mult, ALU.add)
            i.then_inc(scanned, 1)
            for job, par in (("s0e", 0), ("s0o", 1)):
                await_fill(dve, job)
                release(V.scalar_tensor_tensor(p0[:, par::2], pb(job).rearrange("p (n k) -> p n k", n=4), HD ** -0.5,
                                               const("causal")[:, P:S].unsqueeze(1).to_broadcast([P, 4, P]),
                                               ALU.mult, ALU.add), job)
            for job in ("s0e", "s0o"):
                await_read(dve, job)
            V.tensor_reduce(soft[:, 0:8], p0, AX.X, ALU.max, negate=True).then_inc(smax, 1)
            for c in range(4):
                await_fill(dve, f"s1{c}")
                first = 4 * (c // 2) + c % 2
                release(V.scalar_tensor_tensor(p1[:, first:first + 3:2],
                                               pb(f"s1{c}").rearrange("p (n k) -> p n k", n=2), HD ** -0.5,
                                               const("causal").unsqueeze(1).to_broadcast([P, 2, S]),
                                               ALU.mult, ALU.add), f"s1{c}")
            for c in range(4):
                await_read(dve, f"s1{c}")
            V.tensor_reduce(soft[:, 8:16], p1, AX.X, ALU.max, negate=True).then_inc(smax, 1)
            split_lo(13)

            def normalize(h, p):
                dve.wait_ge(sexp, h + 1)
                link(V.reciprocal(soft[:, 16 + 8 * h:24 + 8 * h], soft[:, 16 + 8 * h:24 + 8 * h]))
                V.tensor_tensor(p, p, soft[:, 16 + 8 * h:24 + 8 * h].unsqueeze(2).to_broadcast([P, HEADS, P * (h + 1)]),
                                ALU.mult).then_inc(snorm, 1)

            normalize(0, p0)
            normalize(1, p1)
            split_lo(14)
            plain("xk1", xkT[:, 2:4])
            dve.wait_ge(scanned, 1)
            dve.wait_ge(gelu_tanh, 1)
            link(V.scalar_tensor_tensor(gate_i, gate_i, 1.0, gx, ALU.add, ALU.mult))
            V.scalar_tensor_tensor(ylru, gate_i, 0.5, xc, ALU.mult, ALU.mult).then_inc(ylru_ready, 1)
            dve.wait_ge(ylru_ready, 1)
            dve.wait_ge(ylru_hi, 1)
            for t in range(CT):
                i = rest(ys_[1][:, t], ylru[:, t], param("norm_lru_out", t), ys_[0][:, t])
            i.then_inc(ylru_lo, 1)
            plain("xk3", xkT[:, 6:8])
            for c in (1, 3):
                plain(f"Tp{c}", pTa[:, 2 * c:2 * c + 2])
            plain("Tp5", pTb[:, 4:8], 4)
            split_lo(15)
            split_lo(16)
            for c in range(2):
                await_first_read(dve, f"pv{c}")
                for k in range(2):
                    t = CT + 2 * c + k
                    i = rest(ys_[1][:, t], pb(f"pv{c}")[:, 256 * k:256 * k + 256], param("norm_attn_out", 2 * c + k),
                             ys_[0][:, t])
                release(i, f"pv{c}")
            await_fill(dve, "ss")
            release(V.tensor_scalar(stat[:, MS + SUB:MS + SUB + 4], pb("ss")[:, 0:4], 1.0 / DL, EPS, ALU.mult, ALU.add), "ss")
            split_lo(17)
            dve.wait_ge(sub_rstd, 1)

            def add_out(cb, part):
                for h in range(NH):
                    job = f"out{4 * cb + 2 * part + h}"
                    await_fill(dve, job)
                    if part:
                        await_read(dve, f"out{4 * cb + h}")
                    o = res[:, h, 512 * cb:512 * cb + 512]
                    col = RS + SUB + 2 * part + h
                    release(V.scalar_tensor_tensor(o, pb(job), stat[:, col:col + 1], o, ALU.mult, ALU.add), job)

            add_out(0, 0)
            add_out(1, 0)
            split_lo(18)
            add_out(0, 1)
            split_lo(19)
            add_out(1, 1)
            turned_lo("Th", hs_, "norm_cross", (0, 1))
            split_lo(20)
            split_lo(21)
            turned_lo("Th", hs_, "norm_cross", (2, 3))
            mean_squares(3)
            split_lo(22)
            dve.wait_ge(rstd, 3)
            V.tensor_scalar(soft[:, 48:50], stat[:, RS + 4:RS + 6], XHD ** -0.5, None, ALU.mult).then_inc(xscale, 1)
            plain("xv1", xv[:, 1, 0:512], None)
            split_lo(23)
            split_lo(24)
            plain("xq1", xqT[:, 2:4])
            split_lo(25)
            plain("xq3", xqT[:, 6:8])
            split_lo(26)
            dve.wait_ge(xscale, 1)
            for h in range(NH):
                for c in range(2):
                    job, col = f"xs{2 * h + c}", 32 + 4 * h + 2 * c
                    await_fill(dve, job)
                    release(V.tensor_reduce(soft[:, col:col + 2], pb(job).rearrange("p (n k) -> p n k", n=2), AX.X,
                                            ALU.max, negate=True), job)
                    await_first_read(dve, job)
                    V.tensor_scalar(soft[:, col:col + 2], soft[:, col:col + 2], soft[:, 48 + h:49 + h], None, ALU.mult
                                    ).then_inc(xmax, 1)
            for h in range(NH):
                for c in range(2):
                    await_read(dve, f"xs{2 * h + c}")
                r = soft[:, 40 + 4 * h:44 + 4 * h]
                link(V.reciprocal(r, r))
                V.tensor_tensor(xp[:, h], xp[:, h], r.unsqueeze(2).to_broadcast([P, XH, S]), ALU.mult).then_inc(xnorm, 1)
            for c in (1, 3):
                plain(f"Txp{c}", xpT[:, c // 2, 2:4])
            split_lo(27)
            plain("xv3", xv[:, 1, 512:], None)
            for c in range(4):
                await_first_read(dve, f"xpv{c}")
                release(V.tensor_tensor(ys_[1][:, 2 * c:2 * c + 2], pb(f"xpv{c}").rearrange("p (c t) -> p c t", c=2),
                                        ys_[0][:, 2 * c:2 * c + 2].bitcast(F32), ALU.subtract), f"xpv{c}")
            split_lo(28)
            split_lo(29)

            def add_xo(cb):
                for h in range(NH):
                    job = f"xo{2 * cb + h}"
                    await_fill(dve, job)
                    o = res[:, h, 512 * cb:512 * cb + 512]
                    release(V.tensor_tensor(o, pb(job), o, ALU.add), job)

            def turned_tokens(c):
                await_fill(dve, f"Tf{c}")
                for k in range(2):
                    i = V.tensor_scalar(xT[c // 2][:, 2 * (c % 2) + k], pb(f"Tf{c}")[:, 256 * k:256 * k + 256],
                                        param("norm_ffn", 2 * c + k), None, ALU.mult)
                release(i, f"Tf{c}")

            add_xo(0)
            turned_tokens(1)
            add_xo(1)
            turned_tokens(3)
            mean_squares(4)

            V.memset(rankm_more[:, :, EXPERTS:], -1.0)
            dve.wait_ge(rstd, 4)
            for h in range(NH):
                await_fill(dve, f"route{h}")
                release(V.scalar_tensor_tensor(logit[:, h], pb(f"route{h}")[:, 0:N_ROUTES],
                                               stat[:, RS + 6 + h:RS + 7 + h], route_bias, ALU.mult, ALU.add), f"route{h}")
            for h in range(NH):
                await_read(dve, f"route{h}")

            def by_group(ap):
                return ap.rearrange("p h (g e) -> p h g e", g=GROUPS)

            def numbers(col):
                return soft[:, col:col + NH * GROUPS].rearrange("p (h g) -> p h g", h=NH)

            def spread(ap, like):
                return ap.unsqueeze(len(like.shape) - 1).to_broadcast(list(like.shape))

            def first_of_max(*searches):
                def operate(stage, src, best, cand, index, pick):
                    flat = cand if len(cand.shape) == 3 else cand.rearrange("p h g e -> p h (g e)")
                    if stage == 0:
                        return V.tensor_reduce(best, src, AX.X, ALU.max)
                    if stage == 1:
                        return V.tensor_tensor(cand, src, spread(best, src), ALU.is_equal)
                    if stage == 2:
                        places = iota[:, 0:flat.shape[-1]].unsqueeze(1).to_broadcast(list(flat.shape))
                        return V.scalar_tensor_tensor(flat, flat, -64.0, places, ALU.mult, ALU.add)
                    if stage == 3:
                        return V.tensor_reduce(index, cand, AX.X, ALU.min)
                    return V.tensor_tensor(pick, cand, spread(index, src), ALU.is_equal)

                last = steps[0]
                for stage in range(5):
                    for n, search in enumerate(searches):
                        if stage:
                            dve.wait_ge(dve_step, last + len(searches) * (stage - 1) + n + 1)
                        operate(stage, *search).then_inc(dve_step, 1)
                steps[0] = last + 5 * len(searches)
                dve.wait_ge(dve_step, steps[0])

            g_best, g_index, g_sum = soft[:, 48:50], soft[:, 50:52], soft[:, 52:54]
            g_pick, g_cand, g_logit = rt(10, GROUPS), rt(11, GROUPS), logit[:, :, 0:GROUPS]
            best1, best2, index, less, e21, gate1 = (numbers(col) for col in (0, 8, 16, 24, 32, 40))
            cand, pick1, pick2, picked, rest = (by_group(rt(n)) for n in range(1, 6))
            first_of_max((by_group(logit[:, :, GROUPS:]), best1, cand, index, pick1),
                         (g_logit, g_best, g_cand, g_index, g_pick))
            V.tensor_tensor(rt(8, GROUPS), g_logit, spread(g_best, g_logit), ALU.subtract).then_inc(group_arg, 1)
            link(V.scalar_tensor_tensor(rt(5), rt(2), -BIG, logit[:, :, GROUPS:], ALU.mult, ALU.add))
            first_of_max((rest, best2, cand, index, pick2))
            V.tensor_tensor(less, best2, best1, ALU.subtract)
            link(V.tensor_tensor(picked, pick1, pick2, ALU.add))
            V.tensor_tensor(picked, picked, spread(g_pick, picked), ALU.mult).then_inc(chosen, 1)
            dve.wait_ge(chosen, 1)
            await_fill(dve, "rank")
            release(V.scalar_tensor_tensor(rankm, pb("rank")[:, 0:2 * EXPERTS].rearrange("p (h e) -> p h e", h=NH), 1.0,
                                           rt(4), ALU.add, ALU.mult), "rank")
            await_read(dve, "rank")
            V.tensor_scalar(rankm, rankm, -1.0, None, ALU.add).then_inc(rank_known, 1)
            dve.wait_ge(rank_known, 1)

            shape = [P, BATCH, SLOTS]

            def take_slots(first, n):
                for h in range(NH):
                    i = V.tensor_tensor(take[:, h], rankm_more[:, h, bass.ds(first, BATCH)].unsqueeze(2).to_broadcast(shape),
                                        iota[:, 0:SLOTS].unsqueeze(1).to_broadcast(shape), ALU.is_equal)
                i.then_inc(slots_found, 1)
                dve.wait_ge(slots_found, n)
                for h in range(NH):
                    i = V.tensor_scalar(ntake[:, h], take[:, h].rearrange("p e s -> p (e s)"),
                                        stat[:, RS + 6 + h:RS + 7 + h], None, ALU.mult)
                i.then_inc(taken, 1)

            take_slots(0, 1)
            dve.wait_ge(group_exp, 1)
            link(V.tensor_reduce(g_sum, rt(9, GROUPS), AX.X, ALU.add))
            dve.wait_ge(expert_exp, 1)
            link(V.scalar_tensor_tensor(gate1, e21, 1.0, spread(g_sum, gate1), ALU.add, ALU.mult))
            link(V.reciprocal(gate1, gate1))
            link(V.tensor_tensor(gate1, gate1, g_pick, ALU.mult))
            link(V.tensor_tensor(e21, e21, gate1, ALU.mult))
            V.tensor_tensor(pick1, pick1, spread(gate1, pick1), ALU.mult)
            link(V.tensor_tensor(pick2, pick2, spread(e21, pick2), ALU.mult))
            link(V.tensor_tensor(by_group(gates), pick1, pick2, ALU.add))
            with dve.Fori(0, BATCHES) as g:
                dve.wait_ge(taken, g + 1)
                for h in range(NH):
                    i = V.tensor_tensor(gtake[:, h], take[:, h],
                                        gates[:, h, bass.ds(BATCH * g, BATCH)].unsqueeze(2).to_broadcast(shape), ALU.mult)
                i.then_inc(gtaken, 1)
                for part in range(2):
                    dve.wait_ge(gathered, 2 * g + (1 + part))
                    V.tensor_tensor(xg[:, CT * part:CT * part + CT], bank(4 + part).rearrange("p (c n) -> p c n", c=CT),
                                    param("norm_ffn")[:, CT * part:CT * part + CT].unsqueeze(2).to_broadcast([P, CT, P]),
                                    ALU.mult).then_inc(xg_ready, 1)
                dve.wait_ge(gtaken, g + 1)
                take_slots(BATCH * g + BATCH, g + 2)
                for j in range(BATCH):
                    n = BATCH * g + (j + 1)
                    half = bank(7)[:, 256 * (j % 2):256 * (j % 2) + 256]
                    dve.wait_ge(gu_tanh, n)
                    V.scalar_tensor_tensor(th, th, 1.0, half[:, 0:P], ALU.add, ALU.mult).then_inc(gu_half, 1)
                    dve.wait_ge(gu_half, n)
                    V.scalar_tensor_tensor(hid, th, 0.5, half[:, P:2 * P], ALU.mult, ALU.mult).then_inc(hid_ready, 1)
                    dve.wait_ge(y_done, n)
                    for strip in range(2, 4):
                        r = slice(SLOTS * strip, SLOTS * strip + SLOTS)
                        i = V.tensor_copy(ybuf[SLOTS * j:SLOTS * j + SLOTS, 256 * strip:256 * strip + 256], bank(6)[r, 0:256])
                    i.then_inc(y_dve, 1)

            await_fill(dve, "over")
            dve.wait_ge(y_act, EXPERTS)
            link(V.tensor_reduce(soft[:, 0:1], pb("over")[:, OVER:OVER + NH * EXPERTS], AX.X, ALU.add))
            release(V.tensor_copy(flag, soft[:, 0:1]), "over")
            await_read(dve, "over")
            many = dve.value_load(flag[0:1, 0:1])
            with dve.If(many > 0):
                dve.wait_ge(scattered, NH * BATCHES)
                for h in range(NH):
                    i = V.tensor_scalar(res[:, h], res[:, h], stat[:, RS + 6 + h:RS + 7 + h], None, ALU.mult)
                i.then_inc(ov_normed, 1)
                V.tensor_scalar(ov_gates, rankm, float(SLOTS), None, ALU.is_ge).then_inc(ov_gate, 1)
                dve.wait_ge(ov_gate, 1)
                V.tensor_tensor(ov_gates, ov_gates, gates, ALU.mult).then_inc(ov_gate, 1)
                dve.wait_ge(ov_gate, 2)
                dve.wait_ge(ov_turned, 1)
                for k in range(KC):
                    i = V.tensor_scalar(ov_x[:, k], bank(4 + k // 2)[:, 256 * (k % 2):256 * (k % 2) + 256],
                                        param("norm_ffn", k), None, ALU.mult)
                i.then_inc(ov_xT, 1)
                with dve.Fori(0, EXPERTS) as e:
                    for h in range(NH):
                        n = NH * e + (h + 1)
                        dve.wait_ge(ov_tanh, n)
                        V.scalar_tensor_tensor(ov_th, ov_th, 1.0, bank(4), ALU.add, ALU.mult).then_inc(ov_half, 1)
                        dve.wait_ge(ov_half, n)
                        V.scalar_tensor_tensor(ov_h, ov_th, 0.5, bank(5), ALU.mult, ALU.mult).then_inc(ov_hid, 1)
                        V.tensor_copy(ov_g, ov_gates[:, h, bass.ds(e, 1)]).then_inc(ov_gate, 1)
                        dve.wait_ge(ov_gate, n + 2)
                        dve.wait_ge(ov_y, n)
                        V.tensor_scalar(ov_ysc.rearrange("p (c n) -> p c n", c=2), psum[:, 4:6, :], ov_g, None,
                                        ALU.mult).then_inc(ov_scaled, 1)
                dve.wait_ge(ov_added, NH * EXPERTS + 1)

            dve.wait_ge(gain_loaded, 16)
            for h in range(NH):
                dve.wait_ge(final_sq, h + 1)
                mean(FINAL + h, 1, D).then_inc(final_ms, 1)
                dve.wait_ge(final_rstd, h + 1)
                for cb in range(2):
                    n = slice(512 * cb, 512 * cb + 512)
                    V.scalar_tensor_tensor(fin[:, h, n], bank(ACC_BANKS[2 * h + cb]),
                                           stat[:, RS + FINAL + h:RS + FINAL + h + 1], gain_final[:, n],
                                           ALU.mult, ALU.mult).then_inc(final_out, 1)


_WEIGHTS = ["w_in", "w_out", "w_xq", "w_xkv", "w_xo", "w_gate_up", "w_down", "norm_final"]


def kernel(**inputs):
    import concourse.bacc as bacc
    from concourse.bass_utils import run_bass_kernel_spmd

    nc = bacc.Bacc("TRN2", target_bir_lowering=False, num_devices=1, dynamic_dma_scratch_size=1024)
    arrays = {f"in_{name}": np.ascontiguousarray(inputs[name]) for name in ["x", "mem"] + _WEIGHTS}
    arrays["in_early"] = np.ascontiguousarray(np.concatenate([constants(), lay_out_params(inputs)], axis=1))
    arrays["in_late"] = np.ascontiguousarray(lay_out_late(inputs))
    args = [nc.dram_tensor(name, a.shape, F32, kind="ExternalInput").ap() for name, a in arrays.items()]
    args.append(nc.dram_tensor("out_0", (1, S, D), F32, kind="ExternalOutput").ap())
    block_kernel(nc, *args)
    r = run_bass_kernel_spmd(nc, [arrays], core_ids=[0])
    return r.results[0]["out_0"]
```
